# Optimizing a Trainium2 kernel written in Bass

```python
import jax, jax.numpy as jnp
from jax import lax
import numpy as np

D_MODEL = 1024
BATCH = 1
SEQ = 1024
DEPTH = 1
DEC_BATCH = 1
DEC_SEQ = 64
PAST_LEN = 256

CHUNK = 64
Q_BLOCK = 128
N_FOX_HEADS = 16
FOX_HEAD_DIM = 64
FOX_WIDTH = N_FOX_HEADS * FOX_HEAD_DIM
N_RET_HEADS = 4
RET_KEY_DIM = 256
RET_VAL_DIM = 512
RET_QK_WIDTH = N_RET_HEADS * RET_KEY_DIM
RET_V_WIDTH = N_RET_HEADS * RET_VAL_DIM
MIX_WIDTH = FOX_WIDTH + RET_V_WIDTH
D_FF = 4 * D_MODEL
ROPE_BASE = 10000.0
EPS = 1e-6
B_FORGET_INIT = 3.0
IN_OFFSETS = (
    FOX_WIDTH,
    2 * FOX_WIDTH,
    3 * FOX_WIDTH,
    3 * FOX_WIDTH + N_FOX_HEADS,
    3 * FOX_WIDTH + N_FOX_HEADS + RET_QK_WIDTH,
    3 * FOX_WIDTH + N_FOX_HEADS + 2 * RET_QK_WIDTH,
    3 * FOX_WIDTH + N_FOX_HEADS + 2 * RET_QK_WIDTH + RET_V_WIDTH,
    3 * FOX_WIDTH + N_FOX_HEADS + 2 * RET_QK_WIDTH + 2 * RET_V_WIDTH,
    3 * FOX_WIDTH + N_FOX_HEADS + 2 * RET_QK_WIDTH + 2 * RET_V_WIDTH + D_MODEL,
)
IN_WIDTH = 3 * FOX_WIDTH + N_FOX_HEADS + 2 * RET_QK_WIDTH + 2 * RET_V_WIDTH + 2 * D_MODEL

kernel_name = "hybrid_fox_retention_stream_step"

def _rmsnorm(x, g):
    xf = x.astype(jnp.float32)
    xf = xf * lax.rsqrt(jnp.mean(xf * xf, axis=-1, keepdims=True) + EPS)
    return (xf * g.astype(jnp.float32)).astype(x.dtype)

def _rotary(x, pos):
    d = x.shape[-1]
    inv_freq = ROPE_BASE ** (-jnp.arange(0, d, 2, dtype=jnp.float32) / d)
    ang = pos.astype(jnp.float32)[:, None] * inv_freq[None, :]
    cos = jnp.cos(ang)[None, :, None, :]
    sin = jnp.sin(ang)[None, :, None, :]
    xf = x.astype(jnp.float32)
    x1, x2 = xf[..., : d // 2], xf[..., d // 2:]
    return jnp.concatenate([x1 * cos - x2 * sin, x1 * sin + x2 * cos], axis=-1).astype(x.dtype)

def _ret_log_gamma():
    return jnp.log(1.0 - 2.0 ** (-5.0 - jnp.arange(N_RET_HEADS, dtype=jnp.float32)))

def _project(h, pos, w_in, b_forget):
    b, t = h.shape[0], h.shape[1]
    z = h @ w_in
    zq_f, zk_f, zv_f, zf, zq_r, zk_r, zv_r, zg_r, zga, zgb = jnp.split(z, IN_OFFSETS, axis=-1)
    q_f = zq_f.reshape(b, t, N_FOX_HEADS, FOX_HEAD_DIM)
    k_f = zk_f.reshape(b, t, N_FOX_HEADS, FOX_HEAD_DIM)
    v_f = zv_f.reshape(b, t, N_FOX_HEADS, FOX_HEAD_DIM)
    logf = jax.nn.log_sigmoid((zf + b_forget).astype(jnp.float32))
    q_r = _rotary(zq_r.reshape(b, t, N_RET_HEADS, RET_KEY_DIM), pos)
    k_r = _rotary(zk_r.reshape(b, t, N_RET_HEADS, RET_KEY_DIM), pos) * (RET_KEY_DIM ** -0.5)
    v_r = zv_r.reshape(b, t, N_RET_HEADS, RET_VAL_DIM)
    return q_f, k_f, v_f, logf, q_r, k_r, v_r, zg_r, zga, zgb

def _fox_prompt(q, k, v, logf):
    b, t, h, d = q.shape
    nb = t // Q_BLOCK
    scale = d ** -0.5
    c_t = jnp.cumsum(logf, axis=1).transpose(0, 2, 1)
    kpos = jnp.arange(t)
    qb = q.reshape(b, nb, Q_BLOCK, h, d).transpose(1, 0, 2, 3, 4)
    cb = c_t.reshape(b, h, nb, Q_BLOCK).transpose(2, 0, 1, 3)

    def block(args):
        qi, ci, bi = args
        s = jnp.einsum('bqhd,bkhd->bhqk', qi, k, preferred_element_type=jnp.float32) * scale
        s = s + (ci[..., :, None] - c_t[:, :, None, :])
        qpos = bi * Q_BLOCK + jnp.arange(Q_BLOCK)
        s = jnp.where(kpos[None, :] <= qpos[:, None], s, -jnp.inf)
        p = jax.nn.softmax(s, axis=-1)
        return jnp.einsum('bhqk,bkhd->bqhd', p.astype(v.dtype), v)

    o = lax.map(block, (qb, cb, jnp.arange(nb)))
    return o.transpose(1, 0, 2, 3, 4).reshape(b, t, h, d)

def _fox_sample(q, k, v, logf, cache_k, cache_v, cache_logf):
    b, l, h, d = q.shape
    p_len = cache_k.shape[1]
    scale = d ** -0.5
    k_all = jnp.concatenate([cache_k.astype(k.dtype), k], axis=1)
    v_all = jnp.concatenate([cache_v.astype(v.dtype), v], axis=1)
    logf_all = jnp.concatenate([cache_logf.astype(jnp.float32), logf], axis=1)
    c_t = jnp.cumsum(logf_all, axis=1).transpose(0, 2, 1)
    s = jnp.einsum('bqhd,bkhd->bhqk', q, k_all, preferred_element_type=jnp.float32) * scale
    s = s + (c_t[:, :, p_len:, None] - c_t[:, :, None, :])
    kpos = jnp.arange(p_len + l)
    qpos = p_len + jnp.arange(l)
    s = jnp.where(kpos[None, :] <= qpos[:, None], s, -jnp.inf)
    p = jax.nn.softmax(s, axis=-1)
    return jnp.einsum('bhqk,bkhd->bqhd', p.astype(v.dtype), v_all)

def _ret_chunk(state, qc, kc, vc, lg):
    state = state.astype(jnp.float32)
    l = qc.shape[1]
    idx = jnp.arange(l, dtype=jnp.float32)
    dist = jnp.abs(idx[:, None] - idx[None, :])
    decay = jnp.exp(lg[:, None, None] * dist[None])
    q_dec = jnp.exp(lg[:, None] * (idx + 1.0)[None])
    k_dec = jnp.exp(lg[:, None] * (l - 1.0 - idx)[None])
    qf, kf, vf = qc.astype(jnp.float32), kc.astype(jnp.float32), vc.astype(jnp.float32)
    s = jnp.einsum('bnhk,bmhk->bhnm', qf, kf) * decay[None]
    o = jnp.einsum('bhnm,bmhv->bnhv', s, vf) + jnp.einsum('bnhk,hn,bhkv->bnhv', qf, q_dec, state)
    new_state = jnp.exp(lg * l)[None, :, None, None] * state + jnp.einsum('bmhk,hm,bmhv->bhkv', kf, k_dec, vf)
    return new_state, o

def _ret_prompt(q, k, v, lg):
    b, t = q.shape[0], q.shape[1]
    n = t // CHUNK

    def to_chunks(a):
        return a.reshape(b, n, CHUNK, a.shape[2], a.shape[3]).transpose(1, 0, 2, 3, 4)

    s0 = jnp.zeros((b, N_RET_HEADS, RET_KEY_DIM, RET_VAL_DIM), jnp.float32)
    s_fin, o = lax.scan(lambda s, xs: _ret_chunk(s, xs[0], xs[1], xs[2], lg), s0,
                        (to_chunks(q), to_chunks(k), to_chunks(v)))
    o = o.transpose(1, 0, 2, 3, 4).reshape(b, t, N_RET_HEADS, RET_VAL_DIM)
    return o, s_fin

def _mixer_output(o_fox, y_ret, g_r, gate_a, gate_b, g_ret_norm, w_branch, w_out):
    b, t = o_fox.shape[0], o_fox.shape[1]
    yf = y_ret.astype(jnp.float32)
    yn = yf * lax.rsqrt(jnp.mean(yf * yf, axis=-1, keepdims=True) + EPS)
    yn = yn * g_ret_norm.astype(jnp.float32).reshape(N_RET_HEADS, RET_VAL_DIM)
    o_b = (jax.nn.silu(g_r.astype(jnp.float32)) * yn.reshape(b, t, RET_V_WIDTH)).astype(g_r.dtype)
    o_a = o_fox.reshape(b, t, FOX_WIDTH)
    merged = jax.nn.sigmoid(gate_a) * (o_a @ w_branch[:FOX_WIDTH]) + jax.nn.sigmoid(gate_b) * (o_b @ w_branch[FOX_WIDTH:])
    return merged @ w_out

def _mlp(h, w_up, w_down):
    return jnp.square(jax.nn.relu(h @ w_up)) @ w_down

def setup_inputs(seed: int = 0) -> dict:
    key = jax.random.key(seed)
    ks = jax.random.split(key, 20)
    nrm = jax.random.normal
    f32 = jnp.float32
    return {
        "x_prompt": nrm(ks[0], (BATCH, SEQ, D_MODEL), f32),
        "x_sample": nrm(ks[1], (DEC_BATCH, DEC_SEQ, D_MODEL), f32),
        "cache_fox_k": nrm(ks[2], (DEPTH, DEC_BATCH, PAST_LEN, N_FOX_HEADS, FOX_HEAD_DIM), f32),
        "cache_fox_v": nrm(ks[3], (DEPTH, DEC_BATCH, PAST_LEN, N_FOX_HEADS, FOX_HEAD_DIM), f32),
        "cache_fox_logf": jax.nn.log_sigmoid(B_FORGET_INIT + nrm(ks[4], (DEPTH, DEC_BATCH, PAST_LEN, N_FOX_HEADS), f32)),
        "state_ret": 0.25 * nrm(ks[5], (DEPTH, DEC_BATCH, N_RET_HEADS, RET_KEY_DIM, RET_VAL_DIM), f32),
        "g_attn": 1.0 + 0.01 * nrm(ks[6], (DEPTH, D_MODEL), f32),
        "w_in": nrm(ks[7], (DEPTH, D_MODEL, IN_WIDTH), f32) * (D_MODEL ** -0.5),
        "b_forget": B_FORGET_INIT + 0.1 * nrm(ks[8], (DEPTH, N_FOX_HEADS), f32),
        "g_ret_norm": 1.0 + 0.01 * nrm(ks[9], (DEPTH, RET_V_WIDTH), f32),
        "w_branch": jnp.concatenate([
            nrm(ks[10], (DEPTH, FOX_WIDTH, D_MODEL), f32) * (FOX_WIDTH ** -0.5),
            nrm(ks[11], (DEPTH, RET_V_WIDTH, D_MODEL), f32) * (RET_V_WIDTH ** -0.5)], axis=1),
        "w_out": nrm(ks[12], (DEPTH, D_MODEL, D_MODEL), f32) * (D_MODEL ** -0.5),
        "g_mlp": 1.0 + 0.01 * nrm(ks[13], (DEPTH, D_MODEL), f32),
        "w_up": nrm(ks[14], (DEPTH, D_MODEL, D_FF), f32) * (D_MODEL ** -0.5),
        "w_down": nrm(ks[15], (DEPTH, D_FF, D_MODEL), f32) * (D_FF ** -0.5),
        "g_final": 1.0 + 0.01 * nrm(ks[16], (D_MODEL,), f32),
    }

def reference(x_prompt, x_sample, cache_fox_k, cache_fox_v, cache_fox_logf, state_ret,
              g_attn, w_in, b_forget, g_ret_norm, w_branch, w_out, g_mlp, w_up, w_down, g_final):
    p_len = cache_fox_k.shape[2]
    pos_p = jnp.arange(x_prompt.shape[1])
    pos_s = p_len + jnp.arange(x_sample.shape[1])
    lg = _ret_log_gamma()
    xp, xs = x_prompt, x_sample
    kp_l, vp_l, fp_l, sp_l, ks_l, vs_l, fs_l, ss_l = [], [], [], [], [], [], [], []
    for layer in range(DEPTH):
        hp = _rmsnorm(xp, g_attn[layer])
        q_f, k_f, v_f, lf, q_r, k_r, v_r, g_r, ga, gb = _project(hp, pos_p, w_in[layer], b_forget[layer])
        o_f = _fox_prompt(q_f, k_f, v_f, lf)
        y_r, s_r = _ret_prompt(q_r, k_r, v_r, lg)
        xp = xp + _mixer_output(o_f, y_r, g_r, ga, gb, g_ret_norm[layer], w_branch[layer], w_out[layer])
        xp = xp + _mlp(_rmsnorm(xp, g_mlp[layer]), w_up[layer], w_down[layer])
        kp_l.append(k_f); vp_l.append(v_f); fp_l.append(lf); sp_l.append(s_r)
        hs = _rmsnorm(xs, g_attn[layer])
        q_f, k_f, v_f, lf, q_r, k_r, v_r, g_r, ga, gb = _project(hs, pos_s, w_in[layer], b_forget[layer])
        o_f = _fox_sample(q_f, k_f, v_f, lf, cache_fox_k[layer], cache_fox_v[layer], cache_fox_logf[layer])
        s_r, y_r = _ret_chunk(state_ret[layer], q_r, k_r, v_r, lg)
        xs = xs + _mixer_output(o_f, y_r, g_r, ga, gb, g_ret_norm[layer], w_branch[layer], w_out[layer])
        xs = xs + _mlp(_rmsnorm(xs, g_mlp[layer]), w_up[layer], w_down[layer])
        ks_l.append(k_f); vs_l.append(v_f); fs_l.append(lf); ss_l.append(s_r)
    y_prompt = _rmsnorm(xp, g_final)
    y_sample = _rmsnorm(xs, g_final)
    new_fox_k_prompt = jnp.stack(kp_l)
    new_fox_v_prompt = jnp.stack(vp_l)
    new_fox_logf_prompt = jnp.stack(fp_l)
    new_state_ret_prompt = jnp.stack(sp_l)
    new_fox_k_sample = jnp.stack(ks_l)
    new_fox_v_sample = jnp.stack(vs_l)
    new_fox_logf_sample = jnp.stack(fs_l)
    new_state_ret_sample = jnp.stack(ss_l)
    return (y_prompt, y_sample, new_fox_k_prompt, new_fox_v_prompt, new_fox_logf_prompt, new_state_ret_prompt,
            new_fox_k_sample, new_fox_v_sample, new_fox_logf_sample, new_state_ret_sample)


_drawn_inputs = setup_inputs


def setup_inputs(seed=0):
    import zlib

    import numpy as np

    out = dict(_drawn_inputs(seed))
    spreads = {}
    factors = {'cache_fox_logf': 39.176,
     'g_attn': 3.645,
     'g_ret_norm': 39.536,
     'g_mlp': 30.894,
     'g_final': 32.546,
     'cache_fox_k': 7.157,
     'cache_fox_v': 8.0}
    for name, (base, spread) in spreads.items():
        noise = np.random.default_rng([zlib.crc32(name.encode()), seed]).standard_normal(out[name].shape)
        drawn = base * np.exp(spread * noise) if base else spread * noise
        out[name] = __import__('jax').numpy.asarray(drawn.astype(out[name].dtype))
    for name, factor in factors.items():
        out[name] = (out[name] * factor).astype(out[name].dtype)
    return out
```

```python
from contextlib import ExitStack

import numpy as np
import concourse.bass as bass
from concourse import mybir

F32 = mybir.dt.float32
F32R = mybir.dt.float32r
ACT = mybir.ActivationFunctionType
ALU = mybir.AluOpType
AX = mybir.AxisListType.X

P = 128
D = 1024
DC = D // P
SEQ = 1024
DEC = 64
PAST = 256
TOK = SEQ + DEC
TOKP = SEQ + P
TT = TOKP // P
SLABS = ((0, 384), (384, 384), (768, 320))
BANK = 512
HF = 16
DF = 64
HR = 4
DK = 256
DV = 512
CHUNK = 64
DFF = 4096
EPS = 1e-6
NEG = -1e30
KEYS = SEQ + PAST + P
S_KEY0 = SEQ
KT = KEYS // P
NPLAIN, NROPE, NSILU, NSIG = 16, 16, 16, 16
NFEAT = NPLAIN + NROPE + NSILU + NSIG


def semaphores(nc, es, tag):
    handles = []

    def done():
        nc.clear_and_free_semaphores(handles)
        nc.all_engine_barrier()
    es.callback(done)

    def sem(name):
        handles.append(nc.alloc_semaphore(name=f"{tag}_{name}"))
        return handles[-1]
    return sem


def gemm_tile(nc, psum, bank, w_hi, w_lo, x_hi, x_lo, chunks):
    for c in range(chunks):
        for n, (w, x) in enumerate(((w_hi, x_hi), (w_hi, x_lo), (w_lo, x_hi))):
            for s, (t0, width) in enumerate(SLABS):
                at = (bank + s) * BANK
                last = nc.tensor.matmul(psum[:, at:at + width], w[:, c, :], x[:, c, t0:t0 + width],
                                        start=(c == 0 and n == 0), stop=(c == chunks - 1 and n == 2))
    return last


def slab_views(psum, bank, x):
    at = bank * BANK
    two = psum[:, at:at + 2 * BANK].rearrange("p (s n) -> p s n", n=BANK)[:, :, 0:384]
    return ((two, x[:, 0:768].rearrange("p (s n) -> p s n", n=384)),
            (psum[:, at + 2 * BANK:at + 2 * BANK + 320], x[:, 768:TOK]))


def rms_norm(nc, g, tag, x, load, gain, hi=None, lo=None, out=None):
    with ExitStack() as es:
        sb = lambda n, s, dt=F32: es.enter_context(nc.sbuf_tensor(f"{tag}_{n}", s, dt))
        sem = semaphores(nc, es, tag)
        gcol, sq, acc = sb("gcol", [P, DC]), sb("sq", [P, 2, TOK]), sb("acc", [P, TOK])
        acc_hi, acc_lo = sb("acc_hi", [P, TOK], F32R), sb("acc_lo", [P, TOK], F32R)
        root, rs, prod = sb("root", [P, TOK]), sb("rs", [P, TOK]), sb("prod", [P, 2, TOK])
        loaded = [sem(f"loaded{c}") for c in range(DC)] if load is not None else None
        squared, summed, split = sem("squared"), sem("summed"), sem("split")
        total, rooted, inverted = sem("total"), sem("rooted"), sem("inverted")
        scaled, rounded, ready, stored = sem("scaled"), sem("rounded"), sem("gready"), [sem(f"stored{n}") for n in range(2)]
        rest_even, rest_odd = sem("rest_even"), sem("rest_odd")
        psum = g.psum
        block = es.enter_context(nc.Block())

        @block.sync
        def _(sp):
            sp.dma_start(gcol[:], gain).then_inc(ready, 16)
            if load is not None:
                for c in range(DC):
                    sp.dma_start(x[:, c, :], load[c * P:(c + 1) * P, :]).then_inc(loaded[c], 16)
            if out is not None:
                for c in range(DC):
                    sp.wait_ge(scaled, c + 1)
                    sp.dma_start(out[c * P:(c + 1) * P, :], prod[:, c % 2, :]).then_inc(stored[c % 2], 16)
                for n in range(2):
                    sp.wait_ge(stored[n], 16 * DC // 2)

        @block.scalar
        def _(act):
            for c in range(DC):
                if load is not None:
                    act.wait_ge(loaded[c], 16)
                if c >= 2:
                    act.wait_ge(summed, c - 1)
                nc.scalar.activation(sq[:, c % 2, :], x[:, c, :], ACT.Square).then_inc(squared, 1)
            act.wait_ge(total, 1)
            for a, b in slab_views(psum, 0, root):
                last = nc.scalar.activation(b, a, ACT.Sqrt, bias=g.eps[:, 0:1], scale=1.0 / D)
            last.then_inc(rooted, 1)
            if out is None:
                for c in range(DC):
                    act.wait_ge(scaled, c + 1)
                    nc.scalar.activation(hi[:, c, :], prod[:, c % 2, :], ACT.Copy).then_inc(rounded, 1)

        @block.gpsimd
        def _(pool):
            if out is None:
                for c in range(1, DC, 2):
                    pool.wait_ge(rounded, c + 1)
                    nc.gpsimd.tensor_tensor(lo[:, c, :], prod[:, c % 2, :], hi[:, c, :].bitcast(F32),
                                            ALU.subtract).then_inc(rest_odd, 1)

        @block.vector
        def _(dve):
            for c in range(DC):
                dve.wait_ge(squared, c + 1)
                if c == 0:
                    nc.vector.tensor_copy(acc[:], sq[:, 0, :]).then_inc(summed, 1)
                else:
                    dve.wait_ge(summed, c)
                    nc.vector.tensor_tensor(acc[:], acc[:], sq[:, c % 2, :], ALU.add).then_inc(summed, 1)
            dve.wait_ge(summed, DC)
            nc.vector.tensor_copy(acc_hi[:], acc[:]).then_inc(split, 1)
            dve.wait_ge(split, 1)
            nc.vector.tensor_tensor(acc_lo[:], acc[:], acc_hi[:].bitcast(F32), ALU.subtract).then_inc(split, 1)
            dve.wait_ge(rooted, 1)
            nc.vector.reciprocal(rs[:], root[:]).then_inc(inverted, 1)
            dve.wait_ge(inverted, 1)
            dve.wait_ge(ready, 16)
            for c in range(DC):
                if c >= 2 and out is not None:
                    dve.wait_ge(stored[c % 2], 16 * (c // 2))
                if c >= 2 and out is None and c % 2 == 1:
                    dve.wait_ge(rest_odd, (c - 1) // 2)
                if out is None and c >= 2 and c % 2 == 0:
                    dve.wait_ge(rest_even, c // 2)
                nc.vector.scalar_tensor_tensor(prod[:, c % 2, :], x[:, c, :], gcol[:, c:c + 1], rs[:],
                                               ALU.mult, ALU.mult).then_inc(scaled, 1)
                if out is None and c % 2 == 0:
                    dve.wait_ge(rounded, c + 1)
                    nc.vector.tensor_tensor(lo[:, c, :], prod[:, c % 2, :], hi[:, c, :].bitcast(F32),
                                            ALU.subtract).then_inc(rest_even, 1)

        @block.tensor
        def _(pe):
            pe.wait_ge(split, 2)
            for n, part in enumerate((acc_hi, acc_lo)):
                for s, (t0, width) in enumerate(SLABS):
                    last = nc.tensor.matmul(psum[:, s * BANK:s * BANK + width], g.ones_r[:, :],
                                            part[:, t0:t0 + width], start=(n == 0), stop=(n == 1))
            last.then_inc(total, 1)


def values(nc, g, h_hi, h_lo):
    GROUP = 512
    with ExitStack() as es:
        sb = lambda n, s, dt=F32: es.enter_context(nc.sbuf_tensor(f"val_{n}", s, dt))
        sem = semaphores(nc, es, "val")
        raw = sb("raw", [P, DC, GROUP])
        w_hi, w_lo = sb("w_hi", [P, 2, DC, GROUP], F32R), sb("w_lo", [P, 2, DC, GROUP], F32R)
        stage = sb("stage", [P, 2, GROUP])
        loaded, rounded, split = sem("loaded"), sem("rounded"), sem("split")
        multiplied, staged, stored = sem("multiplied"), sem("staged"), [sem(f"stored{n}") for n in range(2)]
        psum, BANKS = g.psum, 6
        tiles = 2 * TT
        block = es.enter_context(nc.Block())

        @block.sync
        def _(sp):
            for n in range(2):
                sp.sem_inc(stored[n], 16)

            def load(i, j, splits):
                sp.wait_ge(split, splits)
                sp.dma_start(raw[:].rearrange("p c n -> p (c n)"),
                             g.w_tok[2 * i + j, :, :]).then_inc(loaded, 16)

            def store(i, next_i, dst):
                for k in range(tiles):
                    if next_i is not None and k in (4, TT + 4):
                        load(next_i, k // TT, 2 * i + k // TT + 2)
                    j, t = k // TT, k % TT
                    rows = DEC if t == TT - 1 else P
                    sp.wait_ge(staged, tiles * i + k + 1)
                    sp.dma_start(dst(j)[t * P:t * P + rows, :],
                                 stage[0:rows, k % 2, :]).then_inc(stored[k % 2], 16)
            load(0, 0, 0)
            load(0, 1, 1)
            store(0, 1, lambda j: g.v_out[:, j * GROUP:(j + 1) * GROUP])
            with sp.Fori(1, 2) as i:
                store(i, i + 1, lambda j: g.v_ret[2 * i - 2 + j, :, :])
            store(2, None, lambda j: g.v_ret[2 + j, :, :])
            for n in range(2):
                sp.wait_ge(stored[n], 16 + 16 * 3 * tiles // 2)

        @block.scalar
        def _(act):
            def round_group(i, j):
                act.wait_ge(loaded, 32 * i + 16 * (j + 1))
                nc.scalar.activation(w_hi[:, j], raw[:], ACT.Copy).then_inc(rounded, 1)
            round_group(0, 0)
            round_group(0, 1)
            with act.Fori(1, 3) as i:
                for j in range(2):
                    act.wait_ge(multiplied, tiles * i - TT * (1 - j))
                    round_group(i, j)

        @block.vector
        def _(dve):
            def take(i, j):
                dve.wait_ge(rounded, 2 * i + j + 1)
                nc.vector.tensor_tensor(w_lo[:, j], raw[:], w_hi[:, j].bitcast(F32),
                                        ALU.subtract).then_inc(split, 1)
            take(0, 0)

            def evict(i, next_i):
                for k in range(tiles):
                    if k == 3:
                        take(i, 1)
                    if k == TT + 3 and next_i is not None:
                        take(next_i, 0)
                    dve.wait_ge(multiplied, tiles * i + k + 1)
                    dve.wait_ge(stored[k % 2], 8 * tiles * i + 16 * (k // 2 + 1))
                    rows = DEC if k % TT == TT - 1 else P
                    nc.vector.tensor_copy(stage[0:rows, k % 2, :],
                                          psum[0:rows, (k % BANKS) * BANK:(k % BANKS + 1) * BANK])\
                        .then_inc(staged, 1)
            with dve.Fori(0, 2) as i:
                evict(i, i + 1)
            evict(2, None)

        @block.tensor
        def _(pe):
            with pe.Fori(0, 3) as i:
                for k in range(tiles):
                    j, t = k // TT, k % TT
                    if t == 0:
                        pe.wait_ge(split, 2 * i + j + 1)
                    if k >= BANKS:
                        pe.wait_ge(staged, tiles * i + k + 1 - BANKS)
                    else:
                        pe.wait_ge(staged, tiles * i)
                    at = (k % BANKS) * BANK
                    cols = slice(t * P, (t + 1) * P)
                    for c in range(DC):
                        for n, (h, w) in enumerate(((h_hi, w_hi), (h_hi, w_lo), (h_lo, w_hi))):
                            last = nc.tensor.matmul(psum[:, at:at + BANK], h[:, c, cols], w[:, j, c, :],
                                                    start=(c == 0 and n == 0), stop=(c == DC - 1 and n == 2))
                    last.then_inc(multiplied, 1)


def features(nc, g, h_hi, h_lo, zf):
    with ExitStack() as es:
        sb = lambda n, s, dt=F32: es.enter_context(nc.sbuf_tensor(f"ft_{n}", s, dt))
        sem = semaphores(nc, es, "ft")
        raw = sb("raw", [P, 2, DC, P])
        w_hi, w_lo = sb("w_hi", [P, 2, DC, P], F32R), sb("w_lo", [P, 2, DC, P], F32R)
        stage, tmp = sb("stage", [P, 2, TOK]), sb("tmp", [P, 2, TOK])
        prods = sb("prods", [P, 4, TOK])
        cos, sin = sb("cos", [P, TOK]), sb("sin", [P, TOK])
        bias = sb("bias", [HF, 1])
        loaded, rounded, split = [sem(f"loaded{j}") for j in range(2)], sem("rounded"), sem("split")
        tables, multiplied = sem("tables"), sem("multiplied")
        copied, rotated, silued = sem("copied"), sem("rotated"), sem("silued")
        stored, rope_products = [sem(f"stored{j}") for j in range(2)], sem("rope_products")
        sigmoid = sem("sigmoid")
        psum = g.psum
        last_tile = NFEAT
        plain, rope = (0, NPLAIN // 2), (NPLAIN // 2, (NPLAIN + NROPE) // 2)
        silu = (rope[1], rope[1] + NSILU // 2)
        sigm = (silu[1], silu[1] + NSIG // 2)
        block = es.enter_context(nc.Block())

        def at(j):
            return 3 * j

        @block.sync
        def _(sp):
            sp.dma_start(raw[:, 0].rearrange("p c n -> p (c n)"), g.w_feat[0, :, :]).then_inc(loaded[0], 16)
            sp.dma_start(raw[:, 1].rearrange("p c n -> p (c n)"), g.w_feat[1, :, :]).then_inc(loaded[1], 16)
            sp.dma_start(bias[:], g.b_forget).then_inc(tables, 16)
            sp.dma_start(cos[:], g.cos_t).then_inc(tables, 16)
            sp.dma_start(sin[:], g.sin_t).then_inc(tables, 16)

            for j in range(2):
                sp.sem_inc(stored[j], 16)

            def next_load(t, j):
                sp.wait_ge(split, t - 1)
                sp.dma_start(raw[:, j].rearrange("p c n -> p (c n)"), g.w_feat[t, :, :]).then_inc(loaded[j], 16)

            def store(dst, first, staged, before, t, j):
                sp.wait_ge(staged, t + 1 - before)
                sp.dma_start(dst[t - first, :, :], stage[:, j, :]).then_inc(stored[j], 16)

            def bodies(start, end, dst, first, staged, before):
                with sp.Fori(start, end) as i:
                    for j in range(2):
                        next_load(2 * i + 2 + j, j)
                    for j in range(2):
                        store(dst, first, staged, before, 2 * i + j, j)
            bodies(*plain, g.qk_out, 0, copied, 0)
            bodies(*rope, g.qk_ret, NPLAIN, rotated, NPLAIN)
            bodies(*silu, g.gates, NPLAIN + NROPE, silued, NPLAIN + NROPE)
            bodies(sigm[0], sigm[1] - 1, g.gates, NPLAIN + NROPE, copied, NROPE + NSILU)
            next_load(last_tile, 0)
            for j in range(2):
                store(g.gates, NPLAIN + NROPE, copied, NROPE + NSILU, NFEAT - 2 + j, j)
            for j in range(2):
                sp.wait_ge(stored[j], 16 + 16 * NFEAT // 2)

        @block.gpsimd
        def _(pool):
            with pool.Fori(*rope) as i:
                for j in range(2):
                    pool.wait_ge(rope_products, 4 * i - 4 * rope[0] + 3 + j)
                    pool.wait_ge(stored[j], 16 * (i + 1))
                    nc.gpsimd.tensor_tensor(stage[:, j, :], prods[:, 2 * j, :], prods[:, 2 * j + 1, :],
                                            ALU.subtract if j == 0 else ALU.add).then_inc(rotated, 1)

        @block.scalar
        def _(act):
            def round_tile(t, j, nth):
                act.wait_ge(loaded[j], 16 * (nth + 1))
                nc.scalar.activation(w_hi[:, j], raw[:, j], ACT.Copy).then_inc(rounded, 1)

            def ahead(i, j):
                act.wait_ge(multiplied, 2 * i + j)
                round_tile(2 * i + j + 1, 1 - j, i + j)
            round_tile(0, 0, 0)
            with act.Fori(*plain) as i:
                for j in range(2):
                    ahead(i, j)
                    act.wait_ge(multiplied, 2 * i + j + 1)
                    act.wait_ge(stored[j], 16 * (i + 1))
                    views = slab_views(psum, at(j), stage[:, j, :])
                    nc.scalar.activation(views[0][1], views[0][0], ACT.Copy)
                    nc.scalar.activation(views[1][1], views[1][0], ACT.Copy).then_inc(copied, 1)
            with act.Fori(*rope) as i:
                for j in range(2):
                    ahead(i, j)
            with act.Fori(*silu) as i:
                for j in range(2):
                    ahead(i, j)
                    act.wait_ge(multiplied, 2 * i + j + 1)
                    act.wait_ge(silued, 2 * i + j - NPLAIN - NROPE)
                    views = slab_views(psum, at(j), tmp[:, j, :])
                    nc.scalar.activation(views[0][1], views[0][0], ACT.Sigmoid)
                    nc.scalar.activation(views[1][1], views[1][0], ACT.Sigmoid).then_inc(sigmoid, 1)
            with act.Fori(*sigm) as i:
                for j in range(2):
                    ahead(i, j)
                    act.wait_ge(multiplied, 2 * i + j + 1)
                    act.wait_ge(stored[j], 16 * (i + 1))
                    views = slab_views(psum, at(j), stage[:, j, :])
                    nc.scalar.activation(views[0][1], views[0][0], ACT.Sigmoid)
                    nc.scalar.activation(views[1][1], views[1][0], ACT.Sigmoid).then_inc(copied, 1)
            act.wait_ge(tables, 48)
            act.wait_ge(multiplied, last_tile + 1)
            for dst, src in ((zf[:, 0:768].rearrange("p (s n) -> p s n", n=384),
                              psum[0:HF, 0:2 * BANK].rearrange("p (s n) -> p s n", n=BANK)[:, :, 0:384]),
                             (zf[:, 768:TOK], psum[0:HF, 2 * BANK:2 * BANK + 320])):
                nc.scalar.activation(dst, src, ACT.Identity, bias=bias[:, 0:1])

        @block.vector
        def _(dve):
            def rest(t, j):
                dve.wait_ge(rounded, t + 1)
                nc.vector.tensor_tensor(w_lo[:, j], raw[:, j], w_hi[:, j].bitcast(F32),
                                        ALU.subtract).then_inc(split, 1)
            rest(0, 0)
            with dve.Fori(*plain) as i:
                for j in range(2):
                    rest(2 * i + j + 1, 1 - j)
            dve.wait_ge(tables, 48)
            with dve.Fori(*rope) as i:
                rest(2 * i + 1, 1)
                for half, (table, n0, n1) in enumerate(((0, 0, 2), (1, 1, 3))):
                    dve.wait_ge(multiplied, 2 * i + half + 1)
                    if half == 1:
                        rest(2 * i + 2, 0)
                    for dst, table in (((0, cos), (2, sin)) if half == 0 else ((1, sin), (3, cos))):
                        dve.wait_ge(rotated, 2 * i - NPLAIN)
                        pv = slab_views(psum, at(half), prods[:, dst, :])
                        tv = slab_views(psum, at(half), table[:, :])
                        nc.vector.tensor_tensor(pv[0][1], pv[0][0], tv[0][1], ALU.mult)
                        nc.vector.tensor_tensor(pv[1][1], pv[1][0], tv[1][1], ALU.mult).then_inc(rope_products, 1)
            with dve.Fori(*silu) as i:
                for j in range(2):
                    t = 2 * i + j
                    rest(t + 1, 1 - j)
                    dve.wait_ge(sigmoid, t + 1 - 2 * silu[0])
                    dve.wait_ge(stored[j], 16 * (i + 1))
                    views = slab_views(psum, at(j), stage[:, j, :])
                    tv = slab_views(psum, at(j), tmp[:, j, :])
                    nc.vector.tensor_tensor(views[0][1], views[0][0], tv[0][1], ALU.mult)
                    nc.vector.tensor_tensor(views[1][1], views[1][0], tv[1][1], ALU.mult).then_inc(silued, 1)
            with dve.Fori(*sigm) as i:
                for j in range(2):
                    rest(2 * i + j + 1, 1 - j)

        @block.tensor
        def _(pe):
            def tile(t, j):
                pe.wait_ge(split, t + 1)
                gemm_tile(nc, psum, at(j), w_hi[:, j], w_lo[:, j], h_hi, h_lo, DC).then_inc(multiplied, 1)
            tile(0, 0)
            tile(1, 1)

            def bodies(start, end, staged, before):
                with pe.Fori(start, end) as i:
                    for j in range(2):
                        pe.wait_ge(staged, 2 * i + j - 1 - before)
                        tile(2 * i + j, j)
            bodies(1, rope[0] + 1, copied, 0)
            with pe.Fori(rope[0] + 1, rope[1] + 1) as i:
                for j in range(2):
                    pe.wait_ge(rope_products, 4 * i - 4 * rope[0] - 2 + 2 * j)
                    tile(2 * i + j, j)
            bodies(silu[0] + 1, silu[1] + 1, silued, NPLAIN + NROPE)
            bodies(sigm[0] + 1, sigm[1], copied, NROPE + NSILU)
            pe.wait_ge(copied, last_tile - 1 - NROPE - NSILU)
            tile(last_tile, 0)


def decay(nc, g, zf):
    with ExitStack() as es:
        sb = lambda n, s, dt=F32: es.enter_context(nc.sbuf_tensor(f"dc_{n}", s, dt))
        sem = semaphores(nc, es, "dc")
        neg_abs, soft, low = sb("neg_abs", [HF, TOK]), sb("soft", [HF, TOK]), sb("low", [HF, TOK])
        logf, ones, c = sb("logf", [HF, KEYS]), sb("ones", [HF, KEYS]), sb("c", [HF, KEYS])
        c_hi = sb("c_hi", [HF, KEYS], F32R)
        q_rows, k_rows = sb("q_rows", [HF, 4, TOK]), sb("k_rows", [HF, 4, KEYS])
        cached, step, soft_ready = sem("cached"), sem("step"), sem("soft_ready")
        logf_ready, chain, stored = sem("logf_ready"), sem("chain"), sem("stored")
        block = es.enter_context(nc.Block())
        S0 = SEQ + PAST

        @block.sync
        def _(sp):
            sp.dma_start(logf[:, SEQ:S0], g.cache_logf).then_inc(cached, 16)
            sp.wait_ge(logf_ready, 3)
            sp.dma_start(g.logf_out[:, 0:SEQ], logf[:, 0:SEQ]).then_inc(stored, 16)
            sp.dma_start(g.logf_out[:, SEQ:TOK], logf[:, S0:S0 + DEC]).then_inc(stored, 16)
            sp.wait_ge(chain, 11)
            sp.dma_start(g.q_rows, q_rows[:]).then_inc(stored, 16)
            sp.dma_start(g.k_rows, k_rows[:]).then_inc(stored, 16)
            sp.wait_ge(stored, 64)

        @block.scalar
        def _(act):
            nc.scalar.activation(soft[:], zf[:], ACT.Abs).then_inc(step, 1)
            act.wait_ge(step, 1)
            nc.scalar.activation(neg_abs[:], soft[:], ACT.Exp, scale=-1.0).then_inc(step, 1)
            act.wait_ge(step, 2)
            nc.scalar.activation(soft[:], neg_abs[:], ACT.Ln, bias=1.0).then_inc(soft_ready, 1)

        @block.vector
        def _(dve):
            done = [0]

            def then(instruction):
                done[0] += 1
                instruction.then_inc(chain, 1)
                dve.wait_ge(chain, done[0])
            nc.vector.tensor_scalar(low[:], zf[:], 0.0, None, ALU.min).then_inc(logf_ready, 1)
            dve.wait_ge(logf_ready, 1)
            dve.wait_ge(soft_ready, 1)
            nc.vector.memset(logf[:, S0 + DEC:KEYS], 0.0)
            nc.vector.tensor_tensor(logf[:, 0:SEQ], low[:, 0:SEQ], soft[:, 0:SEQ],
                                    ALU.subtract).then_inc(logf_ready, 1)
            nc.vector.tensor_tensor(logf[:, S0:S0 + DEC], low[:, SEQ:TOK], soft[:, SEQ:TOK],
                                    ALU.subtract).then_inc(logf_ready, 1)
            then(nc.vector.memset(ones[:], 1.0))
            dve.wait_ge(logf_ready, 3)
            dve.wait_ge(cached, 16)
            then(nc.vector.tensor_tensor_scan(c[:, 0:SEQ], ones[:, 0:SEQ], logf[:, 0:SEQ], 0.0,
                                              ALU.mult, ALU.add))
            then(nc.vector.tensor_tensor_scan(c[:, SEQ:KEYS], ones[:, SEQ:KEYS], logf[:, SEQ:KEYS], 0.0,
                                              ALU.mult, ALU.add))
            then(nc.vector.tensor_copy(c_hi[:], c[:]))
            hi = c_hi[:].bitcast(F32)
            then(nc.vector.tensor_scalar(k_rows[:, 0, :], hi, -1.0, None, ALU.mult))
            then(nc.vector.tensor_tensor(k_rows[:, 1, :], hi, c[:], ALU.subtract))
            then(nc.vector.memset(k_rows[:, 2:4, :], 1.0))
            then(nc.vector.memset(q_rows[:, 0:2, :], 1.0))
            for q0, k0, n in ((0, 0, SEQ), (SEQ, S0, DEC)):
                nc.vector.tensor_copy(q_rows[:, 2, q0:q0 + n], hi[:, k0:k0 + n])
                then(nc.vector.tensor_tensor(q_rows[:, 3, q0:q0 + n], c[:, k0:k0 + n], hi[:, k0:k0 + n],
                                             ALU.subtract))
            then(nc.vector.memset(ones[:, 0:1], 1.0))


def retention(nc, g):
    NV = DV // P
    steps = [(b, j, max(BANK * b, P * j)) for b in range(2) for j in range(4 * b + 4)]
    steps = [(b, j, n0, BANK * (b + 1) - n0) for b, j, n0 in steps] + [(2, TT - 1, SEQ, DEC)]
    NS = len(steps)
    ends = [max(s for s in range(NS) if steps[s][0] == b) for b in range(3)]
    with ExitStack() as es:
        sb = lambda n, s, dt=F32: es.enter_context(nc.sbuf_tensor(f"rt_{n}", s, dt))
        sem = semaphores(nc, es, "rt")
        q_raw, k_raw = sb("q_raw", [P, 2, TOKP]), sb("k_raw", [P, 2, TOKP])
        v_raw, s_raw = sb("v_raw", [P, TT, DV]), sb("s_raw", [P, 2, DV])
        q_hi, q_lo = sb("q_hi", [P, 2, TOKP], F32R), sb("q_lo", [P, 2, TOKP], F32R)
        k_hi, k_lo = sb("k_hi", [P, 2, TOKP], F32R), sb("k_lo", [P, 2, TOKP], F32R)
        v_hi, v_lo = sb("v_hi", [P, TT, DV], F32R), sb("v_lo", [P, TT, DV], F32R)
        s_hi, s_lo = sb("s_hi", [P, 2, DV], F32R), sb("s_lo", [P, 2, DV], F32R)
        kt, kt_hi, kt_lo = sb("kt", [P, 2, 2, DK]), sb("kt_hi", [P, TT, DK], F32R), sb("kt_lo", [P, TT, DK], F32R)
        qd, qd_hi, qd_lo = sb("qd", [P, 2, DEC]), sb("qd_hi", [P, 2, DEC], F32R), sb("qd_lo", [P, 2, DEC], F32R)
        w, w_hi, w_lo = sb("w", [P, 2, BANK]), sb("w_hi", [P, 2, BANK], F32R), sb("w_lo", [P, 2, BANK], F32R)
        table, cols, qdec = sb("table", [P, SEQ]), sb("cols", [P, TT + 1 + NV]), sb("qdec", [P, DEC])
        y, gate, work = sb("y", [P, NV, TOK]), sb("gate", [P, TOK]), sb("work", [P, 2, TOK])
        acc, rs = sb("acc", [P, TOK]), sb("rs", [P, TOK])
        acc_hi, acc_lo = q_hi[:, 0, 0:TOK], q_lo[:, 0, 0:TOK]
        ident = sb("ident", [P, P])
        qk_loaded, v_loaded, aux_loaded = sem("qk_loaded"), sem("v_loaded"), sem("aux_loaded")
        const_loaded, padded, gate_loaded = sem("const_loaded"), sem("padded"), sem("gate_loaded")
        rounded, split, transposed = sem("rounded"), sem("split"), sem("transposed")
        split_qd = sem("split_qd")
        kt_decayed, kt_rounded, kt_split = sem("kt_decayed"), sem("kt_rounded"), sem("kt_split")
        states, states_copied, states_summed = sem("states"), sem("states_copied"), sem("states_summed")
        states_stored, q_decayed = sem("states_stored"), sem("q_decayed")
        scored, weighted, w_rounded, w_split = sem("scored"), sem("weighted"), sem("w_rounded"), sem("w_split")
        y_step, y_copied, squared, summed = sem("y_step"), sem("y_copied"), sem("squared"), sem("summed")
        acc_split, total, rooted, inverted = sem("acc_split"), sem("total"), sem("rooted"), sem("inverted")
        normed, gated, o_stored = sem("normed"), sem("gated"), sem("o_stored")
        psum = g.psum
        bank = lambda b, n=BANK: psum[:, b * BANK:b * BANK + n]
        block = es.enter_context(nc.Block())
        HEADS = HR - 1

        @block.sync
        def _(sp):
            def load_raw(i):
                sp.dma_start(q_raw[:, :, 0:TOK], g.qk_ret[bass.ds(2 * i, 2), :, :].rearrange("c p t -> p c t"))\
                    .then_inc(qk_loaded, 16)
                sp.dma_start(k_raw[:, :, 0:TOK], g.qk_ret[bass.ds(2 * i + DC, 2), :, :].rearrange("c p t -> p c t"))\
                    .then_inc(qk_loaded, 16)
                sp.dma_start(v_raw[:, 0:TT - 1, :], g.v_ret[i, 0:SEQ, :].rearrange("(t p) n -> p t n", p=P))\
                    .then_inc(v_loaded, 16)
                sp.dma_start(v_raw[0:DEC, TT - 1, :], g.v_ret[i, SEQ:TOK, :]).then_inc(v_loaded, 16)

            def load_aux(i):
                sp.dma_start(table[:], g.ret_decay[i, :, :]).then_inc(aux_loaded, 16)
                sp.dma_start(cols[:], g.ret_cols[i, :, :]).then_inc(aux_loaded, 16)
                sp.dma_start(qdec[:], g.ret_qdec[i, :, :]).then_inc(aux_loaded, 16)
                sp.dma_start(s_raw[:], g.state_in[i, :, :].rearrange("(c p) n -> p c n", p=P)).then_inc(aux_loaded, 16)

            def store(i, next_i):
                sp.wait_ge(split, 4 * i + 4)
                sp.wait_ge(transposed, 5 * i + 5)
                if next_i is not None:
                    load_raw(next_i)
                sp.wait_ge(states_copied, i + 1)
                sp.dma_start(g.state_out[0, i, :, :].rearrange("(c p) n -> p c n", p=P),
                             work[:, 0, 0:2 * DV].rearrange("p (c n) -> p c n", n=DV)).then_inc(states_stored, 16)
                sp.wait_ge(states_summed, i + 1)
                sp.dma_start(g.state_out[1, i, :, :].rearrange("(c p) n -> p c n", p=P),
                             work[:, 1, 0:2 * DV].rearrange("p (c n) -> p c n", n=DV)).then_inc(states_stored, 16)
                for c in range(NV):
                    sp.wait_ge(gated, NV * i + c)
                    sp.dma_start(gate[:], g.gates[NV * i + c, :, :]).then_inc(gate_loaded, 16)
                    if c == 3 and next_i is not None:
                        sp.wait_ge(normed, NV * i + NV)
                        load_aux(next_i)
                sp.wait_ge(gated, NV * i + NV)
                sp.dma_start(g.o_ret[bass.ds(NV * i, NV), :, :].rearrange("c p t -> p c t"), y[:]).then_inc(o_stored, 16)

            sp.dma_start(ident[:], g.ident_t).then_inc(const_loaded, 16)
            load_raw(0)
            load_aux(0)
            with sp.Fori(0, HEADS) as i:
                store(i, i + 1)
            store(HEADS, None)
            sp.wait_ge(o_stored, 16 * HR)
            sp.wait_ge(states_stored, 32 * HR)

        @block.gpsimd
        def _(pool):
            with pool.Fori(0, HR) as i:
                for s, (b, j, n0, n) in enumerate(steps):
                    pool.wait_ge(w_rounded, NS * i + s + 1)
                    if s >= 2:
                        pool.wait_ge(y_step, NS * i + s - 1)
                    nc.gpsimd.tensor_tensor(w_lo[:, s % 2, 0:n], w[:, s % 2, 0:n], w_hi[:, s % 2, 0:n].bitcast(F32),
                                            ALU.subtract).then_inc(w_split, 1)

        @block.scalar
        def _(act):
            act.wait_ge(padded, 3)
            with act.Fori(0, HR) as i:
                act.wait_ge(qk_loaded, 32 * i + 32)
                nc.scalar.activation(q_hi[:], q_raw[:], ACT.Copy).then_inc(rounded, 1)
                nc.scalar.activation(k_hi[:], k_raw[:], ACT.Copy).then_inc(rounded, 1)
                act.wait_ge(v_loaded, 32 * i + 32)
                nc.scalar.activation(v_hi[:], v_raw[:], ACT.Copy).then_inc(rounded, 1)
                act.wait_ge(aux_loaded, 64 * i + 64)
                nc.scalar.activation(s_hi[:], s_raw[:], ACT.Copy).then_inc(rounded, 1)
                act.wait_ge(q_decayed, i + 1)
                nc.scalar.activation(qd_hi[:], qd[:], ACT.Copy).then_inc(rounded, 1)
                for p in range(5):
                    n = 2 if p < 4 else 1
                    act.wait_ge(kt_decayed, TT * i + 2 * p + n)
                    nc.scalar.activation(kt_hi[:, 2 * p:2 * p + n, :], kt[:, p % 2, 0:n, :], ACT.Copy)\
                        .then_inc(kt_rounded, 1)
                act.wait_ge(states, i + 1)
                act.wait_ge(gated, NV * i)
                nc.scalar.activation(work[:, 0, 0:2 * DV], psum[:, 0:2 * DV], ACT.Copy).then_inc(states_copied, 1)
                for s, (b, j, n0, n) in enumerate(steps):
                    act.wait_ge(weighted, NS * i + s + 1)
                    if s >= 2:
                        act.wait_ge(y_step, NS * i + s - 1)
                    nc.scalar.activation(w_hi[:, s % 2, 0:n], w[:, s % 2, 0:n], ACT.Copy).then_inc(w_rounded, 1)
                    if s - 1 in ends[:2]:
                        copy_y = s - 1
                        bb = steps[copy_y][0]
                        act.wait_ge(y_step, NS * i + copy_y + 1)
                        if bb == 0:
                            act.wait_ge(o_stored, 16 * i)
                        nc.scalar.activation(y[:, :, bb * BANK:(bb + 1) * BANK],
                                             psum[:, 0:4 * BANK].rearrange("p (c n) -> p c n", n=BANK),
                                             ACT.Copy).then_inc(y_copied, 1)
                act.wait_ge(y_step, NS * i + NS)
                nc.scalar.activation(y[:, :, SEQ:TOK],
                                     psum[:, 0:4 * BANK].rearrange("p (c n) -> p c n", n=BANK)[:, :, 0:DEC],
                                     ACT.Copy).then_inc(y_copied, 1)
                act.wait_ge(y_copied, 3 * i + 3)
                act.wait_ge(states_stored, 32 * i + 32)
                for c in range(NV):
                    if c >= 2:
                        act.wait_ge(summed, NV * i + c - 1)
                    nc.scalar.activation(work[:, c % 2, :], y[:, c, :], ACT.Square).then_inc(squared, 1)
                act.wait_ge(total, i + 1)
                for src, dst in slab_views(psum, 4, rs):
                    last = nc.scalar.activation(dst, src, ACT.Sqrt, bias=g.eps[:, 0:1], scale=1.0 / DV)
                last.then_inc(rooted, 1)

        @block.vector
        def _(dve):
            nc.vector.memset(q_raw[:, :, TOK:TOKP], 0.0).then_inc(padded, 1)
            nc.vector.memset(k_raw[:, :, TOK:TOKP], 0.0).then_inc(padded, 1)
            nc.vector.memset(v_raw[DEC:P, TT - 1, :], 0.0).then_inc(padded, 1)
            dve.wait_ge(padded, 3)
            with dve.Fori(0, HR) as i:
                for n, (lo, raw, hi) in enumerate(((q_lo, q_raw, q_hi), (k_lo, k_raw, k_hi), (v_lo, v_raw, v_hi),
                                                   (s_lo, s_raw, s_hi))):
                    dve.wait_ge(rounded, 5 * i + n + 1)
                    nc.vector.tensor_tensor(lo[:], raw[:], hi[:].bitcast(F32), ALU.subtract).then_inc(split, 1)
                for c in range(2):
                    last = nc.vector.tensor_tensor(qd[:, c, :], q_raw[:, c, SEQ:TOK], qdec[:], ALU.mult)
                last.then_inc(q_decayed, 1)
                for p in range(5):
                    n = 2 if p < 4 else 1
                    dve.wait_ge(transposed, 5 * i + p + 1)
                    if p >= 2:
                        dve.wait_ge(kt_split, 5 * i + p - 1)
                    for m in range(n):
                        t = 2 * p + m
                        at = (6 + p % 2) * BANK + m * DK
                        nc.vector.tensor_scalar(kt[:, p % 2, m, :], psum[:, at:at + DK], cols[:, t:t + 1], None,
                                                ALU.mult).then_inc(kt_decayed, 1)
                    dve.wait_ge(kt_rounded, 5 * i + p + 1)
                    nc.vector.tensor_tensor(kt_lo[:, 2 * p:2 * p + n, :], kt[:, p % 2, 0:n, :],
                                            kt_hi[:, 2 * p:2 * p + n, :].bitcast(F32), ALU.subtract)\
                        .then_inc(kt_split, 1)
                dve.wait_ge(rounded, 5 * i + 5)
                nc.vector.tensor_tensor(qd_lo[:], qd[:], qd_hi[:].bitcast(F32), ALU.subtract).then_inc(split_qd, 1)
                dve.wait_ge(states, i + 1)
                nc.vector.scalar_tensor_tensor(work[:, 1, 0:2 * DV], s_raw[:].rearrange("p c n -> p (c n)"),
                                               cols[:, TT:TT + 1], psum[:, 2 * DV:4 * DV], ALU.mult, ALU.add)\
                    .then_inc(states_summed, 1)
                for s, (b, j, n0, n) in enumerate(steps):
                    dve.wait_ge(scored, NS * i + s + 1)
                    if s >= 2:
                        dve.wait_ge(w_split, NS * i + s - 1)
                    off = n0 - j * P
                    nc.vector.tensor_tensor(w[:, s % 2, 0:n], bank(4 + s % 2, n), table[:, off:off + n], ALU.mult)\
                        .then_inc(weighted, 1)
                for c in range(NV):
                    dve.wait_ge(squared, NV * i + c + 1)
                    if c == 0:
                        nc.vector.tensor_copy(acc[:], work[:, 0, :]).then_inc(summed, 1)
                    else:
                        dve.wait_ge(summed, NV * i + c)
                        nc.vector.tensor_tensor(acc[:], acc[:], work[:, c % 2, :], ALU.add).then_inc(summed, 1)
                dve.wait_ge(summed, NV * i + NV)
                nc.vector.tensor_copy(acc_hi, acc[:]).then_inc(acc_split, 1)
                dve.wait_ge(acc_split, 2 * i + 1)
                nc.vector.tensor_tensor(acc_lo, acc[:], acc_hi.bitcast(F32), ALU.subtract).then_inc(acc_split, 1)
                dve.wait_ge(acc_split, 2 * i + 2)
                dve.wait_ge(rooted, i + 1)
                nc.vector.reciprocal(acc[:], rs[:]).then_inc(inverted, 1)
                dve.wait_ge(inverted, i + 1)
                for c in range(NV):
                    nc.vector.scalar_tensor_tensor(work[:, c % 2, :], y[:, c, :], cols[:, TT + 1 + c:TT + 2 + c],
                                                   acc[:], ALU.mult, ALU.mult).then_inc(normed, 1)
                    dve.wait_ge(normed, NV * i + c + 1)
                    dve.wait_ge(gate_loaded, 16 * (NV * i + c + 1))
                    nc.vector.tensor_tensor(y[:, c, :], work[:, c % 2, :], gate[:], ALU.mult).then_inc(gated, 1)

        @block.tensor
        def _(pe):
            pe.wait_ge(const_loaded, 16)
            pe.wait_ge(padded, 3)
            three = lambda a_hi, a_lo, b_hi, b_lo: ((a_hi, b_hi), (a_hi, b_lo), (a_lo, b_hi))

            def scores(i, s):
                b, j, n0, n = steps[s]
                if s >= 2:
                    pe.wait_ge(weighted, NS * i + s - 1)
                for c in range(2):
                    for m, (k, q) in enumerate(three(k_hi, k_lo, q_hi, q_lo)):
                        last = nc.tensor.matmul(bank(4 + s % 2, n), k[:, c, j * P:(j + 1) * P], q[:, c, n0:n0 + n],
                                                start=(c == 0 and m == 0), stop=(c == 1 and m == 2))
                last.then_inc(scored, 1)
            with pe.Fori(0, HR) as i:
                pe.wait_ge(qk_loaded, 32 * i + 32)
                pe.wait_ge(rooted, i)
                for p in range(5):
                    n = 2 if p < 4 else 1
                    if p >= 2:
                        pe.wait_ge(kt_decayed, TT * i + 2 * p - 2)
                    for m in range(n):
                        for c in range(2):
                            t, at = 2 * p + m, (6 + p % 2) * BANK + m * DK + c * P
                            last = nc.tensor.transpose(psum[:, at:at + P], k_raw[:, c, t * P:(t + 1) * P], ident[:])
                    last.then_inc(transposed, 1)
                pe.wait_ge(kt_split, 5 * i + 5)
                pe.wait_ge(split, 4 * i + 3)
                for c in range(2):
                    cols_c = slice(c * P, (c + 1) * P)
                    for t in range(TT - 1):
                        for m, (k, v) in enumerate(three(kt_hi, kt_lo, v_hi, v_lo)):
                            nc.tensor.matmul(bank(c), k[:, t, cols_c], v[:, t, :],
                                             start=(t == 0 and m == 0), stop=(t == TT - 2 and m == 2))
                    for m, (k, v) in enumerate(three(kt_hi, kt_lo, v_hi, v_lo)):
                        last = nc.tensor.matmul(bank(2 + c), k[:, TT - 1, cols_c], v[:, TT - 1, :],
                                                start=(m == 0), stop=(m == 2))
                last.then_inc(states, 1)
                pe.wait_ge(split_qd, i + 1)
                scores(i, 0)
                pe.wait_ge(states_copied, i + 1)
                pe.wait_ge(states_summed, i + 1)
                for s, (b, j, n0, n) in enumerate(steps):
                    if s + 1 < NS:
                        scores(i, s + 1)
                    pe.wait_ge(w_split, NS * i + s + 1)
                    first = s == 0 or s - 1 in ends
                    if first and b > 0:
                        pe.wait_ge(y_copied, 3 * i + b)
                    for c in range(NV):
                        out = psum[:, c * BANK + n0 - b * BANK:c * BANK + n0 - b * BANK + n]
                        vc = slice(c * P, (c + 1) * P)
                        if b == 2:
                            for kc in range(2):
                                for m, (st, q) in enumerate(three(s_hi, s_lo, qd_hi, qd_lo)):
                                    nc.tensor.matmul(out, st[:, kc, vc], q[:, kc, :],
                                                     start=(kc == 0 and m == 0), stop=False)
                        for m, (v, x) in enumerate(three(v_hi, v_lo, w_hi, w_lo)):
                            last = nc.tensor.matmul(out, v[:, j, vc], x[:, s % 2, 0:n],
                                                    start=(first and b < 2 and m == 0), stop=(s in ends and m == 2))
                    last.then_inc(y_step, 1)
                pe.wait_ge(acc_split, 2 * i + 2)
                for n, part in enumerate((acc_hi, acc_lo)):
                    for s, (t0, width) in enumerate(SLABS):
                        last = nc.tensor.matmul(bank(4 + s, width), g.ones_r[:, :], part[:, t0:t0 + width],
                                                start=(n == 0), stop=(n == 1))
                last.then_inc(total, 1)


def fox(nc, g):
    UH = TT
    U = 2 * UH
    order = [u for n in range(4) for u in (n, 7 - n)] + [UH - 1]
    units = [(j, u, (0 if u < UH - 1 else UH - 1), (u + 1 if u < UH - 1 else KT - UH + 1))
             for j in range(2) for u in order]
    groups = [(n, t0, min(4, kt - t0)) for n, (_, _, _, kt) in enumerate(units) for t0 in range(0, kt, 4)]
    NG = len(groups)
    last_group = [max(x for x, q in enumerate(groups) if q[0] == n) for n in range(U)]
    outs = [(9 * j + a, 9 * j + b) for j in range(2) for a, b in ((0, 4), (4, 8), (8, 9))]
    NO = len(outs)
    out_of = [next(x for x, (a, b) in enumerate(outs) if a <= n < b) for n in range(U)]
    tails = [(3, 0, 3), (3, 3, 2), (4, 5, 2), (4, 7, 2)]
    NTL = len(tails)
    tail_bank = [(min(x for x, q in enumerate(groups) if q[0] == n) + y) % 2 for y, (n, _, _) in enumerate(tails)]
    after_tail = {min(x for x, q in enumerate(groups) if q[0] == n) + y % 2: y for y, (n, _, _) in enumerate(tails)}
    with ExitStack() as es:
        sb = lambda n, s, dt=F32: es.enter_context(nc.sbuf_tensor(f"fx_{n}", s, dt))
        sem = semaphores(nc, es, "fx")
        two = lambda n: [sem(f"{n}{j}") for j in range(2)]
        k_raw, q_raw, v_raw = sb("k_raw", [P, 2, KEYS]), sb("q_raw", [P, 2, TOKP]), sb("v_raw", [P, 2, KT, DF])
        q_a, q_b = sb("q_a", [P, 2, TOKP], F32R), sb("q_b", [DF + 4, 2, TOKP], F32R)
        k_a, k_b = sb("k_a", [P, 2, KEYS], F32R), sb("k_b", [DF + 4, 2, KEYS], F32R)
        v_a = sb("v_a", [P, 2, KT, 2 * DF], F32R)
        e = sb("e", [P, 2, SEQ])
        p_hi, p_lo = sb("p_hi", [P, 2, 8 * P], F32R), sb("p_lo", [P, 2, 8 * P], F32R)
        neg_max, rowsum, inv = sb("neg_max", [P, U]), sb("rowsum", [P, U]), sb("inv", [P, U])
        o_low, o_tok, o_t = sb("o_low", [P, 2, 4, DF]), sb("o_tok", [P, TT, P]), sb("o_t", [P, TOK])
        ident, masks = sb("ident", [P, P]), sb("masks", [P, 2, P])
        ident_r, masks_r = sb("ident_r", [P, P], F32R), sb("masks_r", [P, 2, P], F32R)
        raw_loaded, rows_loaded = two("raw_loaded"), two("rows_loaded")
        const_loaded, const_ready, padded = sem("const_loaded"), sem("const_ready"), sem("padded")
        rounded, split = sem("rounded"), sem("split")
        scored, maxed, exped = sem("scored"), sem("maxed"), sem("exped")
        transposed, p_rounded, p_split = sem("transposed"), sem("p_rounded"), sem("p_split")
        pv, o_lowered, o_summed, o_done = sem("pv"), sem("o_lowered"), sem("o_summed"), sem("o_done")
        inverted, tail_transposed, tail_copied, o_stored = (sem("inverted"), sem("tail_transposed"),
                                                            sem("tail_copied"), sem("o_stored"))
        psum = g.psum
        block = es.enter_context(nc.Block())
        PAIRS = HF // 2

        @block.sync
        def _(sp):
            def load_raw(i, j):
                rows = slice(j * DF, (j + 1) * DF)
                for half in (slice(0, DF), slice(DF, P)):
                    sp.dma_start(k_raw[half, j, 0:SEQ], g.qk_out[i + DC, rows, 0:SEQ]).then_inc(raw_loaded[j], 16)
                    sp.dma_start(k_raw[half, j, SEQ:SEQ + PAST], g.cache_kt[2 * i + j, :, :]).then_inc(raw_loaded[j], 16)
                    sp.dma_start(k_raw[half, j, SEQ + PAST:SEQ + PAST + DEC], g.qk_out[i + DC, rows, SEQ:TOK])\
                        .then_inc(raw_loaded[j], 16)
                    sp.dma_start(q_raw[half, j, 0:TOK], g.qk_out[i, rows, :]).then_inc(raw_loaded[j], 16)
                cols = bass.ds(i * P + j * DF, DF)
                sp.dma_start(v_raw[:, j, 0:8, :], g.v_out[0:SEQ, cols].rearrange("(t p) n -> p t n", p=P))\
                    .then_inc(raw_loaded[j], 16)
                sp.dma_start(v_raw[:, j, 8:10, :], g.cache_v[:, cols].rearrange("(t p) n -> p t n", p=P))\
                    .then_inc(raw_loaded[j], 16)
                sp.dma_start(v_raw[0:DEC, j, 10, :], g.v_out[SEQ:TOK, cols]).then_inc(raw_loaded[j], 16)

            def load_rows(i, j):
                sp.dma_start(q_b[DF:DF + 4, j, 0:TOK].bitcast(F32), g.q_rows[2 * i + j, :, :])\
                    .then_inc(rows_loaded[j], 16)
                sp.dma_start(k_b[DF:DF + 4, j, :].bitcast(F32), g.k_rows[2 * i + j, :, :]).then_inc(rows_loaded[j], 16)

            def store(i):
                sp.wait_ge(tail_copied, NTL * i + NTL)
                sp.dma_start(g.o_fox[i, :, :], o_t[:]).then_inc(o_stored, 16)

            def pair(i, next_i, first=False):
                if not first:
                    sp.wait_ge(scored, U * i)
                load_rows(i, 1)
                if next_i is not None:
                    sp.wait_ge(split, 6 * i + 3)
                    load_raw(next_i, 0)
                if not first:
                    store(i - 1)
                if next_i is not None:
                    sp.wait_ge(split, 6 * i + 6)
                    load_raw(next_i, 1)
                    sp.wait_ge(scored, U * i + UH)
                    load_rows(next_i, 0)
            sp.dma_start(ident[:], g.ident_t).then_inc(const_loaded, 16)
            sp.dma_start(masks[:], g.masks).then_inc(const_loaded, 16)
            sp.wait_ge(padded, 4)
            load_raw(0, 0)
            load_rows(0, 0)
            load_raw(0, 1)
            sp.sem_inc(o_stored, 16)
            pair(0, 1, first=True)
            with sp.Fori(1, PAIRS - 1) as i:
                pair(i, i + 1)
            pair(PAIRS - 1, None)
            store(PAIRS - 1)
            sp.wait_ge(o_stored, 16 * PAIRS + 16)

        @block.scalar
        def _(act):
            act.wait_ge(const_loaded, 32)
            nc.scalar.activation(ident_r[:], ident[:], ACT.Copy).then_inc(const_ready, 1)
            nc.scalar.activation(masks_r[:], masks[:], ACT.Copy).then_inc(const_ready, 1)
            act.wait_ge(padded, 4)

            def round_part(i, j, part):
                if part == 0:
                    act.wait_ge(raw_loaded[j], 11 * 16 * (i + 1))
                    nc.scalar.activation(k_a[:, j, :], k_raw[:, j, :], ACT.Copy).then_inc(rounded, 1)
                elif part == 1:
                    nc.scalar.activation(q_a[:, j, :], q_raw[:, j, :], ACT.Copy, scale=DF ** -0.5).then_inc(rounded, 1)
                elif part == 2:
                    nc.scalar.activation(q_b[0:DF, j, :], q_raw[0:DF, j, :], ACT.Copy,
                                         scale=DF ** -0.5).then_inc(rounded, 1)
                else:
                    nc.scalar.activation(v_a[:, j, :, 0:DF], v_raw[:, j, :, :], ACT.Copy).then_inc(rounded, 1)

            def exp(i, n, first):
                j, u, k0, kt = units[n]
                act.wait_ge(maxed, U * i + n + 1)
                if n >= 2:
                    act.wait_ge(transposed, NG * i + last_group[n - 2] + 1)
                elif not first:
                    act.wait_ge(transposed, NG * i - NG + last_group[n - 2 + U] + 1)
                s0 = (n % 2) * 2 * BANK
                nc.scalar.activation(e[:, n % 2, 0:kt * P], psum[:, s0:s0 + kt * P], ACT.Exp,
                                     bias=neg_max[:, n:n + 1], accum_out=rowsum[:, n:n + 1]).then_inc(exped, 1)

            def lower(i, x, first=False):
                a, b = outs[x]
                act.wait_ge(pv, U * i + b)
                if x >= 2 or not first:
                    act.wait_ge(o_summed, NO * i + x - 1)
                at = (6 + x % 2) * BANK
                nc.scalar.activation(o_low[:, x % 2, 0:b - a, :],
                                     psum[:, at:at + (b - a) * P].rearrange("p (t n) -> p t n", n=P)[:, :, DF:P],
                                     ACT.Copy).then_inc(o_lowered, 1)

            def tail(i, y):
                _, t0, nt = tails[y]
                act.wait_ge(tail_transposed, NTL * i + y + 1)
                if y == 0:
                    act.wait_ge(o_stored, 16 * i + 16)
                for t in range(t0, t0 + nt):
                    at, u = (4 + tail_bank[y]) * BANK + (t - t0) * P, order[t]
                    width = P if u < UH - 1 else DEC
                    last = nc.scalar.activation(o_t[:, u * P:u * P + width], psum[:, at:at + width], ACT.Copy)
                last.then_inc(tail_copied, 1)

            def pair(i, next_i, first=False):
                for n in range(U):
                    if n + 1 < U:
                        exp(i, n + 1, first)
                    elif next_i is not None:
                        exp(next_i, 0, False)
                    for x, (a, b) in enumerate(outs):
                        if b + 1 == n:
                            lower(i, x, first)
                        elif b + 1 == n + U and not first:
                            lower(i - 1, x)
                    for y, (m, _, _) in enumerate(tails):
                        if m == n and not first:
                            tail(i - 1, y)
                    for x, (m, t0, nt) in enumerate(groups):
                        if m == n:
                            act.wait_ge(transposed, NG * i + x + 1)
                            if n >= 2 or not first:
                                act.wait_ge(pv, U * i + n - 1)
                            at = (4 + x % 2) * BANK
                            nc.scalar.activation(p_hi[:, n % 2, t0 * P:(t0 + nt) * P], psum[:, at:at + nt * P],
                                                 ACT.Copy).then_inc(p_rounded, 1)
                    if 1 <= n <= 4:
                        if n == 1 and not first:
                            act.wait_ge(pv, U * i)
                        round_part(i, 1, n - 1)
                    if UH + 1 <= n <= UH + 4 and next_i is not None:
                        if n == UH + 1:
                            act.wait_ge(pv, U * i + UH)
                        round_part(next_i, 0, n - UH - 1)
            for part in range(4):
                round_part(0, 0, part)
            exp(0, 0, True)
            pair(0, 1, first=True)
            with act.Fori(1, PAIRS - 1) as i:
                pair(i, i + 1)
            pair(PAIRS - 1, None)
            lower(PAIRS - 1, NO - 2)
            lower(PAIRS - 1, NO - 1)
            for y in range(NTL):
                tail(PAIRS - 1, y)

        @block.vector
        def _(dve):
            nc.vector.memset(k_raw[:, :, SEQ + PAST + DEC:KEYS], 0.0).then_inc(padded, 1)
            nc.vector.memset(q_raw[:, :, TOK:TOKP], 0.0).then_inc(padded, 1)
            nc.vector.memset(v_raw[DEC:P, :, 10, :], 0.0).then_inc(padded, 1)
            nc.vector.memset(q_b[DF:DF + 4, :, TOK:TOKP].bitcast(F32), 0.0).then_inc(padded, 1)
            dve.wait_ge(padded, 4)

            def split_part(i, j, part):
                n = 8 * i + 4 * j
                if part == 0:
                    dve.wait_ge(rounded, n + 1)
                    nc.vector.tensor_tensor(k_b[0:DF, j, :], k_raw[0:DF, j, :], k_a[0:DF, j, :].bitcast(F32),
                                            ALU.subtract).then_inc(split, 1)
                elif part == 1:
                    dve.wait_ge(rounded, n + 2)
                    nc.vector.scalar_tensor_tensor(q_a[DF:P, j, :], q_raw[DF:P, j, :], DF ** -0.5,
                                                   q_a[DF:P, j, :].bitcast(F32), ALU.mult,
                                                   ALU.subtract).then_inc(split, 1)
                else:
                    dve.wait_ge(rounded, n + 4)
                    nc.vector.tensor_tensor(v_a[:, j, :, DF:P], v_raw[:, j, :, :], v_a[:, j, :, 0:DF].bitcast(F32),
                                            ALU.subtract).then_inc(split, 1)

            def row_max(i, n):
                j, u, k0, kt = units[n]
                dve.wait_ge(scored, U * i + n + 1)
                s0 = (n % 2) * 2 * BANK
                nc.vector.reduce_max(neg_max[:, n:n + 1], psum[:, s0:s0 + kt * P], AX, negate=True).then_inc(maxed, 1)

            def finish(i, x, first=False):
                a, b = outs[x]
                at = (6 + x % 2) * BANK
                o = o_tok[:, a % UH:a % UH + b - a, (a // UH) * DF:(a // UH + 1) * DF]
                nc.vector.reciprocal(inv[:, a:b], rowsum[:, a:b]).then_inc(inverted, 1)
                dve.wait_ge(o_lowered, NO * i + x + 1)
                if x == 0 and not first:
                    dve.wait_ge(tail_transposed, NTL * i)
                nc.vector.tensor_tensor(o, psum[:, at:at + (b - a) * P].rearrange("p (t n) -> p t n", n=P)[:, :, 0:DF],
                                        o_low[:, x % 2, 0:b - a, :], ALU.add).then_inc(o_summed, 1)
                dve.wait_ge(o_summed, NO * i + x + 1)
                dve.wait_ge(inverted, NO * i + x + 1)
                nc.vector.tensor_tensor(o, o, inv[:, a:b].unsqueeze(2).to_broadcast([P, b - a, DF]),
                                        ALU.mult).then_inc(o_done, 1)

            def pair(i, next_i, first=False):
                for n in range(U):
                    if n + 2 < U:
                        row_max(i, n + 2)
                    elif next_i is not None:
                        row_max(next_i, n + 2 - U)
                    for x, (a, b) in enumerate(outs):
                        if b + 1 == n:
                            finish(i, x, first)
                        elif b + 1 == n + U and not first:
                            finish(i - 1, x)
                    for x, (m, t0, nt) in enumerate(groups):
                        if m == n:
                            dve.wait_ge(p_rounded, NG * i + x + 1)
                            at = (4 + x % 2) * BANK
                            nc.vector.tensor_tensor(p_lo[:, n % 2, t0 * P:(t0 + nt) * P], psum[:, at:at + nt * P],
                                                    p_hi[:, n % 2, t0 * P:(t0 + nt) * P].bitcast(F32),
                                                    ALU.subtract).then_inc(p_split, 1)
                    if n in (2, 3, 5):
                        split_part(i, 1, (2, 3, 5).index(n))
                    if n - UH in (2, 3, 5) and next_i is not None:
                        split_part(next_i, 0, (2, 3, 5).index(n - UH))
            for part in range(3):
                split_part(0, 0, part)
            row_max(0, 0)
            row_max(0, 1)
            pair(0, 1, first=True)
            with dve.Fori(1, PAIRS - 1) as i:
                pair(i, i + 1)
            pair(PAIRS - 1, None)
            finish(PAIRS - 1, NO - 2)
            finish(PAIRS - 1, NO - 1)

        @block.tensor
        def _(pe):
            pe.wait_ge(const_ready, 2)

            def score(i, n):
                j, u, k0, kt = units[n]
                if n % UH == 0:
                    pe.wait_ge(split, 6 * i + 3 * j + 3)
                    pe.wait_ge(rows_loaded[j], 32 * i + 32)
                q = slice(u * P, (u + 1) * P)
                s0 = (n % 2) * 2 * BANK
                for t in range(0, kt, 4):
                    nt = min(4, kt - t)
                    out = psum[:, s0 + t * P:s0 + (t + nt) * P]
                    keys = slice((k0 + t) * P, (k0 + t + nt) * P)
                    masked = t + nt == kt
                    nc.tensor.matmul(out, q_a[:, j, q], k_a[:, j, keys], start=True, stop=False)
                    last = nc.tensor.matmul(out, q_b[:, j, q], k_b[:, j, keys], start=False, stop=not masked)
                    if masked:
                        last = nc.tensor.matmul(psum[:, s0 + (kt - 1) * P:s0 + kt * P], ident_r[:],
                                                masks_r[:, 0 if u < UH - 1 else 1, :], start=False, stop=True)
                last.then_inc(scored, 1)

            def transpose(i, n, first):
                for x, (m, t0, nt) in enumerate(groups):
                    if m == n:
                        if x in after_tail and not first:
                            pe.wait_ge(tail_copied, NTL * i - NTL + after_tail[x] + 1)
                        elif x >= 2 or not first:
                            pe.wait_ge(p_split, NG * i + x - 1)
                        for t in range(nt):
                            at = (4 + x % 2) * BANK + t * P
                            last = nc.tensor.transpose(psum[:, at:at + P], e[:, n % 2, (t0 + t) * P:(t0 + t + 1) * P],
                                                       ident[:])
                        last.then_inc(transposed, 1)

            def values(i, n, first=False):
                j, u, k0, kt = units[n]
                x = out_of[n]
                pe.wait_ge(p_split, NG * i + last_group[n] + 1)
                if n == outs[x][0] and (x >= 2 or not first):
                    pe.wait_ge(o_summed, NO * i + x - 1)
                at = (6 + x % 2) * BANK + (n - outs[x][0]) * P
                for t in range(kt):
                    keys = slice(t * P, (t + 1) * P)
                    nc.tensor.matmul(psum[:, at:at + P], p_hi[:, n % 2, keys], v_a[:, j, k0 + t, :],
                                     start=(t == 0), stop=False)
                    last = nc.tensor.matmul(psum[:, at:at + DF], p_lo[:, n % 2, keys], v_a[:, j, k0 + t, 0:DF],
                                            start=False, stop=(t == kt - 1))
                last.then_inc(pv, 1)

            def tail(i, y, splits):
                _, t0, nt = tails[y]
                pe.wait_ge(o_done, NO * i + NO)
                pe.wait_ge(p_split, splits)
                if y >= 2 and tails[y - 2][0] == tails[y][0]:
                    pe.wait_ge(tail_copied, NTL * i + y - 1)
                for t in range(t0, t0 + nt):
                    at = (4 + tail_bank[y]) * BANK + (t - t0) * P
                    last = nc.tensor.transpose(psum[:, at:at + P], o_tok[:, t, :], ident[:])
                last.then_inc(tail_transposed, 1)

            def pair(i, next_i, first=False):
                for n in range(U):
                    pe.wait_ge(exped, U * i + n + 1)
                    if n + 2 < U:
                        score(i, n + 2)
                    elif next_i is not None:
                        score(next_i, n + 2 - U)
                    own_tails = [y for y, q in enumerate(tails) if q[0] == n and not first]
                    for y in own_tails:
                        tail(i - 1, y, NG * i + last_group[n - 1] + y % 2)
                    if own_tails:
                        values(i, n - 1, first)
                    transpose(i, n, first)
                    if n >= 1 and not own_tails:
                        values(i, n - 1, first)
                    if n == 0 and not first:
                        values(i - 1, U - 1)
            score(0, 0)
            score(0, 1)
            pair(0, 1, first=True)
            with pe.Fori(1, PAIRS - 1) as i:
                pair(i, i + 1)
            pair(PAIRS - 1, None)
            values(PAIRS - 1, U - 1)
            for y in range(NTL):
                if y >= 2:
                    pe.wait_ge(tail_copied, NTL * (PAIRS - 1) + y - 1)
                tail(PAIRS - 1, y, NG * PAIRS)


def project(nc, g, tag, weights, tiles, source, resident, evict, extras=()):
    op, out, gate_src = evict["op"], evict["out"], evict.get("gate")
    with ExitStack() as es:
        sb = lambda n, s, dt=F32: es.enter_context(nc.sbuf_tensor(f"{tag}_{n}", s, dt))
        sem = semaphores(nc, es, tag)
        two = lambda n: [sem(f"{n}{j}") for j in range(2)]
        x_hi, x_lo = sb("x_hi", [P, DC, TOK], F32R), sb("x_lo", [P, DC, TOK], F32R)
        x_raw = None if resident else sb("x_raw", [P, 2, TOK])
        raw, w_hi, w_lo = sb("raw", [P, 2, DC, P]), sb("w_hi", [P, 2, DC, P], F32R), sb("w_lo", [P, 2, DC, P], F32R)
        gate = sb("gate", [P, 2, TOK]) if gate_src is not None else None
        loaded, x_loaded, gate_loaded = two("loaded"), two("x_loaded"), two("gate_loaded")
        rounded, split, x_rounded, x_split = sem("rounded"), sem("split"), sem("x_rounded"), sem("x_split")
        multiplied, evicted, step = sem("multiplied"), sem("evicted"), sem("step")
        psum = g.psum
        block = es.enter_context(nc.Block())

        def chunk(c):
            return source[:, c, :] if resident else x_raw[:, c % 2, :]

        @block.sync
        def _(sp):
            def load(t):
                if t >= 2:
                    sp.wait_ge(split, t - 1)
                sp.dma_start(raw[:, t % 2].rearrange("p c n -> p (c n)"), weights(t)).then_inc(loaded[t % 2], 16)

            def load_gate(t):
                if gate is not None:
                    if t >= 2:
                        sp.wait_ge(evicted, t - 1)
                    sp.dma_start(gate[:, t % 2, :], gate_src(t)).then_inc(gate_loaded[t % 2], 16)
            load(0)
            if not resident:
                for c in range(DC):
                    if c >= 2:
                        sp.wait_ge(x_split, c - 1)
                    sp.dma_start(x_raw[:, c % 2, :], source(c)).then_inc(x_loaded[c % 2], 16)
            load(1)
            load_gate(0)
            load_gate(1)
            for t in range(2, tiles):
                load(t)
                load_gate(t)

        @block.scalar
        def _(act):
            def round_tile(t):
                act.wait_ge(loaded[t % 2], 16 * (t // 2 + 1))
                if t >= 2:
                    act.wait_ge(multiplied, t - 1)
                nc.scalar.activation(w_hi[:, t % 2], raw[:, t % 2], ACT.Copy).then_inc(rounded, 1)
            round_tile(0)
            for c in range(DC):
                if not resident:
                    act.wait_ge(x_loaded[c % 2], 16 * (c // 2 + 1))
                nc.scalar.activation(x_hi[:, c, :], chunk(c), ACT.Copy).then_inc(x_rounded, 1)
            for t in range(1, tiles):
                round_tile(t)

        @block.vector
        def _(dve):
            done = [0]

            def rest(t):
                dve.wait_ge(rounded, t + 1)
                nc.vector.tensor_tensor(w_lo[:, t % 2], raw[:, t % 2], w_hi[:, t % 2].bitcast(F32),
                                        ALU.subtract).then_inc(split, 1)
            rest(0)
            for c in range(DC):
                dve.wait_ge(x_rounded, c + 1)
                nc.vector.tensor_tensor(x_lo[:, c, :], chunk(c), x_hi[:, c, :].bitcast(F32),
                                        ALU.subtract).then_inc(x_split, 1)
            for t in range(tiles):
                if t + 1 < tiles:
                    rest(t + 1)
                dve.wait_ge(multiplied, t + 1)
                if gate is not None:
                    dve.wait_ge(gate_loaded[t % 2], 16 * (t // 2 + 1))
                s = slab_views(psum, 3 * (t % 2), out[:, t, :])
                gv = slab_views(psum, 0, gate[:, t % 2, :]) if gate is not None else s
                for n in range(2):
                    (p, o), (_, x) = s[n], gv[n]
                    if op == "copy":
                        last = nc.vector.tensor_copy(o, p)
                    elif op in ("mul", "add"):
                        last = nc.vector.tensor_tensor(o, p, x, ALU.mult if op == "mul" else ALU.add)
                    else:
                        last = nc.vector.tensor_tensor(o, p, o, ALU.add)
                if op == "add_mul_add":
                    last.then_inc(step, 1)
                    dve.wait_ge(step, 2 * t + 1)
                    nc.vector.tensor_tensor(out[:, t, :], out[:, t, :], gate[:, t % 2, :], ALU.mult).then_inc(step, 1)
                    dve.wait_ge(step, 2 * t + 2)
                    last = nc.vector.tensor_tensor(out[:, t, :], out[:, t, :], evict["plus"][:, t, :], ALU.add)
                last.then_inc(evicted, 1)

        @block.tensor
        def _(pe):
            for t in range(tiles):
                pe.wait_ge(split, t + 1)
                if t >= 2:
                    pe.wait_ge(evicted, t - 1)
                for c in range(DC):
                    if t == 0:
                        pe.wait_ge(x_split, c + 1)
                    for n, (w, x) in enumerate(((w_hi, x_hi), (w_hi, x_lo), (w_lo, x_hi))):
                        for s, (t0, width) in enumerate(SLABS):
                            at = (3 * (t % 2) + s) * BANK
                            last = nc.tensor.matmul(psum[:, at:at + width], w[:, t % 2, c, :], x[:, c, t0:t0 + width],
                                                    start=(c == 0 and n == 0), stop=(c == DC - 1 and n == 2))
                last.then_inc(multiplied, 1)


def merge(nc, g, x1):
    GA, GB = NSILU, NSILU + DC
    part_a = x1
    with nc.sbuf_tensor("part_r", [P, DC, TOK], F32) as part_r:
        project(nc, g, "ma", lambda t: g.w_branch[t, :, :], DC, lambda c: g.o_fox[c, :, :], False,
                {"op": "mul", "out": part_a, "gate": lambda t: g.gates[GA + t, :, :]})
        project(nc, g, "mr0", lambda t: g.w_branch[DC + t, :, :], DC, lambda c: g.o_ret[c, :, :], False,
                {"op": "copy", "out": part_r})
        project(nc, g, "mr1", lambda t: g.w_branch[2 * DC + t, :, :], DC, lambda c: g.o_ret[DC + c, :, :], False,
                {"op": "add_mul_add", "out": part_r, "plus": part_a, "gate": lambda t: g.gates[GB + t, :, :]})
        project(nc, g, "mo", lambda t: g.w_out[t, :, :], DC, part_r, True,
                {"op": "add", "out": x1, "gate": lambda t: g.x_t[t * P:(t + 1) * P, :]})


def mlp(nc, g, x1, h_hi, h_lo):
    GROUPS = DFF // D
    NT = 2 * DC
    with ExitStack() as es:
        sb = lambda n, s, dt=F32: es.enter_context(nc.sbuf_tensor(f"ml_{n}", s, dt))
        sem = semaphores(nc, es, "ml")
        raw, w_hi, w_lo = sb("raw", [P, DC, P]), sb("w_hi", [P, 2, DC, P], F32R), sb("w_lo", [P, 2, DC, P], F32R)
        u_hi, u_lo = sb("u_hi", [P, DC, TOK], F32R), sb("u_lo", [P, DC, TOK], F32R)
        relu = sb("relu", [P, TOK])
        loaded, rounded, split, multiplied = sem("loaded"), sem("rounded"), sem("split"), sem("multiplied")
        relued, squared, u_rounded, u_split, added = (sem("relued"), sem("squared"), sem("u_rounded"),
                                                      sem("u_split"), sem("added"))
        psum = g.psum
        block = es.enter_context(nc.Block())

        @block.sync
        def _(sp):
            with sp.Fori(0, GROUPS) as i:
                for k in range(NT):
                    src = g.w_up[DC * i + k, :, :] if k < DC else g.w_down[DC * i + k - DC, :, :]
                    sp.wait_ge(split, NT * i + k)
                    sp.dma_start(raw[:].rearrange("p c n -> p (c n)"), src).then_inc(loaded, 16)

        @block.scalar
        def _(act):
            def round_tile(i, k):
                act.wait_ge(loaded, 16 * (NT * i + k + 1))
                nc.scalar.activation(w_hi[:, k % 2], raw[:], ACT.Copy).then_inc(rounded, 1)

            def group(i, next_i):
                for k in range(NT):
                    if k + 1 < NT or next_i is not None:
                        act.wait_ge(multiplied, NT * i + k)
                        if k + 1 < NT:
                            round_tile(i, k + 1)
                        else:
                            round_tile(next_i, 0)
                    if k < DC:
                        act.wait_ge(squared, DC * i + k + 1)
                        nc.scalar.activation(u_hi[:, k, :], relu[:], ACT.Copy).then_inc(u_rounded, 1)
            round_tile(0, 0)
            with act.Fori(0, GROUPS - 1) as i:
                group(i, i + 1)
            group(GROUPS - 1, None)

        @block.vector
        def _(dve):
            def rest(i, k):
                dve.wait_ge(rounded, NT * i + k + 1)
                nc.vector.tensor_tensor(w_lo[:, k % 2], raw[:], w_hi[:, k % 2].bitcast(F32), ALU.subtract)\
                    .then_inc(split, 1)

            def group(i, next_i):
                for k in range(NT):
                    if k + 1 < NT:
                        rest(i, k + 1)
                    elif next_i is not None:
                        rest(next_i, 0)
                    dve.wait_ge(multiplied, NT * i + k + 1)
                    if k < DC:
                        for src, dst in slab_views(psum, 3 * (k % 2), relu):
                            last = nc.vector.tensor_scalar(dst, src, 0.0, None, ALU.max)
                        last.then_inc(relued, 1)
                        dve.wait_ge(relued, DC * i + k + 1)
                        nc.vector.tensor_tensor(relu[:], relu[:], relu[:], ALU.mult).then_inc(squared, 1)
                        dve.wait_ge(u_rounded, DC * i + k + 1)
                        nc.vector.tensor_tensor(u_lo[:, k, :], relu[:], u_hi[:, k, :].bitcast(F32), ALU.subtract)\
                            .then_inc(u_split, 1)
                        dve.wait_ge(u_split, DC * i + k + 1)
                    else:
                        for src, dst in slab_views(psum, 3 * (k % 2), x1[:, k - DC, :]):
                            last = nc.vector.tensor_tensor(dst, src, dst, ALU.add)
                        last.then_inc(added, 1)
            rest(0, 0)
            with dve.Fori(0, GROUPS - 1) as i:
                group(i, i + 1)
            group(GROUPS - 1, None)

        @block.tensor
        def _(pe):
            with pe.Fori(0, GROUPS) as i:
                for k in range(NT):
                    pe.wait_ge(split, NT * i + k + 1)
                    up = k < DC
                    if k < 2:
                        pe.wait_ge(added, DC * i)
                    elif k < DC + 2:
                        pe.wait_ge(relued, DC * i + k - 1)
                    else:
                        pe.wait_ge(added, DC * i + k - 1 - DC)
                    x_hi, x_lo = (h_hi, h_lo) if up else (u_hi, u_lo)
                    for c in range(DC):
                        if k == DC:
                            pe.wait_ge(u_split, DC * i + c + 1)
                        for n, (w, x) in enumerate(((w_hi, x_hi), (w_hi, x_lo), (w_lo, x_hi))):
                            for s, (t0, width) in enumerate(SLABS):
                                at = (3 * (k % 2) + s) * BANK
                                last = nc.tensor.matmul(psum[:, at:at + width], w[:, k % 2, c, :],
                                                        x[:, c, t0:t0 + width],
                                                        start=(c == 0 and n == 0), stop=(c == DC - 1 and n == 2))
                    last.then_inc(multiplied, 1)


class Shared:
    pass


def run(nc, a):
    with ExitStack() as es:
        g = Shared()
        (g.x_t, g.w_tok, g.w_feat, g.b_forget, g.g_attn, g.g_mlp, g.g_final, g.cos_t, g.sin_t, g.cache_logf,
         g.cache_kt, g.cache_v, g.state_in, g.w_branch, g.w_out, g.w_up, g.w_down,
         g.ret_cols, g.ret_decay, g.ret_qdec, g.masks, g.ident_t) = a["ins"]
        g.v_out, g.qk_out, g.logf_out, g.state_out, g.y_out = a["outs"]
        scratch = lambda n, s: nc.dram_tensor(n, s, F32, kind="Internal").ap()
        g.qk_ret, g.gates = scratch("qk_ret", [NROPE, P, TOK]), scratch("gates", [NSILU + NSIG, P, TOK])
        g.v_ret, g.o_ret = scratch("v_ret", [HR, TOK, DV]), scratch("o_ret", [2 * DC, P, TOK])
        g.o_fox = scratch("o_fox", [DC, P, TOK])
        g.q_rows, g.k_rows = scratch("q_rows", [HF, 4, TOK]), scratch("k_rows", [HF, 4, KEYS])
        g.psum = es.enter_context(nc.psum_tensor("psum", [P, 8 * BANK], F32))
        sb = lambda n, s, dt=F32: es.enter_context(nc.sbuf_tensor(n, s, dt))
        g.ones_r, g.eps = sb("ones_r", [P, P], F32R), sb("eps", [P, 1])
        zf = sb("zf", [HF, TOK])
        with nc.Block() as block:
            @block.vector
            def _(dve):
                nc.vector.memset(g.ones_r[:].bitcast(F32), 1.0)
                nc.vector.memset(g.eps[:], EPS)
        with ExitStack() as hs:
            h_hi = hs.enter_context(nc.sbuf_tensor("h_hi", [P, DC, TOKP], F32R))
            h_lo = hs.enter_context(nc.sbuf_tensor("h_lo", [P, DC, TOKP], F32R))
            with nc.Block() as block:
                @block.vector
                def _(dve):
                    nc.vector.memset(h_hi[:, :, TOK:TOKP].bitcast(F32), 0.0)
                    nc.vector.memset(h_lo[:, :, TOK:TOKP].bitcast(F32), 0.0)
            with nc.sbuf_tensor("x0", [P, DC, TOK], F32) as x0:
                rms_norm(nc, g, "n1", x0, g.x_t, g.g_attn, hi=h_hi[:, :, 0:TOK], lo=h_lo[:, :, 0:TOK])
            values(nc, g, h_hi, h_lo)
            features(nc, g, h_hi, h_lo, zf)
        decay(nc, g, zf)
        retention(nc, g)
        fox(nc, g)
        x1 = sb("x1", [P, DC, TOK])
        merge(nc, g, x1)
        with ExitStack() as hs:
            h_hi = hs.enter_context(nc.sbuf_tensor("m_hi", [P, DC, TOK], F32R))
            h_lo = hs.enter_context(nc.sbuf_tensor("m_lo", [P, DC, TOK], F32R))
            rms_norm(nc, g, "n2", x1, None, g.g_mlp, hi=h_hi, lo=h_lo)
            mlp(nc, g, x1, h_hi, h_lo)
        rms_norm(nc, g, "n3", x1, None, g.g_final, out=g.y_out)



def _tiles(w, chunks, width):
    k, n = w.shape
    return np.ascontiguousarray(w.reshape(chunks, P, n // width, width).transpose(2, 1, 0, 3)
                                .reshape(n // width, P, chunks * width))


def _cols(v):
    return np.ascontiguousarray(v.reshape(-1, P).T)


def _tables():
    f = np.float32
    inv = (f(10000.0) ** (-np.arange(0, DK, 2, dtype=f) / f(DK))).astype(f)
    pos = np.concatenate([np.arange(SEQ), PAST + np.arange(DEC)]).astype(f)
    ang = inv[:, None] * pos[None, :]
    lg = np.log(f(1.0) - f(2.0) ** (f(-5.0) - np.arange(HR, dtype=f))).astype(f)
    m, j = np.arange(P), np.arange(SEQ)
    dist = np.abs(j[None, :] - m[:, None]).astype(f)
    seen = (m[:, None] // CHUNK) <= (j[None, :] // CHUNK)
    kscale = f(DK ** -0.5)
    table = np.where(seen[None], np.exp(lg[:, None, None] * dist[None]), 0).astype(f) * kscale
    cols = np.zeros((HR, P, TT + 1), f)
    for t in range(TT - 1):
        cols[:, :, t] = np.exp(lg[:, None] * (SEQ - 1 - t * P - m)[None].astype(f)) * kscale
    cols[:, :DEC, TT - 1] = np.exp(lg[:, None] * (DEC - 1 - m[:DEC])[None].astype(f)) * kscale
    cols[:, :, TT] = np.exp(lg * f(DEC))[:, None]
    qdec = np.broadcast_to(np.exp(lg[:, None] * (np.arange(DEC, dtype=f) + 1))[:, None, :], (HR, P, DEC))
    q, k = np.arange(P)[:, None], np.arange(P)[None, :]
    masks = np.stack([np.where(k <= q, 0, NEG), np.where((k <= q) & (k < DEC), 0, NEG)], 1).astype(f)
    return (np.cos(ang).astype(f), np.sin(ang).astype(f), cols, np.ascontiguousarray(table),
            np.ascontiguousarray(qdec), np.ascontiguousarray(masks), np.eye(P, dtype=f))


def kernel(x_prompt, x_sample, cache_fox_k, cache_fox_v, cache_fox_logf, state_ret,
           g_attn, w_in, b_forget, g_ret_norm, w_branch, w_out, g_mlp, w_up, w_down, g_final):
    import concourse.bacc as bacc
    from concourse.bass_utils import run_bass_kernel_spmd

    npa = lambda v: np.asarray(v)
    x_t = np.ascontiguousarray(np.concatenate([npa(x_prompt)[0], npa(x_sample)[0]], 0).T)
    w_in, w_branch, w_out, w_up, w_down = (npa(w)[0] for w in (w_in, w_branch, w_out, w_up, w_down))
    widths = (1024, 1024, 1024, HF, 1024, 1024, 2048, 2048, 1024, 1024)
    qf, kf, vf, ff, qr, kr, vr, gr, ga, gb = np.split(w_in, np.cumsum(widths)[:-1], 1)
    w_tok = _tiles(np.concatenate([vf, vr], 1), DC, 512)
    w_feat = _tiles(np.concatenate([qf, kf, qr, kr, gr, ga, gb, ff, np.zeros((D, P - HF), np.float32)], 1), DC, P)
    cos, sin, cols, table, qdec, masks, ident = _tables()
    ret_cols = np.concatenate([cols, npa(g_ret_norm)[0].reshape(HR, DV // P, P).transpose(0, 2, 1)], 2)
    ins = {
        "x_t": x_t, "w_tok": w_tok, "w_feat": w_feat, "b_forget": npa(b_forget)[0].reshape(HF, 1),
        "g_attn": _cols(npa(g_attn)[0]), "g_mlp": _cols(npa(g_mlp)[0]), "g_final": _cols(npa(g_final)),
        "cos_t": cos, "sin_t": sin,
        "cache_logf": npa(cache_fox_logf)[0, 0].T, "cache_kt": npa(cache_fox_k)[0, 0].transpose(1, 2, 0),
        "cache_v": npa(cache_fox_v)[0, 0].reshape(PAST, HF * DF), "state_in": npa(state_ret)[0, 0],
        "w_branch": np.concatenate([_tiles(w_branch[n * D:(n + 1) * D], DC, P) for n in range(3)], 0),
        "w_out": _tiles(w_out, DC, P), "w_up": _tiles(w_up, DC, P),
        "w_down": np.concatenate([_tiles(w_down[n * D:(n + 1) * D], DC, P) for n in range(DFF // D)], 0),
        "ret_cols": ret_cols, "ret_decay": table, "ret_qdec": qdec, "masks": masks, "ident_t": ident,
    }
    ins = {n: np.ascontiguousarray(v) for n, v in ins.items()}
    outs = {"v": (TOK, D), "qk": (NPLAIN, P, TOK), "logf": (HF, TOK),
            "state": (2, HR, DK, DV), "y": (D, TOK)}
    nc = bacc.Bacc("TRN2", target_bir_lowering=False, num_devices=1)
    args = {
        "ins": [nc.dram_tensor(f"in_{n}", v.shape, F32, kind="ExternalInput").ap() for n, v in ins.items()],
        "outs": [nc.dram_tensor(f"out_{n}", s, F32, kind="ExternalOutput").ap() for n, s in outs.items()],
    }
    run(nc, args)
    got = run_bass_kernel_spmd(nc, [{f"in_{n}": v for n, v in ins.items()}], core_ids=[0]).results[0]
    v, qk, logf, state, y = (got[f"out_{n}"] for n in outs)
    y = y.T
    k = qk[DC:].reshape(D, TOK).T.reshape(TOK, HF, DF)
    v = v.reshape(TOK, HF, DF)
    f = logf.T
    own = np.ascontiguousarray
    return (own(y[None, :SEQ]), own(y[None, SEQ:]), own(k[None, None, :SEQ]), own(v[None, None, :SEQ]),
            own(f[None, None, :SEQ]), own(state[None, 0:1]), own(k[None, None, SEQ:]),
            own(v[None, None, SEQ:]), own(f[None, None, SEQ:]), own(state[None, 1:2]))
```

```python
from contextlib import ExitStack

import numpy as np
import concourse.bass as bass
from concourse import mybir

F32 = mybir.dt.float32
F32R = mybir.dt.float32r
ACT = mybir.ActivationFunctionType
ALU = mybir.AluOpType
AX = mybir.AxisListType.X

P = 128
D = 1024
DC = D // P
SEQ = 1024
DEC = 64
PAST = 256
TOK = SEQ + DEC
TOKP = SEQ + P
TT = TOKP // P
SLABS = ((0, 384), (384, 384), (768, 320))
BANK = 512
HF = 16
DF = 64
HR = 4
DK = 256
DV = 512
CHUNK = 64
DFF = 4096
EPS = 1e-6
NEG = -1e30
KEYS = SEQ + PAST + P
S_KEY0 = SEQ
KT = KEYS // P
NPLAIN, NROPE, NSILU, NSIG = 16, 16, 16, 16
NFEAT = NPLAIN + NROPE + NSILU + NSIG


def semaphores(nc, es, tag):
    handles = []

    def done():
        nc.clear_and_free_semaphores(handles)
        nc.all_engine_barrier()
    es.callback(done)

    def sem(name):
        handles.append(nc.alloc_semaphore(name=f"{tag}_{name}"))
        return handles[-1]
    return sem


def gemm_tile(nc, psum, bank, w_hi, w_lo, x_hi, x_lo, chunks):
    for c in range(chunks):
        for n, (w, x) in enumerate(((w_hi, x_hi), (w_hi, x_lo), (w_lo, x_hi))):
            for s, (t0, width) in enumerate(SLABS):
                at = (bank + s) * BANK
                last = nc.tensor.matmul(psum[:, at:at + width], w[:, c, :], x[:, c, t0:t0 + width],
                                        start=(c == 0 and n == 0), stop=(c == chunks - 1 and n == 2))
    return last


def slab_views(psum, bank, x):
    at = bank * BANK
    two = psum[:, at:at + 2 * BANK].rearrange("p (s n) -> p s n", n=BANK)[:, :, 0:384]
    return ((two, x[:, 0:768].rearrange("p (s n) -> p s n", n=384)),
            (psum[:, at + 2 * BANK:at + 2 * BANK + 320], x[:, 768:TOK]))


def rms_norm(nc, g, tag, x, load, gain, hi=None, lo=None, out=None):
    with ExitStack() as es:
        sb = lambda n, s, dt=F32: es.enter_context(nc.sbuf_tensor(f"{tag}_{n}", s, dt))
        sem = semaphores(nc, es, tag)
        gcol, sq, acc = sb("gcol", [P, DC]), sb("sq", [P, 2, TOK]), sb("acc", [P, TOK])
        rs, prod = sb("rs", [P, TOK]), sb("prod", [P, 2, TOK])
        loaded = [sem(f"loaded{c}") for c in range(DC)] if load is not None else None
        squared, summed = sem("squared"), sem("summed")
        total, logged, inverted = sem("total"), sem("logged"), sem("inverted")
        scaled, rounded, ready, stored = sem("scaled"), sem("rounded"), sem("gready"), [sem(f"stored{n}") for n in range(2)]
        rest_even, rest_odd = sem("rest_even"), sem("rest_odd")
        psum = g.psum
        block = es.enter_context(nc.Block())

        @block.sync
        def _(sp):
            sp.dma_start(gcol[:], gain).then_inc(ready, 16)
            if load is not None:
                for c in range(DC):
                    sp.dma_start(x[:, c, :], load[c * P:(c + 1) * P, :]).then_inc(loaded[c], 16)
            if out is not None:
                for c in range(DC):
                    sp.wait_ge(scaled, c + 1)
                    sp.dma_start(out[c * P:(c + 1) * P, :], prod[:, c % 2, :]).then_inc(stored[c % 2], 16)
                for n in range(2):
                    sp.wait_ge(stored[n], 16 * DC // 2)

        @block.scalar
        def _(act):
            for c in range(DC):
                if load is not None:
                    act.wait_ge(loaded[c], 16)
                if c >= 2:
                    act.wait_ge(summed, c - 1)
                nc.scalar.activation(sq[:, c % 2, :], x[:, c, :], ACT.Square).then_inc(squared, 1)
            act.wait_ge(total, 1)
            for a, b in slab_views(psum, 0, rs):
                last = nc.scalar.activation(b, a, ACT.Ln, bias=g.eps[:, 0:1], scale=1.0 / D)
            last.then_inc(logged, 1)
            act.wait_ge(logged, 1)
            nc.scalar.activation(rs[:], rs[:], ACT.Exp, scale=-0.5).then_inc(inverted, 1)
            if out is None:
                for c in range(DC):
                    act.wait_ge(scaled, c + 1)
                    nc.scalar.activation(hi[:, c, :], prod[:, c % 2, :], ACT.Copy).then_inc(rounded, 1)

        @block.gpsimd
        def _(pool):
            if out is None:
                for c in range(1, DC, 2):
                    pool.wait_ge(rounded, c + 1)
                    nc.gpsimd.tensor_tensor(lo[:, c, :], prod[:, c % 2, :], hi[:, c, :].bitcast(F32),
                                            ALU.subtract).then_inc(rest_odd, 1)

        @block.vector
        def _(dve):
            for c in range(DC):
                dve.wait_ge(squared, c + 1)
                if c == 0:
                    nc.vector.tensor_copy(acc[:], sq[:, 0, :]).then_inc(summed, 1)
                else:
                    dve.wait_ge(summed, c)
                    nc.vector.tensor_tensor(acc[:], acc[:], sq[:, c % 2, :], ALU.add).then_inc(summed, 1)
            dve.wait_ge(inverted, 1)
            dve.wait_ge(ready, 16)
            for c in range(DC):
                if c >= 2 and out is not None:
                    dve.wait_ge(stored[c % 2], 16 * (c // 2))
                if c >= 2 and out is None and c % 2 == 1:
                    dve.wait_ge(rest_odd, (c - 1) // 2)
                if out is None and c >= 2 and c % 2 == 0:
                    dve.wait_ge(rest_even, c // 2)
                nc.vector.scalar_tensor_tensor(prod[:, c % 2, :], x[:, c, :], gcol[:, c:c + 1], rs[:],
                                               ALU.mult, ALU.mult).then_inc(scaled, 1)
                if out is None and c % 2 == 0:
                    dve.wait_ge(rounded, c + 1)
                    nc.vector.tensor_tensor(lo[:, c, :], prod[:, c % 2, :], hi[:, c, :].bitcast(F32),
                                            ALU.subtract).then_inc(rest_even, 1)

        @block.tensor
        def _(pe):
            pe.wait_ge(summed, DC)
            for s, (t0, width) in enumerate(SLABS):
                last = nc.tensor.matmul(psum[:, s * BANK:s * BANK + width], g.ones[:, :], acc[:, t0:t0 + width],
                                        start=True, stop=True)
            last.then_inc(total, 1)


def values(nc, g, h_hi, h_lo):
    GROUP = 512
    with ExitStack() as es:
        sb = lambda n, s, dt=F32: es.enter_context(nc.sbuf_tensor(f"val_{n}", s, dt))
        sem = semaphores(nc, es, "val")
        raw = sb("raw", [P, DC, GROUP])
        w_hi, w_lo = sb("w_hi", [P, 2, DC, GROUP], F32R), sb("w_lo", [P, 2, DC, GROUP], F32R)
        stage = sb("stage", [P, 2, GROUP])
        loaded, rounded, split = sem("loaded"), sem("rounded"), sem("split")
        multiplied, staged, stored = sem("multiplied"), sem("staged"), [sem(f"stored{n}") for n in range(2)]
        psum, BANKS = g.psum, 6
        tiles = 2 * TT
        block = es.enter_context(nc.Block())

        @block.sync
        def _(sp):
            for n in range(2):
                sp.sem_inc(stored[n], 16)

            def load(i, j, splits):
                sp.wait_ge(split, splits)
                sp.dma_start(raw[:].rearrange("p c n -> p (c n)"),
                             g.w_tok[2 * i + j, :, :]).then_inc(loaded, 16)

            def store(i, next_i, dst, prompt0=0, sample0=SEQ):
                for k in range(tiles):
                    if next_i is not None and k in (4, TT + 4):
                        load(next_i, k // TT, 2 * i + k // TT + 2)
                    j, t = k // TT, k % TT
                    rows = DEC if t == TT - 1 else P
                    sp.wait_ge(staged, tiles * i + k + 1)
                    row = sample0 if t == TT - 1 else prompt0 + t * P
                    sp.dma_start(dst(j)[row:row + rows, :],
                                 stage[0:rows, k % 2, :]).then_inc(stored[k % 2], 16)
            load(0, 0, 0)
            load(0, 1, 1)
            store(0, 1, lambda j: g.v_out[:, j * GROUP:(j + 1) * GROUP])
            with sp.Fori(1, 2) as i:
                store(i, i + 1, lambda j: g.v_ret[2 * i - 2 + j, :, :], DEC, 0)
            store(2, None, lambda j: g.v_ret[2 + j, :, :], DEC, 0)
            for n in range(2):
                sp.wait_ge(stored[n], 16 + 16 * 3 * tiles // 2)

        @block.scalar
        def _(act):
            def round_group(i, j):
                act.wait_ge(loaded, 32 * i + 16 * (j + 1))
                nc.scalar.activation(w_hi[:, j], raw[:], ACT.Copy).then_inc(rounded, 1)
            round_group(0, 0)
            round_group(0, 1)
            with act.Fori(1, 3) as i:
                for j in range(2):
                    act.wait_ge(multiplied, tiles * i - TT * (1 - j))
                    round_group(i, j)

        @block.vector
        def _(dve):
            def take(i, j):
                dve.wait_ge(rounded, 2 * i + j + 1)
                nc.vector.tensor_tensor(w_lo[:, j], raw[:], w_hi[:, j].bitcast(F32),
                                        ALU.subtract).then_inc(split, 1)
            take(0, 0)

            def evict(i, next_i):
                for k in range(tiles):
                    if k == 3:
                        take(i, 1)
                    if k == TT + 3 and next_i is not None:
                        take(next_i, 0)
                    dve.wait_ge(multiplied, tiles * i + k + 1)
                    dve.wait_ge(stored[k % 2], 8 * tiles * i + 16 * (k // 2 + 1))
                    rows = DEC if k % TT == TT - 1 else P
                    nc.vector.tensor_copy(stage[0:rows, k % 2, :],
                                          psum[0:rows, (k % BANKS) * BANK:(k % BANKS + 1) * BANK])\
                        .then_inc(staged, 1)
            with dve.Fori(0, 2) as i:
                evict(i, i + 1)
            evict(2, None)

        @block.tensor
        def _(pe):
            with pe.Fori(0, 3) as i:
                for k in range(tiles):
                    j, t = k // TT, k % TT
                    if t == 0:
                        pe.wait_ge(split, 2 * i + j + 1)
                    if k >= BANKS:
                        pe.wait_ge(staged, tiles * i + k + 1 - BANKS)
                    else:
                        pe.wait_ge(staged, tiles * i)
                    at = (k % BANKS) * BANK
                    cols = slice(t * P, (t + 1) * P)
                    for c in range(DC):
                        for n, (h, w) in enumerate(((h_hi, w_hi), (h_hi, w_lo), (h_lo, w_hi))):
                            last = nc.tensor.matmul(psum[:, at:at + BANK], h[:, c, cols], w[:, j, c, :],
                                                    start=(c == 0 and n == 0), stop=(c == DC - 1 and n == 2))
                    last.then_inc(multiplied, 1)


def features(nc, g, h_hi, h_lo, zf):
    with ExitStack() as es:
        sb = lambda n, s, dt=F32: es.enter_context(nc.sbuf_tensor(f"ft_{n}", s, dt))
        sem = semaphores(nc, es, "ft")
        raw = sb("raw", [P, 2, DC, P])
        w_hi, w_lo = sb("w_hi", [P, 2, DC, P], F32R), sb("w_lo", [P, 2, DC, P], F32R)
        stage, tmp = sb("stage", [P, 2, TOK]), sb("tmp", [P, 2, TOK])
        prods = sb("prods", [P, 4, TOK])
        cos, sin = sb("cos", [P, TOK]), sb("sin", [P, TOK])
        bias = sb("bias", [HF, 1])
        loaded, rounded, split = [sem(f"loaded{j}") for j in range(2)], sem("rounded"), sem("split")
        tables, multiplied = sem("tables"), sem("multiplied")
        copied, rotated, silued = sem("copied"), sem("rotated"), sem("silued")
        stored, rope_products = [sem(f"stored{j}") for j in range(2)], sem("rope_products")
        sigmoid = sem("sigmoid")
        psum = g.psum
        last_tile = NFEAT
        plain, rope = (0, NPLAIN // 2), (NPLAIN // 2, (NPLAIN + NROPE) // 2)
        silu = (rope[1], rope[1] + NSILU // 2)
        sigm = (silu[1], silu[1] + NSIG // 2)
        block = es.enter_context(nc.Block())

        def at(j):
            return 3 * j

        @block.sync
        def _(sp):
            sp.dma_start(raw[:, 0].rearrange("p c n -> p (c n)"), g.w_feat[0, :, :]).then_inc(loaded[0], 16)
            sp.dma_start(raw[:, 1].rearrange("p c n -> p (c n)"), g.w_feat[1, :, :]).then_inc(loaded[1], 16)
            sp.dma_start(bias[:], g.b_forget).then_inc(tables, 16)
            sp.dma_start(cos[:], g.cos_t).then_inc(tables, 16)
            sp.dma_start(sin[:], g.sin_t).then_inc(tables, 16)

            for j in range(2):
                sp.sem_inc(stored[j], 16)

            def next_load(t, j):
                sp.wait_ge(split, t - 1)
                sp.dma_start(raw[:, j].rearrange("p c n -> p (c n)"), g.w_feat[t, :, :]).then_inc(loaded[j], 16)

            def store(dst, first, staged, before, t, j):
                sp.wait_ge(staged, t + 1 - before)
                sp.dma_start(dst[t - first, :, :], stage[:, j, :]).then_inc(stored[j], 16)

            def bodies(start, end, dst, first, staged, before):
                with sp.Fori(start, end) as i:
                    for j in range(2):
                        next_load(2 * i + 2 + j, j)
                    for j in range(2):
                        store(dst, first, staged, before, 2 * i + j, j)
            bodies(*plain, g.qk_out, 0, copied, 0)
            bodies(*rope, g.qk_ret, NPLAIN, rotated, NPLAIN)
            bodies(*silu, g.gates, NPLAIN + NROPE, silued, NPLAIN + NROPE)
            bodies(sigm[0], sigm[1] - 1, g.gates, NPLAIN + NROPE, copied, NROPE + NSILU)
            next_load(last_tile, 0)
            for j in range(2):
                store(g.gates, NPLAIN + NROPE, copied, NROPE + NSILU, NFEAT - 2 + j, j)
            for j in range(2):
                sp.wait_ge(stored[j], 16 + 16 * NFEAT // 2)

        @block.gpsimd
        def _(pool):
            with pool.Fori(*rope) as i:
                for j in range(2):
                    pool.wait_ge(rope_products, 4 * i - 4 * rope[0] + 3 + j)
                    pool.wait_ge(stored[j], 16 * (i + 1))
                    nc.gpsimd.tensor_tensor(stage[:, j, :], prods[:, 2 * j, :], prods[:, 2 * j + 1, :],
                                            ALU.subtract if j == 0 else ALU.add).then_inc(rotated, 1)

        @block.scalar
        def _(act):
            def round_tile(t, j, nth):
                act.wait_ge(loaded[j], 16 * (nth + 1))
                nc.scalar.activation(w_hi[:, j], raw[:, j], ACT.Copy).then_inc(rounded, 1)

            def ahead(i, j):
                act.wait_ge(multiplied, 2 * i + j)
                round_tile(2 * i + j + 1, 1 - j, i + j)
            round_tile(0, 0, 0)
            with act.Fori(*plain) as i:
                for j in range(2):
                    ahead(i, j)
                    act.wait_ge(multiplied, 2 * i + j + 1)
                    act.wait_ge(stored[j], 16 * (i + 1))
                    views = slab_views(psum, at(j), stage[:, j, :])
                    nc.scalar.activation(views[0][1], views[0][0], ACT.Copy)
                    nc.scalar.activation(views[1][1], views[1][0], ACT.Copy).then_inc(copied, 1)
            with act.Fori(*rope) as i:
                for j in range(2):
                    ahead(i, j)
            with act.Fori(*silu) as i:
                for j in range(2):
                    ahead(i, j)
                    act.wait_ge(multiplied, 2 * i + j + 1)
                    act.wait_ge(silued, 2 * i + j - NPLAIN - NROPE)
                    views = slab_views(psum, at(j), tmp[:, j, :])
                    nc.scalar.activation(views[0][1], views[0][0], ACT.Sigmoid)
                    nc.scalar.activation(views[1][1], views[1][0], ACT.Sigmoid).then_inc(sigmoid, 1)
            with act.Fori(*sigm) as i:
                for j in range(2):
                    ahead(i, j)
                    act.wait_ge(multiplied, 2 * i + j + 1)
                    act.wait_ge(stored[j], 16 * (i + 1))
                    views = slab_views(psum, at(j), stage[:, j, :])
                    nc.scalar.activation(views[0][1], views[0][0], ACT.Sigmoid)
                    nc.scalar.activation(views[1][1], views[1][0], ACT.Sigmoid).then_inc(copied, 1)
            act.wait_ge(tables, 48)
            act.wait_ge(multiplied, last_tile + 1)
            for dst, src in ((zf[:, 0:768].rearrange("p (s n) -> p s n", n=384),
                              psum[0:HF, 0:2 * BANK].rearrange("p (s n) -> p s n", n=BANK)[:, :, 0:384]),
                             (zf[:, 768:TOK], psum[0:HF, 2 * BANK:2 * BANK + 320])):
                nc.scalar.activation(dst, src, ACT.Identity, bias=bias[:, 0:1])

        @block.vector
        def _(dve):
            def rest(t, j):
                dve.wait_ge(rounded, t + 1)
                nc.vector.tensor_tensor(w_lo[:, j], raw[:, j], w_hi[:, j].bitcast(F32),
                                        ALU.subtract).then_inc(split, 1)
            rest(0, 0)
            with dve.Fori(*plain) as i:
                for j in range(2):
                    rest(2 * i + j + 1, 1 - j)
            dve.wait_ge(tables, 48)
            with dve.Fori(*rope) as i:
                rest(2 * i + 1, 1)
                for half, (table, n0, n1) in enumerate(((0, 0, 2), (1, 1, 3))):
                    dve.wait_ge(multiplied, 2 * i + half + 1)
                    if half == 1:
                        rest(2 * i + 2, 0)
                    for dst, table in (((0, cos), (2, sin)) if half == 0 else ((1, sin), (3, cos))):
                        dve.wait_ge(rotated, 2 * i - NPLAIN)
                        pv = slab_views(psum, at(half), prods[:, dst, :])
                        tv = slab_views(psum, at(half), table[:, :])
                        nc.vector.tensor_tensor(pv[0][1], pv[0][0], tv[0][1], ALU.mult)
                        nc.vector.tensor_tensor(pv[1][1], pv[1][0], tv[1][1], ALU.mult).then_inc(rope_products, 1)
            with dve.Fori(*silu) as i:
                for j in range(2):
                    t = 2 * i + j
                    rest(t + 1, 1 - j)
                    dve.wait_ge(sigmoid, t + 1 - 2 * silu[0])
                    dve.wait_ge(stored[j], 16 * (i + 1))
                    views = slab_views(psum, at(j), stage[:, j, :])
                    tv = slab_views(psum, at(j), tmp[:, j, :])
                    nc.vector.tensor_tensor(views[0][1], views[0][0], tv[0][1], ALU.mult)
                    nc.vector.tensor_tensor(views[1][1], views[1][0], tv[1][1], ALU.mult).then_inc(silued, 1)
            with dve.Fori(*sigm) as i:
                for j in range(2):
                    rest(2 * i + j + 1, 1 - j)

        @block.tensor
        def _(pe):
            def tile(t, j):
                pe.wait_ge(split, t + 1)
                gemm_tile(nc, psum, at(j), w_hi[:, j], w_lo[:, j], h_hi, h_lo, DC).then_inc(multiplied, 1)
            tile(0, 0)
            tile(1, 1)

            def bodies(start, end, staged, before):
                with pe.Fori(start, end) as i:
                    for j in range(2):
                        pe.wait_ge(staged, 2 * i + j - 1 - before)
                        tile(2 * i + j, j)
            bodies(1, rope[0] + 1, copied, 0)
            with pe.Fori(rope[0] + 1, rope[1] + 1) as i:
                for j in range(2):
                    pe.wait_ge(rope_products, 4 * i - 4 * rope[0] - 2 + 2 * j)
                    tile(2 * i + j, j)
            bodies(silu[0] + 1, silu[1] + 1, silued, NPLAIN + NROPE)
            bodies(sigm[0] + 1, sigm[1], copied, NROPE + NSILU)
            pe.wait_ge(copied, last_tile - 1 - NROPE - NSILU)
            tile(last_tile, 0)


def decay(nc, g, zf):
    with ExitStack() as es:
        sb = lambda n, s, dt=F32: es.enter_context(nc.sbuf_tensor(f"dc_{n}", s, dt))
        sem = semaphores(nc, es, "dc")
        neg_abs, soft, low = sb("neg_abs", [HF, TOK]), sb("soft", [HF, TOK]), sb("low", [HF, TOK])
        logf, ones, c = sb("logf", [HF, KEYS]), sb("ones", [HF, KEYS]), sb("c", [HF, KEYS])
        c_hi = sb("c_hi", [HF, KEYS], F32R)
        q_rows, k_rows = sb("q_rows", [HF, 4, TOK]), sb("k_rows", [HF, 4, KEYS])
        cached, step, soft_ready = sem("cached"), sem("step"), sem("soft_ready")
        logf_ready, chain, stored = sem("logf_ready"), sem("chain"), sem("stored")
        block = es.enter_context(nc.Block())
        S0 = SEQ + PAST

        @block.sync
        def _(sp):
            sp.dma_start(logf[:, SEQ:S0], g.cache_logf).then_inc(cached, 16)
            sp.wait_ge(logf_ready, 3)
            sp.dma_start(g.logf_out[:, 0:SEQ], logf[:, 0:SEQ]).then_inc(stored, 16)
            sp.dma_start(g.logf_out[:, SEQ:TOK], logf[:, S0:S0 + DEC]).then_inc(stored, 16)
            sp.wait_ge(chain, 11)
            sp.dma_start(g.q_rows, q_rows[:]).then_inc(stored, 16)
            sp.dma_start(g.k_rows, k_rows[:]).then_inc(stored, 16)
            sp.wait_ge(stored, 64)

        @block.scalar
        def _(act):
            nc.scalar.activation(soft[:], zf[:], ACT.Abs).then_inc(step, 1)
            act.wait_ge(step, 1)
            nc.scalar.activation(neg_abs[:], soft[:], ACT.Exp, scale=-1.0).then_inc(step, 1)
            act.wait_ge(step, 2)
            nc.scalar.activation(soft[:], neg_abs[:], ACT.Ln, bias=1.0).then_inc(soft_ready, 1)

        @block.vector
        def _(dve):
            done = [0]

            def then(instruction):
                done[0] += 1
                instruction.then_inc(chain, 1)
                dve.wait_ge(chain, done[0])
            nc.vector.tensor_scalar(low[:], zf[:], 0.0, None, ALU.min).then_inc(logf_ready, 1)
            dve.wait_ge(logf_ready, 1)
            dve.wait_ge(soft_ready, 1)
            nc.vector.memset(logf[:, S0 + DEC:KEYS], 0.0)
            nc.vector.tensor_tensor(logf[:, 0:SEQ], low[:, 0:SEQ], soft[:, 0:SEQ],
                                    ALU.subtract).then_inc(logf_ready, 1)
            nc.vector.tensor_tensor(logf[:, S0:S0 + DEC], low[:, SEQ:TOK], soft[:, SEQ:TOK],
                                    ALU.subtract).then_inc(logf_ready, 1)
            then(nc.vector.memset(ones[:], 1.0))
            dve.wait_ge(logf_ready, 3)
            dve.wait_ge(cached, 16)
            then(nc.vector.tensor_tensor_scan(c[:, 0:SEQ], ones[:, 0:SEQ], logf[:, 0:SEQ], 0.0,
                                              ALU.mult, ALU.add))
            then(nc.vector.tensor_tensor_scan(c[:, SEQ:KEYS], ones[:, SEQ:KEYS], logf[:, SEQ:KEYS], 0.0,
                                              ALU.mult, ALU.add))
            then(nc.vector.tensor_copy(c_hi[:], c[:]))
            hi = c_hi[:].bitcast(F32)
            then(nc.vector.tensor_scalar(k_rows[:, 0, :], hi, -1.0, None, ALU.mult))
            then(nc.vector.tensor_tensor(k_rows[:, 1, :], hi, c[:], ALU.subtract))
            then(nc.vector.memset(k_rows[:, 2:4, :], 1.0))
            then(nc.vector.memset(q_rows[:, 0:2, :], 1.0))
            for q0, k0, n in ((0, 0, SEQ), (SEQ, S0, DEC)):
                nc.vector.tensor_copy(q_rows[:, 2, q0:q0 + n], hi[:, k0:k0 + n])
                then(nc.vector.tensor_tensor(q_rows[:, 3, q0:q0 + n], c[:, k0:k0 + n], hi[:, k0:k0 + n],
                                             ALU.subtract))
            then(nc.vector.memset(ones[:, 0:1], 1.0))


def retention(nc, g):
    NV = DV // P
    steps = [(b, j, max(BANK * b, P * j)) for b in range(2) for j in range(4 * b + 4)]
    steps = [(b, j, n0, BANK * (b + 1) - n0) for b, j, n0 in steps] + [(2, TT - 1, SEQ, DEC)]
    NS = len(steps)
    ends = [max(s for s in range(NS) if steps[s][0] == b) for b in range(3)]
    blocks = ((0, BANK), (BANK, BANK), (SEQ, DEC))
    v_order = [TT - 1] + list(range(TT - 1))
    pairs = [list(range(2 * p, min(2 * p + 2, TT))) for p in range((TT + 1) // 2)]
    NPR = len(pairs)
    VR = 3
    with ExitStack() as es:
        sb = lambda n, s, dt=F32: es.enter_context(nc.sbuf_tensor(f"rt_{n}", s, dt))
        sem = semaphores(nc, es, "rt")
        slots = lambda n, k: [sem(f"{n}{j}") for j in range(k)]
        q_raw, k_raw = sb("q_raw", [P, 2, TOKP]), sb("k_raw", [P, 2, TOKP])
        v_raw, s_raw = sb("v_raw", [P, VR, DV]), sb("s_raw", [P, 2, DV])
        q_hi, q_lo = sb("q_hi", [P, 2, TOKP], F32R), sb("q_lo", [P, 2, TOKP], F32R)
        k_hi, k_lo = sb("k_hi", [P, 2, TOKP], F32R), sb("k_lo", [P, 2, TOKP], F32R)
        v_hi, v_lo = sb("v_hi", [P, TT, DV], F32R), sb("v_lo", [P, TT, DV], F32R)
        s_hi, s_lo = sb("s_hi", [P, 2, DV], F32R), sb("s_lo", [P, 2, DV], F32R)
        kt, kt_hi, kt_lo = sb("kt", [P, 2, 2, DK]), sb("kt_hi", [P, TT, DK], F32R), sb("kt_lo", [P, TT, DK], F32R)
        qd, qd_hi, qd_lo = sb("qd", [P, 2, DEC]), sb("qd_hi", [P, 2, DEC], F32R), sb("qd_lo", [P, 2, DEC], F32R)
        w, w_hi, w_lo = sb("w", [P, 2, BANK]), sb("w_hi", [P, 2, BANK], F32R), sb("w_lo", [P, 2, BANK], F32R)
        table, cols, qdec = sb("table", [P, SEQ]), sb("cols", [P, TT + 1 + NV]), sb("qdec", [P, DEC])
        y, sq, new_state = sb("y", [P, NV, TOK]), sb("sq", [P, NV, BANK]), sb("new_state", [P, 2 * DV])
        sums = sb("sums", [P, TOK])
        gain, gate, out = sb("gain", [P, NV]), sb("gate", [P, 2, TOK]), sb("out", [P, 2, TOK])
        ident = sb("ident", [P, P])
        const_loaded, padded = sem("const_loaded"), sem("padded")
        q_loaded, k_loaded, v_loaded = sem("q_loaded"), sem("k_loaded"), slots("v_loaded", VR)
        table_loaded, aux_loaded, gate_loaded = sem("table_loaded"), sem("aux_loaded"), slots("gate_loaded", 2)
        k_rounded, q_rounded, v_rounded, s_rounded = (sem("k_rounded"), sem("q_rounded"), sem("v_rounded"),
                                                      sem("s_rounded"))
        k_split, q_split, v_split, s_split = sem("k_split"), sem("q_split"), sem("v_split"), sem("s_split")
        q_decayed, qd_rounded, qd_split = sem("q_decayed"), sem("qd_rounded"), sem("qd_split")
        transposed, kt_decayed, kt_rounded, kt_split = (sem("transposed"), sem("kt_decayed"), sem("kt_rounded"),
                                                        sem("kt_split"))
        scored, weighted, w_rounded, w_split = sem("scored"), sem("weighted"), sem("w_rounded"), sem("w_split")
        y_step, y_copied, squared, summed = sem("y_step"), sem("y_copied"), sem("squared"), sem("summed")
        state_tile, states_copied, states_summed = sem("state_tile"), sem("states_copied"), sem("states_summed")
        states_stored, total, logged, inverted = sem("states_stored"), sem("total"), sem("logged"), sem("inverted")
        gain_ready, gate_scaled, gated, o_stored = (sem("gain_ready"), sem("gate_scaled"), sem("gated"),
                                                    slots("o_stored", 2))
        psum = g.psum
        bank = lambda b, n=BANK: psum[:, b * BANK:b * BANK + n]
        block = es.enter_context(nc.Block())

        @block.sync
        def _(sp):
            def load_q(i):
                sp.dma_start(q_raw[:, :, 0:TOK], g.qk_ret[bass.ds(2 * i, 2), :, :].rearrange("c p t -> p c t"))\
                    .then_inc(q_loaded, 16)

            def load_k(i):
                sp.dma_start(k_raw[:, :, 0:TOK], g.qk_ret[bass.ds(2 * i + DC, 2), :, :].rearrange("c p t -> p c t"))\
                    .then_inc(k_loaded, 16)

            def load_v(i, m):
                t = v_order[m]
                rows = DEC if t == TT - 1 else P
                row = 0 if t == TT - 1 else DEC + t * P
                sp.dma_start(v_raw[0:rows, m % VR, :], g.v_ret[i, row:row + rows, :]).then_inc(v_loaded[m % VR], 16)

            def load_table(i):
                sp.dma_start(table[:], g.ret_decay[i, :, :]).then_inc(table_loaded, 16)

            def load_aux(i):
                sp.dma_start(cols[:], g.ret_cols[i, :, :]).then_inc(aux_loaded, 16)
                sp.dma_start(qdec[:], g.ret_qdec[i, :, :]).then_inc(aux_loaded, 16)
                sp.dma_start(s_raw[:], g.state_in[i, :, :].rearrange("(c p) n -> p c n", p=P)).then_inc(aux_loaded, 16)

            def load_gate(i, c):
                sp.dma_start(gate[:, c % 2, :], g.gates[NV * i + c, :, :]).then_inc(gate_loaded[c % 2], 16)

            def store_state(i, which):
                sp.dma_start(g.state_out[which, i, :, :].rearrange("(c p) n -> p c n", p=P),
                             new_state[:].rearrange("p (c n) -> p c n", n=DV)).then_inc(states_stored, 16)

            def store_out(i, c):
                sp.wait_ge(gated, NV * i + c + 1)
                sp.dma_start(g.o_ret[NV * i + c, :, :], out[:, c % 2, :]).then_inc(o_stored[c % 2], 16)

            def head(i, next_i, first=False):
                if not first:
                    for c in range(2, NV):
                        store_out(i - 1, c)
                        load_gate(i, c - 2)
                if next_i is not None:
                    for m in range(VR):
                        sp.wait_ge(v_split, TT * i + TT - VR + m + 1)
                        load_v(next_i, m)
                    sp.wait_ge(q_decayed, i + 1)
                    load_q(next_i)
                    sp.wait_ge(transposed, NPR * i + NPR)
                    load_k(next_i)
                    sp.wait_ge(weighted, NS * i + NS)
                    load_table(next_i)
                sp.wait_ge(states_summed, i + 1)
                store_state(i, 0)
                if next_i is not None:
                    sp.wait_ge(gain_ready, i + 1)
                    load_aux(next_i)
                    for m in range(VR, TT):
                        sp.wait_ge(v_split, TT * i + TT + m - VR + 1)
                        load_v(next_i, m)
                for c in range(2):
                    store_out(i, c)
                    load_gate(i, c + 2)
                sp.wait_ge(states_copied, i + 1)
                store_state(i, 1)

            sp.dma_start(ident[:], g.ident_t).then_inc(const_loaded, 16)
            for n in range(2):
                sp.sem_inc(o_stored[n], 16)
            load_k(0)
            load_q(0)
            for m in range(VR):
                load_v(0, m)
            load_table(0)
            load_aux(0)
            load_gate(0, 0)
            load_gate(0, 1)
            for m in range(VR, TT):
                sp.wait_ge(v_split, m - VR + 1)
                load_v(0, m)
            head(0, 1, first=True)
            with sp.Fori(1, HR - 1) as i:
                head(i, i + 1)
            head(HR - 1, None)
            for c in range(2, NV):
                store_out(HR - 1, c)
            for n in range(2):
                sp.wait_ge(o_stored[n], 16 + 16 * HR * NV // 2)
            sp.wait_ge(states_stored, 32 * HR)

        @block.gpsimd
        def _(pool):
            def rest_k(i):
                pool.wait_ge(k_rounded, i + 1)
                nc.gpsimd.tensor_tensor(k_lo[:], k_raw[:], k_hi[:].bitcast(F32), ALU.subtract).then_inc(k_split, 1)

            def head(i, next_i):
                if next_i is not None:
                    rest_k(next_i)
                for c in range(NV):
                    pool.wait_ge(gate_loaded[c % 2], 32 * i + 16 * (c // 2 + 1))
                    if c == 0:
                        pool.wait_ge(inverted, i + 1)
                    nc.gpsimd.tensor_tensor(gate[:, c % 2, :], gate[:, c % 2, :], sums[:], ALU.mult)\
                        .then_inc(gate_scaled, 1)
            rest_k(0)
            with pool.Fori(0, HR - 1) as i:
                head(i, i + 1)
            head(HR - 1, None)

        @block.scalar
        def _(act):
            def round_k(i):
                act.wait_ge(k_loaded, 16 * (i + 1))
                nc.scalar.activation(k_hi[:], k_raw[:], ACT.Copy).then_inc(k_rounded, 1)

            def round_q(i):
                act.wait_ge(q_loaded, 16 * (i + 1))
                nc.scalar.activation(q_hi[:], q_raw[:], ACT.Copy).then_inc(q_rounded, 1)

            def round_v(i, m):
                t = v_order[m]
                rows = DEC if t == TT - 1 else P
                act.wait_ge(v_loaded[m % VR], 48 * i + 16 * (m // VR + 1))
                nc.scalar.activation(v_hi[0:rows, t, :], v_raw[0:rows, m % VR, :], ACT.Copy).then_inc(v_rounded, 1)

            def copy_y(i, b):
                n0, n = blocks[b]
                act.wait_ge(y_step, NS * i + ends[b] + 1)
                src = psum[:, 0:NV * BANK] if b < 2 else bank(6, NV * DEC)
                nc.scalar.activation(y[:, :, n0:n0 + n], src.rearrange("p (c n) -> p c n", c=NV),
                                     ACT.Copy).then_inc(y_copied, 1)

            def square(i, b, first):
                n0, n = blocks[b]
                act.wait_ge(y_copied, 3 * i + b + 1)
                if b > 0 or not first:
                    act.wait_ge(summed, 3 * i + b)
                nc.scalar.activation(sq[:, :, 0:n], y[:, :, n0:n0 + n], ACT.Square).then_inc(squared, 1)

            def head(i, next_i, first=False):
                for s, (b, j, n0, n) in enumerate(steps):
                    act.wait_ge(weighted, NS * i + s + 1)
                    if s >= 2:
                        act.wait_ge(y_step, NS * i + s - 1)
                    elif not first:
                        act.wait_ge(y_step, NS * i)
                    nc.scalar.activation(w_hi[:, s % 2, 0:n], w[:, s % 2, 0:n], ACT.Copy).then_inc(w_rounded, 1)
                    if s % 2 == 1 and s // 2 < NPR:
                        p, tiles = s // 2, pairs[s // 2]
                        act.wait_ge(kt_decayed, TT * i + tiles[-1] + 1)
                        nc.scalar.activation(kt_hi[:, tiles[0]:tiles[-1] + 1, :], kt[:, p % 2, 0:len(tiles), :],
                                             ACT.Copy).then_inc(kt_rounded, 1)
                    if s == ends[0] + 1:
                        if not first:
                            act.wait_ge(gated, NV * i)
                        copy_y(i, 0)
                    if s == ends[0] + 2:
                        square(i, 0, first)
                    if s == 6:
                        act.wait_ge(aux_loaded, 48 * (i + 1))
                        nc.scalar.activation(s_hi[:], s_raw[:], ACT.Copy).then_inc(s_rounded, 1)
                    if s == 8:
                        act.wait_ge(q_decayed, i + 1)
                        nc.scalar.activation(qd_hi[:], qd[:], ACT.Copy).then_inc(qd_rounded, 1)
                    if s == 11:
                        act.wait_ge(scored, NS * i + NS)
                        if next_i is not None:
                            round_k(next_i)
                copy_y(i, 1)
                copy_y(i, 2)
                square(i, 1, first)
                if next_i is not None:
                    round_q(next_i)
                square(i, 2, first)
                for m in range(TT):
                    if next_i is not None:
                        act.wait_ge(state_tile, TT * i + m + 1)
                        round_v(next_i, m)
                    if m == 6:
                        act.wait_ge(total, i + 1)
                        for src, dst in slab_views(psum, 0, sums):
                            last = nc.scalar.activation(dst, src, ACT.Ln, bias=g.eps[:, 0:1], scale=1.0 / DV)
                        last.then_inc(logged, 1)
                        act.wait_ge(logged, i + 1)
                        nc.scalar.activation(sums[:], sums[:], ACT.Exp, scale=-0.5).then_inc(inverted, 1)
                act.wait_ge(state_tile, TT * i + TT)
                act.wait_ge(states_stored, 32 * i + 16)
                nc.scalar.activation(new_state[:], psum[:, 6 * BANK:8 * BANK], ACT.Copy).then_inc(states_copied, 1)

            act.wait_ge(padded, 4)
            round_k(0)
            round_q(0)
            for m in range(TT):
                round_v(0, m)
            head(0, 1, first=True)
            with act.Fori(1, HR - 1) as i:
                head(i, i + 1)
            head(HR - 1, None)

        @block.vector
        def _(dve):
            nc.vector.memset(q_raw[:, :, TOK:TOKP], 0.0).then_inc(padded, 1)
            nc.vector.memset(k_raw[:, :, TOK:TOKP], 0.0).then_inc(padded, 1)
            nc.vector.memset(v_hi[DEC:P, TT - 1, :].bitcast(F32), 0.0).then_inc(padded, 1)
            nc.vector.memset(v_lo[DEC:P, TT - 1, :].bitcast(F32), 0.0).then_inc(padded, 1)

            def rest_q(i):
                dve.wait_ge(q_rounded, i + 1)
                nc.vector.tensor_tensor(q_lo[:], q_raw[:], q_hi[:].bitcast(F32), ALU.subtract).then_inc(q_split, 1)

            def rest_v(i, m):
                t = v_order[m]
                rows = DEC if t == TT - 1 else P
                dve.wait_ge(v_rounded, TT * i + m + 1)
                nc.vector.tensor_tensor(v_lo[0:rows, t, :], v_raw[0:rows, m % VR, :],
                                        v_hi[0:rows, t, :].bitcast(F32), ALU.subtract).then_inc(v_split, 1)

            def rest_kt(i, p):
                tiles = pairs[p]
                dve.wait_ge(kt_rounded, NPR * i + p + 1)
                nc.vector.tensor_tensor(kt_lo[:, tiles[0]:tiles[-1] + 1, :], kt[:, p % 2, 0:len(tiles), :],
                                        kt_hi[:, tiles[0]:tiles[-1] + 1, :].bitcast(F32), ALU.subtract)\
                    .then_inc(kt_split, 1)

            def sum_squares(i, b):
                n0, n = blocks[b]
                dve.wait_ge(squared, 3 * i + b + 1)
                nc.vector.reduce_sum(sums[:, n0:n0 + n], sq[:, :, 0:n].rearrange("p c n -> p n c"), AX)\
                    .then_inc(summed, 1)

            def apply_gate(i, c):
                dve.wait_ge(gate_scaled, NV * i + c + 1)
                dve.wait_ge(o_stored[c % 2], 32 * i + 16 * (c // 2 + 1))
                nc.vector.scalar_tensor_tensor(out[:, c % 2, :], y[:, c, :], gain[:, c:c + 1], gate[:, c % 2, :],
                                               ALU.mult, ALU.mult).then_inc(gated, 1)

            def head(i, next_i, first=False):
                dve.wait_ge(table_loaded, 16 * (i + 1))
                dve.wait_ge(aux_loaded, 48 * (i + 1))
                for s, (b, j, n0, n) in enumerate(steps):
                    dve.wait_ge(scored, NS * i + s + 1)
                    if s >= 2 or not first:
                        dve.wait_ge(w_split, NS * i + s - 1)
                    off = n0 - j * P
                    nc.vector.tensor_tensor(w[:, s % 2, 0:n], bank(4 + s % 2, n), table[:, off:off + n], ALU.mult)\
                        .then_inc(weighted, 1)
                    dve.wait_ge(w_rounded, NS * i + s + 1)
                    nc.vector.tensor_tensor(w_lo[:, s % 2, 0:n], w[:, s % 2, 0:n], w_hi[:, s % 2, 0:n].bitcast(F32),
                                            ALU.subtract).then_inc(w_split, 1)
                    if s % 2 == 1 and s // 2 < NPR:
                        p = s // 2
                        dve.wait_ge(transposed, NPR * i + p + 1)
                        if p >= 2 or not first:
                            dve.wait_ge(kt_split, NPR * i + p - 1)
                        for m, t in enumerate(pairs[p]):
                            at = (6 + p % 2) * BANK + m * DK
                            nc.vector.tensor_scalar(kt[:, p % 2, m, :], psum[:, at:at + DK], cols[:, t:t + 1], None,
                                                    ALU.mult).then_inc(kt_decayed, 1)
                    if s % 2 == 0 and 0 < s // 2 <= NPR:
                        rest_kt(i, s // 2 - 1)
                    if s in (2, 3) and not first:
                        apply_gate(i - 1, s)
                    if s == 5:
                        for c in range(2):
                            last = nc.vector.tensor_tensor(qd[:, c, :], q_raw[:, c, SEQ:TOK], qdec[:], ALU.mult)
                        last.then_inc(q_decayed, 1)
                    if s == 7:
                        dve.wait_ge(s_rounded, i + 1)
                        nc.vector.tensor_tensor(s_lo[:], s_raw[:], s_hi[:].bitcast(F32), ALU.subtract)\
                            .then_inc(s_split, 1)
                    if s == 8:
                        sum_squares(i, 0)
                    if s == 9:
                        dve.wait_ge(qd_rounded, i + 1)
                        nc.vector.tensor_tensor(qd_lo[:], qd[:], qd_hi[:].bitcast(F32), ALU.subtract)\
                            .then_inc(qd_split, 1)
                dve.wait_ge(state_tile, TT * i + 1)
                if not first:
                    dve.wait_ge(states_stored, 32 * i)
                nc.vector.scalar_tensor_tensor(new_state[:], s_raw[:].rearrange("p c n -> p (c n)"),
                                               cols[:, TT:TT + 1], psum[:, 4 * BANK:6 * BANK], ALU.mult, ALU.add)\
                    .then_inc(states_summed, 1)
                if not first:
                    dve.wait_ge(gated, NV * i)
                nc.vector.tensor_copy(gain[:], cols[:, TT + 1:TT + 1 + NV]).then_inc(gain_ready, 1)
                sum_squares(i, 1)
                if next_i is not None:
                    rest_q(next_i)
                sum_squares(i, 2)
                if next_i is not None:
                    for m in range(TT):
                        rest_v(next_i, m)
                dve.wait_ge(gain_ready, i + 1)
                for c in range(2):
                    apply_gate(i, c)

            dve.wait_ge(padded, 4)
            rest_q(0)
            for m in range(TT):
                rest_v(0, m)
            head(0, 1, first=True)
            with dve.Fori(1, HR - 1) as i:
                head(i, i + 1)
            head(HR - 1, None)
            for c in range(2, NV):
                apply_gate(HR - 1, c)

        @block.tensor
        def _(pe):
            three = lambda a_hi, a_lo, b_hi, b_lo: ((a_hi, b_hi), (a_hi, b_lo), (a_lo, b_hi))

            def scores(i, s):
                b, j, n0, n = steps[s]
                for c in range(2):
                    for m, (k, q) in enumerate(three(k_hi, k_lo, q_hi, q_lo)):
                        last = nc.tensor.matmul(bank(4 + s % 2, n), k[:, c, j * P:(j + 1) * P], q[:, c, n0:n0 + n],
                                                start=(c == 0 and m == 0), stop=(c == 1 and m == 2))
                last.then_inc(scored, 1)

            def head(i, first=False):
                pe.wait_ge(k_split, i + 1)
                pe.wait_ge(q_split, i + 1)
                if not first:
                    pe.wait_ge(states_summed, i)
                scores(i, 0)
                scores(i, 1)
                for s, (b, j, n0, n) in enumerate(steps):
                    if s + 2 < NS:
                        pe.wait_ge(weighted, NS * i + s + 1)
                        scores(i, s + 2)
                    if s % 2 == 1 and s // 2 < NPR:
                        p = s // 2
                        if p >= 2:
                            pe.wait_ge(kt_decayed, TT * i + 2 * p - 2)
                        elif not first:
                            pe.wait_ge(states_copied, i)
                        for m, t in enumerate(pairs[p]):
                            for c in range(2):
                                at = (6 + p % 2) * BANK + m * DK + c * P
                                last = nc.tensor.transpose(psum[:, at:at + P], k_raw[:, c, t * P:(t + 1) * P], ident[:])
                        last.then_inc(transposed, 1)
                    pe.wait_ge(w_split, NS * i + s + 1)
                    pe.wait_ge(v_split, TT * i + v_order.index(j) + 1)
                    new = s == 0 or s - 1 in ends
                    if new and b == 1:
                        pe.wait_ge(y_copied, 3 * i + 1)
                    elif new and b == 2:
                        pe.wait_ge(kt_decayed, TT * i + TT)
                    elif new and not first:
                        pe.wait_ge(logged, i)
                    if b == 2:
                        pe.wait_ge(s_split, i + 1)
                        pe.wait_ge(qd_split, i + 1)
                    for c in range(NV):
                        at = c * BANK + n0 - b * BANK if b < 2 else 6 * BANK + c * n
                        dst = psum[:, at:at + n]
                        vc = slice(c * P, (c + 1) * P)
                        if b == 2:
                            for kc in range(2):
                                for m, (st, q) in enumerate(three(s_hi, s_lo, qd_hi, qd_lo)):
                                    nc.tensor.matmul(dst, st[:, kc, vc], q[:, kc, :],
                                                     start=(kc == 0 and m == 0), stop=False)
                        for m, (v, x) in enumerate(three(v_hi, v_lo, w_hi, w_lo)):
                            last = nc.tensor.matmul(dst, v[:, j, vc], x[:, s % 2, 0:n],
                                                    start=(new and b < 2 and m == 0), stop=(s in ends and m == 2))
                    last.then_inc(y_step, 1)
                pe.wait_ge(kt_split, NPR * i + NPR)
                for n, t in enumerate(v_order):
                    sample = t == TT - 1
                    if n == 1:
                        pe.wait_ge(y_copied, 3 * i + 3)
                    for c in range(2):
                        for m, (k, v) in enumerate(three(kt_hi, kt_lo, v_hi, v_lo)):
                            last = nc.tensor.matmul(bank((4 if sample else 6) + c), k[:, t, c * P:(c + 1) * P],
                                                    v[:, t, :], start=(m == 0 and (sample or t == 0)),
                                                    stop=(m == 2 and t >= TT - 2))
                    last.then_inc(state_tile, 1)
                    if n == 6:
                        pe.wait_ge(summed, 3 * i + 3)
                        for sl, (t0, width) in enumerate(SLABS):
                            last = nc.tensor.matmul(bank(sl, width), g.ones[:, :],
                                                    sums[:, t0:t0 + width], start=True, stop=True)
                        last.then_inc(total, 1)
            pe.wait_ge(const_loaded, 16)
            head(0, first=True)
            with pe.Fori(1, HR) as i:
                head(i)


def fox(nc, g):
    UH = TT
    U = 2 * UH
    order = [u for n in range(4) for u in (n, 7 - n)] + [UH - 1]
    units = [(j, u, (0 if u < UH - 1 else UH - 1), (u + 1 if u < UH - 1 else KT - UH + 1))
             for j in range(2) for u in order]
    groups = [(n, t0, min(4, kt - t0)) for n, (_, _, _, kt) in enumerate(units) for t0 in range(0, kt, 4)]
    NG = len(groups)
    last_group = [max(x for x, q in enumerate(groups) if q[0] == n) for n in range(U)]
    outs = [(9 * j + a, 9 * j + b) for j in range(2) for a, b in ((0, 4), (4, 8), (8, 9))]
    NO = len(outs)
    out_of = [next(x for x, (a, b) in enumerate(outs) if a <= n < b) for n in range(U)]
    tails = [(3, 0, 3), (3, 3, 2), (4, 5, 2), (4, 7, 2)]
    NTL = len(tails)
    tail_bank = [(min(x for x, q in enumerate(groups) if q[0] == n) + y) % 2 for y, (n, _, _) in enumerate(tails)]
    after_tail = {min(x for x, q in enumerate(groups) if q[0] == n) + y % 2: y for y, (n, _, _) in enumerate(tails)}
    with ExitStack() as es:
        sb = lambda n, s, dt=F32: es.enter_context(nc.sbuf_tensor(f"fx_{n}", s, dt))
        sem = semaphores(nc, es, "fx")
        two = lambda n: [sem(f"{n}{j}") for j in range(2)]
        k_raw, q_raw, v_raw = sb("k_raw", [P, 2, KEYS]), sb("q_raw", [P, 2, TOKP]), sb("v_raw", [P, 2, KT, DF])
        q_a, q_b = sb("q_a", [P, 2, TOKP], F32R), sb("q_b", [DF + 4, 2, TOKP], F32R)
        k_a, k_b = sb("k_a", [P, 2, KEYS], F32R), sb("k_b", [DF + 4, 2, KEYS], F32R)
        v_a = sb("v_a", [P, 2, KT, 2 * DF], F32R)
        e = sb("e", [P, 2, SEQ])
        p_hi, p_lo = sb("p_hi", [P, 2, 8 * P], F32R), sb("p_lo", [P, 2, 8 * P], F32R)
        neg_max, rowsum, inv = sb("neg_max", [P, U]), sb("rowsum", [P, U]), sb("inv", [P, U])
        o_low, o_tok, o_t = sb("o_low", [P, 2, 4, DF]), sb("o_tok", [P, TT, P]), sb("o_t", [P, TOK])
        ident, masks = sb("ident", [P, P]), sb("masks", [P, 2, P])
        ident_r, masks_r = sb("ident_r", [P, P], F32R), sb("masks_r", [P, 2, P], F32R)
        raw_loaded, rows_loaded = two("raw_loaded"), two("rows_loaded")
        const_loaded, const_ready, padded = sem("const_loaded"), sem("const_ready"), sem("padded")
        rounded, split = sem("rounded"), sem("split")
        scored, maxed, exped = sem("scored"), sem("maxed"), sem("exped")
        transposed, p_rounded, p_split = sem("transposed"), sem("p_rounded"), sem("p_split")
        pv, o_lowered, o_summed, o_done = sem("pv"), sem("o_lowered"), sem("o_summed"), sem("o_done")
        inverted, tail_transposed, tail_copied, o_stored = (sem("inverted"), sem("tail_transposed"),
                                                            sem("tail_copied"), sem("o_stored"))
        psum = g.psum
        block = es.enter_context(nc.Block())
        PAIRS = HF // 2

        @block.sync
        def _(sp):
            def load_raw(i, j):
                rows = slice(j * DF, (j + 1) * DF)
                for half in (slice(0, DF), slice(DF, P)):
                    sp.dma_start(k_raw[half, j, 0:SEQ], g.qk_out[i + DC, rows, 0:SEQ]).then_inc(raw_loaded[j], 16)
                    sp.dma_start(k_raw[half, j, SEQ:SEQ + PAST], g.cache_kt[2 * i + j, :, :]).then_inc(raw_loaded[j], 16)
                    sp.dma_start(k_raw[half, j, SEQ + PAST:SEQ + PAST + DEC], g.qk_out[i + DC, rows, SEQ:TOK])\
                        .then_inc(raw_loaded[j], 16)
                    sp.dma_start(q_raw[half, j, 0:TOK], g.qk_out[i, rows, :]).then_inc(raw_loaded[j], 16)
                cols = bass.ds(i * P + j * DF, DF)
                sp.dma_start(v_raw[:, j, 0:8, :], g.v_out[0:SEQ, cols].rearrange("(t p) n -> p t n", p=P))\
                    .then_inc(raw_loaded[j], 16)
                sp.dma_start(v_raw[:, j, 8:10, :], g.cache_v[:, cols].rearrange("(t p) n -> p t n", p=P))\
                    .then_inc(raw_loaded[j], 16)
                sp.dma_start(v_raw[0:DEC, j, 10, :], g.v_out[SEQ:TOK, cols]).then_inc(raw_loaded[j], 16)

            def load_rows(i, j):
                sp.dma_start(q_b[DF:DF + 4, j, 0:TOK].bitcast(F32), g.q_rows[2 * i + j, :, :])\
                    .then_inc(rows_loaded[j], 16)
                sp.dma_start(k_b[DF:DF + 4, j, :].bitcast(F32), g.k_rows[2 * i + j, :, :]).then_inc(rows_loaded[j], 16)

            def store(i):
                sp.wait_ge(tail_copied, NTL * i + NTL)
                sp.dma_start(g.o_fox[i, :, :], o_t[:]).then_inc(o_stored, 16)

            def pair(i, next_i, first=False):
                if not first:
                    sp.wait_ge(scored, U * i)
                load_rows(i, 1)
                if next_i is not None:
                    sp.wait_ge(split, 6 * i + 3)
                    load_raw(next_i, 0)
                if not first:
                    store(i - 1)
                if next_i is not None:
                    sp.wait_ge(split, 6 * i + 6)
                    load_raw(next_i, 1)
                    sp.wait_ge(scored, U * i + UH)
                    load_rows(next_i, 0)
            sp.dma_start(ident[:], g.ident_t).then_inc(const_loaded, 16)
            sp.dma_start(masks[:], g.masks).then_inc(const_loaded, 16)
            sp.wait_ge(padded, 4)
            load_raw(0, 0)
            load_rows(0, 0)
            load_raw(0, 1)
            sp.sem_inc(o_stored, 16)
            pair(0, 1, first=True)
            with sp.Fori(1, PAIRS - 1) as i:
                pair(i, i + 1)
            pair(PAIRS - 1, None)
            store(PAIRS - 1)
            sp.wait_ge(o_stored, 16 * PAIRS + 16)

        @block.scalar
        def _(act):
            act.wait_ge(const_loaded, 32)
            nc.scalar.activation(ident_r[:], ident[:], ACT.Copy).then_inc(const_ready, 1)
            nc.scalar.activation(masks_r[:], masks[:], ACT.Copy).then_inc(const_ready, 1)
            act.wait_ge(padded, 4)

            def round_part(i, j, part):
                if part == 0:
                    act.wait_ge(raw_loaded[j], 11 * 16 * (i + 1))
                    nc.scalar.activation(k_a[:, j, :], k_raw[:, j, :], ACT.Copy).then_inc(rounded, 1)
                elif part == 1:
                    nc.scalar.activation(q_a[:, j, :], q_raw[:, j, :], ACT.Copy, scale=DF ** -0.5).then_inc(rounded, 1)
                elif part == 2:
                    nc.scalar.activation(q_b[0:DF, j, :], q_raw[0:DF, j, :], ACT.Copy,
                                         scale=DF ** -0.5).then_inc(rounded, 1)
                else:
                    nc.scalar.activation(v_a[:, j, :, 0:DF], v_raw[:, j, :, :], ACT.Copy).then_inc(rounded, 1)

            def exp(i, n, first):
                j, u, k0, kt = units[n]
                act.wait_ge(maxed, U * i + n + 1)
                if n >= 2:
                    act.wait_ge(transposed, NG * i + last_group[n - 2] + 1)
                elif not first:
                    act.wait_ge(transposed, NG * i - NG + last_group[n - 2 + U] + 1)
                s0 = (n % 2) * 2 * BANK
                nc.scalar.activation(e[:, n % 2, 0:kt * P], psum[:, s0:s0 + kt * P], ACT.Exp,
                                     bias=neg_max[:, n:n + 1], accum_out=rowsum[:, n:n + 1]).then_inc(exped, 1)

            def lower(i, x, first=False):
                a, b = outs[x]
                act.wait_ge(pv, U * i + b)
                if x >= 2 or not first:
                    act.wait_ge(o_summed, NO * i + x - 1)
                at = (6 + x % 2) * BANK
                nc.scalar.activation(o_low[:, x % 2, 0:b - a, :],
                                     psum[:, at:at + (b - a) * P].rearrange("p (t n) -> p t n", n=P)[:, :, DF:P],
                                     ACT.Copy).then_inc(o_lowered, 1)

            def tail(i, y):
                _, t0, nt = tails[y]
                act.wait_ge(tail_transposed, NTL * i + y + 1)
                if y == 0:
                    act.wait_ge(o_stored, 16 * i + 16)
                for t in range(t0, t0 + nt):
                    at, u = (4 + tail_bank[y]) * BANK + (t - t0) * P, order[t]
                    width = P if u < UH - 1 else DEC
                    last = nc.scalar.activation(o_t[:, u * P:u * P + width], psum[:, at:at + width], ACT.Copy)
                last.then_inc(tail_copied, 1)

            def pair(i, next_i, first=False):
                for n in range(U):
                    if n + 1 < U:
                        exp(i, n + 1, first)
                    elif next_i is not None:
                        exp(next_i, 0, False)
                    for x, (a, b) in enumerate(outs):
                        if b + 1 == n:
                            lower(i, x, first)
                        elif b + 1 == n + U and not first:
                            lower(i - 1, x)
                    for y, (m, _, _) in enumerate(tails):
                        if m == n and not first:
                            tail(i - 1, y)
                    for x, (m, t0, nt) in enumerate(groups):
                        if m == n:
                            act.wait_ge(transposed, NG * i + x + 1)
                            if n >= 2 or not first:
                                act.wait_ge(pv, U * i + n - 1)
                            at = (4 + x % 2) * BANK
                            nc.scalar.activation(p_hi[:, n % 2, t0 * P:(t0 + nt) * P], psum[:, at:at + nt * P],
                                                 ACT.Copy).then_inc(p_rounded, 1)
                    if 1 <= n <= 4:
                        if n == 1 and not first:
                            act.wait_ge(pv, U * i)
                        round_part(i, 1, n - 1)
                    if UH + 1 <= n <= UH + 4 and next_i is not None:
                        if n == UH + 1:
                            act.wait_ge(pv, U * i + UH)
                        round_part(next_i, 0, n - UH - 1)
            for part in range(4):
                round_part(0, 0, part)
            exp(0, 0, True)
            pair(0, 1, first=True)
            with act.Fori(1, PAIRS - 1) as i:
                pair(i, i + 1)
            pair(PAIRS - 1, None)
            lower(PAIRS - 1, NO - 2)
            lower(PAIRS - 1, NO - 1)
            for y in range(NTL):
                tail(PAIRS - 1, y)

        @block.vector
        def _(dve):
            nc.vector.memset(k_raw[:, :, SEQ + PAST + DEC:KEYS], 0.0).then_inc(padded, 1)
            nc.vector.memset(q_raw[:, :, TOK:TOKP], 0.0).then_inc(padded, 1)
            nc.vector.memset(v_raw[DEC:P, :, 10, :], 0.0).then_inc(padded, 1)
            nc.vector.memset(q_b[DF:DF + 4, :, TOK:TOKP].bitcast(F32), 0.0).then_inc(padded, 1)
            dve.wait_ge(padded, 4)

            def split_part(i, j, part):
                n = 8 * i + 4 * j
                if part == 0:
                    dve.wait_ge(rounded, n + 1)
                    nc.vector.tensor_tensor(k_b[0:DF, j, :], k_raw[0:DF, j, :], k_a[0:DF, j, :].bitcast(F32),
                                            ALU.subtract).then_inc(split, 1)
                elif part == 1:
                    dve.wait_ge(rounded, n + 2)
                    nc.vector.scalar_tensor_tensor(q_a[DF:P, j, :], q_raw[DF:P, j, :], DF ** -0.5,
                                                   q_a[DF:P, j, :].bitcast(F32), ALU.mult,
                                                   ALU.subtract).then_inc(split, 1)
                else:
                    dve.wait_ge(rounded, n + 4)
                    nc.vector.tensor_tensor(v_a[:, j, :, DF:P], v_raw[:, j, :, :], v_a[:, j, :, 0:DF].bitcast(F32),
                                            ALU.subtract).then_inc(split, 1)

            def row_max(i, n):
                j, u, k0, kt = units[n]
                dve.wait_ge(scored, U * i + n + 1)
                s0 = (n % 2) * 2 * BANK
                nc.vector.reduce_max(neg_max[:, n:n + 1], psum[:, s0:s0 + kt * P], AX, negate=True).then_inc(maxed, 1)

            def finish(i, x, first=False):
                a, b = outs[x]
                at = (6 + x % 2) * BANK
                o = o_tok[:, a % UH:a % UH + b - a, (a // UH) * DF:(a // UH + 1) * DF]
                nc.vector.reciprocal(inv[:, a:b], rowsum[:, a:b]).then_inc(inverted, 1)
                dve.wait_ge(o_lowered, NO * i + x + 1)
                if x == 0 and not first:
                    dve.wait_ge(tail_transposed, NTL * i)
                nc.vector.tensor_tensor(o, psum[:, at:at + (b - a) * P].rearrange("p (t n) -> p t n", n=P)[:, :, 0:DF],
                                        o_low[:, x % 2, 0:b - a, :], ALU.add).then_inc(o_summed, 1)
                dve.wait_ge(o_summed, NO * i + x + 1)
                dve.wait_ge(inverted, NO * i + x + 1)
                nc.vector.tensor_tensor(o, o, inv[:, a:b].unsqueeze(2).to_broadcast([P, b - a, DF]),
                                        ALU.mult).then_inc(o_done, 1)

            def pair(i, next_i, first=False):
                for n in range(U):
                    if n + 2 < U:
                        row_max(i, n + 2)
                    elif next_i is not None:
                        row_max(next_i, n + 2 - U)
                    for x, (a, b) in enumerate(outs):
                        if b + 1 == n:
                            finish(i, x, first)
                        elif b + 1 == n + U and not first:
                            finish(i - 1, x)
                    for x, (m, t0, nt) in enumerate(groups):
                        if m == n:
                            dve.wait_ge(p_rounded, NG * i + x + 1)
                            at = (4 + x % 2) * BANK
                            nc.vector.tensor_tensor(p_lo[:, n % 2, t0 * P:(t0 + nt) * P], psum[:, at:at + nt * P],
                                                    p_hi[:, n % 2, t0 * P:(t0 + nt) * P].bitcast(F32),
                                                    ALU.subtract).then_inc(p_split, 1)
                    if n in (2, 3, 5):
                        split_part(i, 1, (2, 3, 5).index(n))
                    if n - UH in (2, 3, 5) and next_i is not None:
                        split_part(next_i, 0, (2, 3, 5).index(n - UH))
            for part in range(3):
                split_part(0, 0, part)
            row_max(0, 0)
            row_max(0, 1)
            pair(0, 1, first=True)
            with dve.Fori(1, PAIRS - 1) as i:
                pair(i, i + 1)
            pair(PAIRS - 1, None)
            finish(PAIRS - 1, NO - 2)
            finish(PAIRS - 1, NO - 1)

        @block.tensor
        def _(pe):
            pe.wait_ge(const_ready, 2)

            def score(i, n):
                j, u, k0, kt = units[n]
                if n % UH == 0:
                    pe.wait_ge(split, 6 * i + 3 * j + 3)
                    pe.wait_ge(rows_loaded[j], 32 * i + 32)
                q = slice(u * P, (u + 1) * P)
                s0 = (n % 2) * 2 * BANK
                for t in range(0, kt, 4):
                    nt = min(4, kt - t)
                    out = psum[:, s0 + t * P:s0 + (t + nt) * P]
                    keys = slice((k0 + t) * P, (k0 + t + nt) * P)
                    masked = t + nt == kt
                    nc.tensor.matmul(out, q_a[:, j, q], k_a[:, j, keys], start=True, stop=False)
                    last = nc.tensor.matmul(out, q_b[:, j, q], k_b[:, j, keys], start=False, stop=not masked)
                    if masked:
                        last = nc.tensor.matmul(psum[:, s0 + (kt - 1) * P:s0 + kt * P], ident_r[:],
                                                masks_r[:, 0 if u < UH - 1 else 1, :], start=False, stop=True)
                last.then_inc(scored, 1)

            def transpose(i, n, first):
                for x, (m, t0, nt) in enumerate(groups):
                    if m == n:
                        if x in after_tail and not first:
                            pe.wait_ge(tail_copied, NTL * i - NTL + after_tail[x] + 1)
                        elif x >= 2 or not first:
                            pe.wait_ge(p_split, NG * i + x - 1)
                        for t in range(nt):
                            at = (4 + x % 2) * BANK + t * P
                            last = nc.tensor.transpose(psum[:, at:at + P], e[:, n % 2, (t0 + t) * P:(t0 + t + 1) * P],
                                                       ident[:])
                        last.then_inc(transposed, 1)

            def values(i, n, first=False):
                j, u, k0, kt = units[n]
                x = out_of[n]
                pe.wait_ge(p_split, NG * i + last_group[n] + 1)
                if n == outs[x][0] and (x >= 2 or not first):
                    pe.wait_ge(o_summed, NO * i + x - 1)
                at = (6 + x % 2) * BANK + (n - outs[x][0]) * P
                for t in range(kt):
                    keys = slice(t * P, (t + 1) * P)
                    nc.tensor.matmul(psum[:, at:at + P], p_hi[:, n % 2, keys], v_a[:, j, k0 + t, :],
                                     start=(t == 0), stop=False)
                    last = nc.tensor.matmul(psum[:, at:at + DF], p_lo[:, n % 2, keys], v_a[:, j, k0 + t, 0:DF],
                                            start=False, stop=(t == kt - 1))
                last.then_inc(pv, 1)

            def tail(i, y, splits):
                _, t0, nt = tails[y]
                pe.wait_ge(o_done, NO * i + NO)
                pe.wait_ge(p_split, splits)
                if y >= 2 and tails[y - 2][0] == tails[y][0]:
                    pe.wait_ge(tail_copied, NTL * i + y - 1)
                for t in range(t0, t0 + nt):
                    at = (4 + tail_bank[y]) * BANK + (t - t0) * P
                    last = nc.tensor.transpose(psum[:, at:at + P], o_tok[:, t, :], ident[:])
                last.then_inc(tail_transposed, 1)

            def pair(i, next_i, first=False):
                for n in range(U):
                    pe.wait_ge(exped, U * i + n + 1)
                    if n + 2 < U:
                        score(i, n + 2)
                    elif next_i is not None:
                        score(next_i, n + 2 - U)
                    own_tails = [y for y, q in enumerate(tails) if q[0] == n and not first]
                    for y in own_tails:
                        tail(i - 1, y, NG * i + last_group[n - 1] + y % 2)
                    if own_tails:
                        values(i, n - 1, first)
                    transpose(i, n, first)
                    if n >= 1 and not own_tails:
                        values(i, n - 1, first)
                    if n == 0 and not first:
                        values(i - 1, U - 1)
            score(0, 0)
            score(0, 1)
            pair(0, 1, first=True)
            with pe.Fori(1, PAIRS - 1) as i:
                pair(i, i + 1)
            pair(PAIRS - 1, None)
            values(PAIRS - 1, U - 1)
            for y in range(NTL):
                if y >= 2:
                    pe.wait_ge(tail_copied, NTL * (PAIRS - 1) + y - 1)
                tail(PAIRS - 1, y, NG * PAIRS)


def project(nc, g, tag, weights, tiles, source, resident, evict, extras=()):
    op, out, gate_src = evict["op"], evict["out"], evict.get("gate")
    with ExitStack() as es:
        sb = lambda n, s, dt=F32: es.enter_context(nc.sbuf_tensor(f"{tag}_{n}", s, dt))
        sem = semaphores(nc, es, tag)
        two = lambda n: [sem(f"{n}{j}") for j in range(2)]
        x_hi, x_lo = sb("x_hi", [P, DC, TOK], F32R), sb("x_lo", [P, DC, TOK], F32R)
        x_raw = None if resident else sb("x_raw", [P, 2, TOK])
        raw, w_hi, w_lo = sb("raw", [P, 2, DC, P]), sb("w_hi", [P, 2, DC, P], F32R), sb("w_lo", [P, 2, DC, P], F32R)
        gate = sb("gate", [P, 2, TOK]) if gate_src is not None else None
        loaded, x_loaded, gate_loaded = two("loaded"), two("x_loaded"), two("gate_loaded")
        rounded, split, x_rounded, x_split = sem("rounded"), sem("split"), sem("x_rounded"), sem("x_split")
        multiplied, evicted, step = sem("multiplied"), sem("evicted"), sem("step")
        psum = g.psum
        block = es.enter_context(nc.Block())

        def chunk(c):
            return source[:, c, :] if resident else x_raw[:, c % 2, :]

        @block.sync
        def _(sp):
            def load(t):
                if t >= 2:
                    sp.wait_ge(split, t - 1)
                sp.dma_start(raw[:, t % 2].rearrange("p c n -> p (c n)"), weights(t)).then_inc(loaded[t % 2], 16)

            def load_gate(t):
                if gate is not None:
                    if t >= 2:
                        sp.wait_ge(evicted, t - 1)
                    sp.dma_start(gate[:, t % 2, :], gate_src(t)).then_inc(gate_loaded[t % 2], 16)
            load(0)
            if not resident:
                for c in range(DC):
                    if c >= 2:
                        sp.wait_ge(x_split, c - 1)
                    sp.dma_start(x_raw[:, c % 2, :], source(c)).then_inc(x_loaded[c % 2], 16)
            load(1)
            load_gate(0)
            load_gate(1)
            for t in range(2, tiles):
                load(t)
                load_gate(t)

        @block.scalar
        def _(act):
            def round_tile(t):
                act.wait_ge(loaded[t % 2], 16 * (t // 2 + 1))
                if t >= 2:
                    act.wait_ge(multiplied, t - 1)
                nc.scalar.activation(w_hi[:, t % 2], raw[:, t % 2], ACT.Copy).then_inc(rounded, 1)
            round_tile(0)
            for c in range(DC):
                if not resident:
                    act.wait_ge(x_loaded[c % 2], 16 * (c // 2 + 1))
                nc.scalar.activation(x_hi[:, c, :], chunk(c), ACT.Copy).then_inc(x_rounded, 1)
            for t in range(1, tiles):
                round_tile(t)

        @block.vector
        def _(dve):
            done = [0]

            def rest(t):
                dve.wait_ge(rounded, t + 1)
                nc.vector.tensor_tensor(w_lo[:, t % 2], raw[:, t % 2], w_hi[:, t % 2].bitcast(F32),
                                        ALU.subtract).then_inc(split, 1)
            rest(0)
            for c in range(DC):
                dve.wait_ge(x_rounded, c + 1)
                nc.vector.tensor_tensor(x_lo[:, c, :], chunk(c), x_hi[:, c, :].bitcast(F32),
                                        ALU.subtract).then_inc(x_split, 1)
            for t in range(tiles):
                if t + 1 < tiles:
                    rest(t + 1)
                dve.wait_ge(multiplied, t + 1)
                if gate is not None:
                    dve.wait_ge(gate_loaded[t % 2], 16 * (t // 2 + 1))
                s = slab_views(psum, 3 * (t % 2), out[:, t, :])
                gv = slab_views(psum, 0, gate[:, t % 2, :]) if gate is not None else s
                for n in range(2):
                    (p, o), (_, x) = s[n], gv[n]
                    if op == "copy":
                        last = nc.vector.tensor_copy(o, p)
                    elif op in ("mul", "add"):
                        last = nc.vector.tensor_tensor(o, p, x, ALU.mult if op == "mul" else ALU.add)
                    else:
                        last = nc.vector.tensor_tensor(o, p, o, ALU.add)
                if op == "add_mul_add":
                    last.then_inc(step, 1)
                    dve.wait_ge(step, 2 * t + 1)
                    nc.vector.tensor_tensor(out[:, t, :], out[:, t, :], gate[:, t % 2, :], ALU.mult).then_inc(step, 1)
                    dve.wait_ge(step, 2 * t + 2)
                    last = nc.vector.tensor_tensor(out[:, t, :], out[:, t, :], evict["plus"][:, t, :], ALU.add)
                last.then_inc(evicted, 1)

        @block.tensor
        def _(pe):
            for t in range(tiles):
                pe.wait_ge(split, t + 1)
                if t >= 2:
                    pe.wait_ge(evicted, t - 1)
                for c in range(DC):
                    if t == 0:
                        pe.wait_ge(x_split, c + 1)
                    for n, (w, x) in enumerate(((w_hi, x_hi), (w_hi, x_lo), (w_lo, x_hi))):
                        for s, (t0, width) in enumerate(SLABS):
                            at = (3 * (t % 2) + s) * BANK
                            last = nc.tensor.matmul(psum[:, at:at + width], w[:, t % 2, c, :], x[:, c, t0:t0 + width],
                                                    start=(c == 0 and n == 0), stop=(c == DC - 1 and n == 2))
                last.then_inc(multiplied, 1)


def merge(nc, g, x1):
    GA, GB = NSILU, NSILU + DC
    part_a = x1
    with nc.sbuf_tensor("part_r", [P, DC, TOK], F32) as part_r:
        project(nc, g, "ma", lambda t: g.w_branch[t, :, :], DC, lambda c: g.o_fox[c, :, :], False,
                {"op": "mul", "out": part_a, "gate": lambda t: g.gates[GA + t, :, :]})
        project(nc, g, "mr0", lambda t: g.w_branch[DC + t, :, :], DC, lambda c: g.o_ret[c, :, :], False,
                {"op": "copy", "out": part_r})
        project(nc, g, "mr1", lambda t: g.w_branch[2 * DC + t, :, :], DC, lambda c: g.o_ret[DC + c, :, :], False,
                {"op": "add_mul_add", "out": part_r, "plus": part_a, "gate": lambda t: g.gates[GB + t, :, :]})
        project(nc, g, "mo", lambda t: g.w_out[t, :, :], DC, part_r, True,
                {"op": "add", "out": x1, "gate": lambda t: g.x_t[t * P:(t + 1) * P, :]})


def mlp(nc, g, x1, h_hi, h_lo):
    GROUPS = DFF // D
    NT = 2 * DC
    with ExitStack() as es:
        sb = lambda n, s, dt=F32: es.enter_context(nc.sbuf_tensor(f"ml_{n}", s, dt))
        sem = semaphores(nc, es, "ml")
        raw, w_hi, w_lo = sb("raw", [P, DC, P]), sb("w_hi", [P, 2, DC, P], F32R), sb("w_lo", [P, 2, DC, P], F32R)
        u_hi, u_lo = sb("u_hi", [P, DC, TOK], F32R), sb("u_lo", [P, DC, TOK], F32R)
        relu = sb("relu", [P, TOK])
        loaded, rounded, split, multiplied = sem("loaded"), sem("rounded"), sem("split"), sem("multiplied")
        relued, squared, u_rounded, u_split, added = (sem("relued"), sem("squared"), sem("u_rounded"),
                                                      sem("u_split"), sem("added"))
        psum = g.psum
        block = es.enter_context(nc.Block())

        @block.sync
        def _(sp):
            with sp.Fori(0, GROUPS) as i:
                for k in range(NT):
                    src = g.w_up[DC * i + k, :, :] if k < DC else g.w_down[DC * i + k - DC, :, :]
                    sp.wait_ge(split, NT * i + k)
                    sp.dma_start(raw[:].rearrange("p c n -> p (c n)"), src).then_inc(loaded, 16)

        @block.scalar
        def _(act):
            def round_tile(i, k):
                act.wait_ge(loaded, 16 * (NT * i + k + 1))
                nc.scalar.activation(w_hi[:, k % 2], raw[:], ACT.Copy).then_inc(rounded, 1)

            def group(i, next_i):
                for k in range(NT):
                    if k + 1 < NT or next_i is not None:
                        act.wait_ge(multiplied, NT * i + k)
                        if k + 1 < NT:
                            round_tile(i, k + 1)
                        else:
                            round_tile(next_i, 0)
                    if k < DC:
                        act.wait_ge(squared, DC * i + k + 1)
                        nc.scalar.activation(u_hi[:, k, :], relu[:], ACT.Copy).then_inc(u_rounded, 1)
            round_tile(0, 0)
            with act.Fori(0, GROUPS - 1) as i:
                group(i, i + 1)
            group(GROUPS - 1, None)

        @block.vector
        def _(dve):
            def rest(i, k):
                dve.wait_ge(rounded, NT * i + k + 1)
                nc.vector.tensor_tensor(w_lo[:, k % 2], raw[:], w_hi[:, k % 2].bitcast(F32), ALU.subtract)\
                    .then_inc(split, 1)

            def group(i, next_i):
                for k in range(NT):
                    if k + 1 < NT:
                        rest(i, k + 1)
                    elif next_i is not None:
                        rest(next_i, 0)
                    dve.wait_ge(multiplied, NT * i + k + 1)
                    if k < DC:
                        for src, dst in slab_views(psum, 3 * (k % 2), relu):
                            last = nc.vector.tensor_scalar(dst, src, 0.0, None, ALU.max)
                        last.then_inc(relued, 1)
                        dve.wait_ge(relued, DC * i + k + 1)
                        nc.vector.tensor_tensor(relu[:], relu[:], relu[:], ALU.mult).then_inc(squared, 1)
                        dve.wait_ge(u_rounded, DC * i + k + 1)
                        nc.vector.tensor_tensor(u_lo[:, k, :], relu[:], u_hi[:, k, :].bitcast(F32), ALU.subtract)\
                            .then_inc(u_split, 1)
                        dve.wait_ge(u_split, DC * i + k + 1)
                    else:
                        for src, dst in slab_views(psum, 3 * (k % 2), x1[:, k - DC, :]):
                            last = nc.vector.tensor_tensor(dst, src, dst, ALU.add)
                        last.then_inc(added, 1)
            rest(0, 0)
            with dve.Fori(0, GROUPS - 1) as i:
                group(i, i + 1)
            group(GROUPS - 1, None)

        @block.tensor
        def _(pe):
            with pe.Fori(0, GROUPS) as i:
                for k in range(NT):
                    pe.wait_ge(split, NT * i + k + 1)
                    up = k < DC
                    if k < 2:
                        pe.wait_ge(added, DC * i)
                    elif k < DC + 2:
                        pe.wait_ge(relued, DC * i + k - 1)
                    else:
                        pe.wait_ge(added, DC * i + k - 1 - DC)
                    x_hi, x_lo = (h_hi, h_lo) if up else (u_hi, u_lo)
                    for c in range(DC):
                        if k == DC:
                            pe.wait_ge(u_split, DC * i + c + 1)
                        for n, (w, x) in enumerate(((w_hi, x_hi), (w_hi, x_lo), (w_lo, x_hi))):
                            for s, (t0, width) in enumerate(SLABS):
                                at = (3 * (k % 2) + s) * BANK
                                last = nc.tensor.matmul(psum[:, at:at + width], w[:, k % 2, c, :],
                                                        x[:, c, t0:t0 + width],
                                                        start=(c == 0 and n == 0), stop=(c == DC - 1 and n == 2))
                    last.then_inc(multiplied, 1)


class Shared:
    pass


def run(nc, a):
    with ExitStack() as es:
        g = Shared()
        (g.x_t, g.w_tok, g.w_feat, g.b_forget, g.g_attn, g.g_mlp, g.g_final, g.cos_t, g.sin_t, g.cache_logf,
         g.cache_kt, g.cache_v, g.state_in, g.w_branch, g.w_out, g.w_up, g.w_down,
         g.ret_cols, g.ret_decay, g.ret_qdec, g.masks, g.ident_t) = a["ins"]
        g.v_out, g.qk_out, g.logf_out, g.state_out, g.y_out = a["outs"]
        scratch = lambda n, s: nc.dram_tensor(n, s, F32, kind="Internal").ap()
        g.qk_ret, g.gates = scratch("qk_ret", [NROPE, P, TOK]), scratch("gates", [NSILU + NSIG, P, TOK])
        g.v_ret, g.o_ret = scratch("v_ret", [HR, TOK, DV]), scratch("o_ret", [2 * DC, P, TOK])
        g.o_fox = scratch("o_fox", [DC, P, TOK])
        g.q_rows, g.k_rows = scratch("q_rows", [HF, 4, TOK]), scratch("k_rows", [HF, 4, KEYS])
        g.psum = es.enter_context(nc.psum_tensor("psum", [P, 8 * BANK], F32))
        sb = lambda n, s, dt=F32: es.enter_context(nc.sbuf_tensor(n, s, dt))
        g.ones, g.eps = sb("ones", [P, P]), sb("eps", [P, 1])
        zf = sb("zf", [HF, TOK])
        with nc.Block() as block:
            @block.vector
            def _(dve):
                nc.vector.memset(g.ones[:], 1.0)
                nc.vector.memset(g.eps[:], EPS)
        with ExitStack() as hs:
            h_hi = hs.enter_context(nc.sbuf_tensor("h_hi", [P, DC, TOKP], F32R))
            h_lo = hs.enter_context(nc.sbuf_tensor("h_lo", [P, DC, TOKP], F32R))
            with nc.Block() as block:
                @block.vector
                def _(dve):
                    nc.vector.memset(h_hi[:, :, TOK:TOKP].bitcast(F32), 0.0)
                    nc.vector.memset(h_lo[:, :, TOK:TOKP].bitcast(F32), 0.0)
            with nc.sbuf_tensor("x0", [P, DC, TOK], F32) as x0:
                rms_norm(nc, g, "n1", x0, g.x_t, g.g_attn, hi=h_hi[:, :, 0:TOK], lo=h_lo[:, :, 0:TOK])
            values(nc, g, h_hi, h_lo)
            features(nc, g, h_hi, h_lo, zf)
        decay(nc, g, zf)
        retention(nc, g)
        fox(nc, g)
        x1 = sb("x1", [P, DC, TOK])
        merge(nc, g, x1)
        with ExitStack() as hs:
            h_hi = hs.enter_context(nc.sbuf_tensor("m_hi", [P, DC, TOK], F32R))
            h_lo = hs.enter_context(nc.sbuf_tensor("m_lo", [P, DC, TOK], F32R))
            rms_norm(nc, g, "n2", x1, None, g.g_mlp, hi=h_hi, lo=h_lo)
            mlp(nc, g, x1, h_hi, h_lo)
        rms_norm(nc, g, "n3", x1, None, g.g_final, out=g.y_out)



def _tiles(w, chunks, width):
    k, n = w.shape
    return np.ascontiguousarray(w.reshape(chunks, P, n // width, width).transpose(2, 1, 0, 3)
                                .reshape(n // width, P, chunks * width))


def _cols(v):
    return np.ascontiguousarray(v.reshape(-1, P).T)


def _tables():
    f = np.float32
    inv = (f(10000.0) ** (-np.arange(0, DK, 2, dtype=f) / f(DK))).astype(f)
    pos = np.concatenate([np.arange(SEQ), PAST + np.arange(DEC)]).astype(f)
    ang = inv[:, None] * pos[None, :]
    lg = np.log(f(1.0) - f(2.0) ** (f(-5.0) - np.arange(HR, dtype=f))).astype(f)
    m, j = np.arange(P), np.arange(SEQ)
    dist = np.abs(j[None, :] - m[:, None]).astype(f)
    seen = (m[:, None] // CHUNK) <= (j[None, :] // CHUNK)
    kscale = f(DK ** -0.5)
    table = np.where(seen[None], np.exp(lg[:, None, None] * dist[None]), 0).astype(f) * kscale
    cols = np.zeros((HR, P, TT + 1), f)
    for t in range(TT - 1):
        cols[:, :, t] = np.exp(lg[:, None] * (SEQ - 1 - t * P - m)[None].astype(f)) * kscale
    cols[:, :DEC, TT - 1] = np.exp(lg[:, None] * (DEC - 1 - m[:DEC])[None].astype(f)) * kscale
    cols[:, :, TT] = np.exp(lg * f(DEC))[:, None]
    qdec = np.broadcast_to(np.exp(lg[:, None] * (np.arange(DEC, dtype=f) + 1))[:, None, :], (HR, P, DEC))
    q, k = np.arange(P)[:, None], np.arange(P)[None, :]
    masks = np.stack([np.where(k <= q, 0, NEG), np.where((k <= q) & (k < DEC), 0, NEG)], 1).astype(f)
    return (np.cos(ang).astype(f), np.sin(ang).astype(f), cols, np.ascontiguousarray(table),
            np.ascontiguousarray(qdec), np.ascontiguousarray(masks), np.eye(P, dtype=f))


def kernel(x_prompt, x_sample, cache_fox_k, cache_fox_v, cache_fox_logf, state_ret,
           g_attn, w_in, b_forget, g_ret_norm, w_branch, w_out, g_mlp, w_up, w_down, g_final):
    import concourse.bacc as bacc
    from concourse.bass_utils import run_bass_kernel_spmd

    npa = lambda v: np.asarray(v)
    x_t = np.ascontiguousarray(np.concatenate([npa(x_prompt)[0], npa(x_sample)[0]], 0).T)
    w_in, w_branch, w_out, w_up, w_down = (npa(w)[0] for w in (w_in, w_branch, w_out, w_up, w_down))
    widths = (1024, 1024, 1024, HF, 1024, 1024, 2048, 2048, 1024, 1024)
    qf, kf, vf, ff, qr, kr, vr, gr, ga, gb = np.split(w_in, np.cumsum(widths)[:-1], 1)
    w_tok = _tiles(np.concatenate([vf, vr], 1), DC, 512)
    w_feat = _tiles(np.concatenate([qf, kf, qr, kr, gr, ga, gb, ff, np.zeros((D, P - HF), np.float32)], 1), DC, P)
    cos, sin, cols, table, qdec, masks, ident = _tables()
    ret_cols = np.concatenate([cols, npa(g_ret_norm)[0].reshape(HR, DV // P, P).transpose(0, 2, 1)], 2)
    ins = {
        "x_t": x_t, "w_tok": w_tok, "w_feat": w_feat, "b_forget": npa(b_forget)[0].reshape(HF, 1),
        "g_attn": _cols(npa(g_attn)[0]), "g_mlp": _cols(npa(g_mlp)[0]), "g_final": _cols(npa(g_final)),
        "cos_t": cos, "sin_t": sin,
        "cache_logf": npa(cache_fox_logf)[0, 0].T, "cache_kt": npa(cache_fox_k)[0, 0].transpose(1, 2, 0),
        "cache_v": npa(cache_fox_v)[0, 0].reshape(PAST, HF * DF), "state_in": npa(state_ret)[0, 0],
        "w_branch": np.concatenate([_tiles(w_branch[n * D:(n + 1) * D], DC, P) for n in range(3)], 0),
        "w_out": _tiles(w_out, DC, P), "w_up": _tiles(w_up, DC, P),
        "w_down": np.concatenate([_tiles(w_down[n * D:(n + 1) * D], DC, P) for n in range(DFF // D)], 0),
        "ret_cols": ret_cols, "ret_decay": table, "ret_qdec": qdec, "masks": masks, "ident_t": ident,
    }
    ins = {n: np.ascontiguousarray(v) for n, v in ins.items()}
    outs = {"v": (TOK, D), "qk": (NPLAIN, P, TOK), "logf": (HF, TOK),
            "state": (2, HR, DK, DV), "y": (D, TOK)}
    nc = bacc.Bacc("TRN2", target_bir_lowering=False, num_devices=1)
    args = {
        "ins": [nc.dram_tensor(f"in_{n}", v.shape, F32, kind="ExternalInput").ap() for n, v in ins.items()],
        "outs": [nc.dram_tensor(f"out_{n}", s, F32, kind="ExternalOutput").ap() for n, s in outs.items()],
    }
    run(nc, args)
    got = run_bass_kernel_spmd(nc, [{f"in_{n}": v for n, v in ins.items()}], core_ids=[0]).results[0]
    v, qk, logf, state, y = (got[f"out_{n}"] for n in outs)
    y = y.T
    k = qk[DC:].reshape(D, TOK).T.reshape(TOK, HF, DF)
    v = v.reshape(TOK, HF, DF)
    f = logf.T
    own = np.ascontiguousarray
    return (own(y[None, :SEQ]), own(y[None, SEQ:]), own(k[None, None, :SEQ]), own(v[None, None, :SEQ]),
            own(f[None, None, :SEQ]), own(state[None, 1:2]), own(k[None, None, SEQ:]),
            own(v[None, None, SEQ:]), own(f[None, None, SEQ:]), own(state[None, 0:1]))
```

```python
from contextlib import ExitStack

import numpy as np
import concourse.bass as bass
from concourse import mybir

F32 = mybir.dt.float32
F32R = mybir.dt.float32r
ACT = mybir.ActivationFunctionType
ALU = mybir.AluOpType
AX = mybir.AxisListType.X

P = 128
D = 1024
DC = D // P
SEQ = 1024
DEC = 64
PAST = 256
TOK = SEQ + DEC
TOKP = SEQ + P
TT = TOKP // P
SLABS = ((0, 384), (384, 384), (768, 320))
BANK = 512
HF = 16
DF = 64
HR = 4
DK = 256
DV = 512
CHUNK = 64
DFF = 4096
EPS = 1e-6
NEG = -1e30
KEYS = SEQ + PAST + P
KT = KEYS // P
NPLAIN, NROPE, NSILU, NSIG = 16, 16, 16, 16
VGROUP = 512
NFEAT = NPLAIN + NROPE + NSILU + NSIG


def semaphores(nc, es, tag):
    handles = []

    def done():
        nc.clear_and_free_semaphores(handles)
        nc.all_engine_barrier()
    es.callback(done)

    def sem(name):
        handles.append(nc.alloc_semaphore(name=f"{tag}_{name}"))
        return handles[-1]
    return sem


def gemm_tile(nc, psum, bank, w_hi, w_lo, x_hi, x_lo, chunks):
    for c in range(chunks):
        for n, (w, x) in enumerate(((w_hi, x_hi), (w_hi, x_lo), (w_lo, x_hi))):
            for s, (t0, width) in enumerate(SLABS):
                at = (bank + s) * BANK
                last = nc.tensor.matmul(psum[:, at:at + width], w[:, c, :], x[:, c, t0:t0 + width],
                                        start=(c == 0 and n == 0), stop=(c == chunks - 1 and n == 2))
    return last


def slab_views(psum, bank, x):
    at = bank * BANK
    two = psum[:, at:at + 2 * BANK].rearrange("p (s n) -> p s n", n=BANK)[:, :, 0:384]
    return ((two, x[:, 0:768].rearrange("p (s n) -> p s n", n=384)),
            (psum[:, at + 2 * BANK:at + 2 * BANK + 320], x[:, 768:TOK]))


def rms_norm(nc, g, tag, x, gain, load=None, hi=None, lo=None, out=None, ahead=None):
    SLOTS = 4
    pool_chunks = (1, 4) if out is None else ()
    with ExitStack() as es:
        sb = lambda n, s, dt=F32: es.enter_context(nc.sbuf_tensor(f"{tag}_{n}", s, dt))
        sem = semaphores(nc, es, tag)
        gcol, sq = sb("gcol", [P, DC]), sb("sq", [P, 2, TOK]) if load is not None else None
        rs, prod, acc = sb("rs", [P, TOK]), sb("prod", [P, SLOTS, TOK]), g.acc
        loaded = [sem(f"loaded{c}") for c in range(DC)] if load is not None else None
        squared, summed = sem("squared"), sem("summed")
        total, logged, inverted = sem("total"), sem("logged"), sem("inverted")
        scaled, rounded, gain_loaded = sem("scaled"), sem("rounded"), sem("gain_loaded")
        stored = [sem(f"stored{n}") for n in range(SLOTS)] if out is not None else None
        rest_dve, rest_pool = sem("rest_dve"), sem("rest_pool")
        w_loaded, w_rounded, w_split = sem("w_loaded"), sem("w_rounded"), sem("w_split")
        psum = g.psum
        block = es.enter_context(nc.Block())

        def load_chunk(engine, c):
            engine.dma_start(x[:, c, :], load[c * P:(c + 1) * P, :]).then_inc(loaded[c], 16)

        def store_chunk(engine, c):
            engine.wait_ge(scaled, c + 1)
            engine.dma_start(out[c * P:(c + 1) * P, :], prod[:, c % SLOTS, :]).then_inc(stored[c % SLOTS], 16)

        @block.sync
        def _(sp):
            if load is not None:
                for c in range(0, DC, 2):
                    load_chunk(sp, c)
            sp.dma_start(gcol[:], gain).then_inc(gain_loaded, 16)
            if ahead is not None:
                sp.dma_start(ahead[0], ahead[3]).then_inc(w_loaded, 16)
            if out is not None:
                for c in range(0, DC, 2):
                    store_chunk(sp, c)
                for n in range(SLOTS):
                    sp.wait_ge(stored[n], 16 * DC // SLOTS)

        @block.scalar
        def _(act):
            if load is not None:
                for c in range(1, DC, 2):
                    load_chunk(act, c)
                for c in range(DC):
                    act.wait_ge(loaded[c], 16)
                    if c >= 2:
                        act.wait_ge(summed, c - 1)
                    nc.scalar.activation(sq[:, c % 2, :], x[:, c, :], ACT.Square).then_inc(squared, 1)
            act.wait_ge(total, 1)
            for a, b in slab_views(psum, 0, rs):
                last = nc.scalar.activation(b, a, ACT.Ln, bias=g.eps[:, 0:1], scale=1.0 / D)
            last.then_inc(logged, 1)
            act.wait_ge(logged, 1)
            nc.scalar.activation(rs[:], rs[:], ACT.Exp, scale=-0.5).then_inc(inverted, 1)
            if out is None:
                for c in range(DC):
                    act.wait_ge(scaled, c + 1)
                    nc.scalar.activation(hi[:, c, :], prod[:, c % SLOTS, :], ACT.Copy).then_inc(rounded, 1)
                    if c == 2:
                        act.wait_ge(w_loaded, 16)
                        nc.scalar.activation(ahead[1], ahead[0], ACT.Copy).then_inc(w_rounded, 1)
            else:
                for c in range(1, DC, 2):
                    store_chunk(act, c)

        @block.gpsimd
        def _(pool):
            for c in pool_chunks:
                if c == pool_chunks[-1]:
                    pool.wait_ge(w_rounded, 1)
                    nc.gpsimd.tensor_tensor(ahead[2], ahead[0], ahead[1].bitcast(F32),
                                            ALU.subtract).then_inc(w_split, 1)
                pool.wait_ge(rounded, c + 1)
                nc.gpsimd.tensor_tensor(lo[:, c, :], prod[:, c % SLOTS, :], hi[:, c, :].bitcast(F32),
                                        ALU.subtract).then_inc(rest_pool, 1)

        @block.vector
        def _(dve):
            if load is not None:
                for c in range(DC):
                    dve.wait_ge(squared, c + 1)
                    if c == 0:
                        nc.vector.tensor_copy(acc[:], sq[:, 0, :]).then_inc(summed, 1)
                    else:
                        dve.wait_ge(summed, c)
                        nc.vector.tensor_tensor(acc[:], acc[:], sq[:, c % 2, :], ALU.add).then_inc(summed, 1)
            dve.wait_ge(inverted, 1)
            dve.wait_ge(gain_loaded, 16)
            own = [c for c in range(DC) if c not in pool_chunks]

            def rest(c):
                dve.wait_ge(rounded, c + 1)
                nc.vector.tensor_tensor(lo[:, c, :], prod[:, c % SLOTS, :], hi[:, c, :].bitcast(F32),
                                        ALU.subtract).then_inc(rest_dve, 1)
            for c in range(DC):
                before = c - SLOTS
                if before >= 0:
                    if out is not None:
                        dve.wait_ge(stored[c % SLOTS], 16)
                    elif before in own:
                        dve.wait_ge(rest_dve, own.index(before) + 1)
                    else:
                        dve.wait_ge(rest_pool, pool_chunks.index(before) + 1)
                nc.vector.scalar_tensor_tensor(prod[:, c % SLOTS, :], x[:, c, :], gcol[:, c:c + 1], rs[:],
                                               ALU.mult, ALU.mult).then_inc(scaled, 1)
                if out is None and c >= 2 and c - 2 in own:
                    rest(c - 2)
            if out is None:
                rest(DC - 2)
                rest(DC - 1)

        @block.tensor
        def _(pe):
            if load is not None:
                pe.wait_ge(summed, DC)
            for s, (t0, width) in enumerate(SLABS):
                last = nc.tensor.matmul(psum[:, s * BANK:s * BANK + width], g.ones[:, :], acc[:, t0:t0 + width],
                                        start=True, stop=True)
            last.then_inc(total, 1)


def values(nc, g, h_hi, h_lo, raw, w_hi0, w_lo0):
    GROUP = VGROUP
    with ExitStack() as es:
        sb = lambda n, s, dt=F32: es.enter_context(nc.sbuf_tensor(f"val_{n}", s, dt))
        sem = semaphores(nc, es, "val")
        w_hi = (w_hi0, sb("w_hi1", [P, DC, GROUP], F32R))
        w_lo = (w_lo0, sb("w_lo1", [P, DC, GROUP], F32R))
        stage = sb("stage", [P, 2, GROUP])
        loaded, rounded, split = sem("loaded"), sem("rounded"), sem("split")
        multiplied, staged, stored = sem("multiplied"), sem("staged"), [sem(f"stored{n}") for n in range(2)]
        psum, BANKS = g.psum, 6
        tiles = 2 * TT
        block = es.enter_context(nc.Block())

        @block.sync
        def _(sp):
            for n in range(2):
                sp.sem_inc(stored[n], 16)

            def load(i, j, splits):
                sp.wait_ge(split, splits)
                sp.dma_start(raw[:].rearrange("p c n -> p (c n)"),
                             g.w_tok[2 * i + j, :, :]).then_inc(loaded, 16)

            def store(i, next_i, dst, prompt0=0, sample0=SEQ):
                for k in range(tiles):
                    if next_i is not None and k in (4, TT + 4):
                        load(next_i, k // TT, 2 * i + k // TT + 2)
                    j, t = k // TT, k % TT
                    rows = DEC if t == TT - 1 else P
                    sp.wait_ge(staged, tiles * i + k + 1)
                    row = sample0 if t == TT - 1 else prompt0 + t * P
                    sp.dma_start(dst(j)[row:row + rows, :],
                                 stage[0:rows, k % 2, :]).then_inc(stored[k % 2], 16)
            sp.sem_inc(loaded, 16)
            sp.dma_start(raw[:].rearrange("p c n -> p (c n)"), g.w_tok[1, :, :]).then_inc(loaded, 16)
            store(0, 1, lambda j: g.v_out[:, j * GROUP:(j + 1) * GROUP])
            with sp.Fori(1, 2) as i:
                store(i, i + 1, lambda j: g.v_ret[2 * i - 2 + j, :, :], DEC, 0)
            store(2, None, lambda j: g.v_ret[2 + j, :, :], DEC, 0)
            for n in range(2):
                sp.wait_ge(stored[n], 16 + 16 * 3 * tiles // 2)

        @block.scalar
        def _(act):
            def round_group(i, j):
                act.wait_ge(loaded, 32 * i + 16 * (j + 1))
                nc.scalar.activation(w_hi[j][:], raw[:], ACT.Copy).then_inc(rounded, 1)
            act.sem_inc(rounded, 1)
            round_group(0, 1)
            with act.Fori(1, 3) as i:
                for j in range(2):
                    act.wait_ge(multiplied, tiles * i - TT * (1 - j))
                    round_group(i, j)

        @block.vector
        def _(dve):
            def take(i, j):
                dve.wait_ge(rounded, 2 * i + j + 1)
                nc.vector.tensor_tensor(w_lo[j][:], raw[:], w_hi[j][:].bitcast(F32),
                                        ALU.subtract).then_inc(split, 1)
            dve.sem_inc(split, 1)

            def evict(i, next_i):
                for k in range(tiles):
                    if k == 3:
                        take(i, 1)
                    if k == TT + 3 and next_i is not None:
                        take(next_i, 0)
                    dve.wait_ge(multiplied, tiles * i + k + 1)
                    dve.wait_ge(stored[k % 2], 8 * tiles * i + 16 * (k // 2 + 1))
                    rows = DEC if k % TT == TT - 1 else P
                    nc.vector.tensor_copy(stage[0:rows, k % 2, :],
                                          psum[0:rows, (k % BANKS) * BANK:(k % BANKS + 1) * BANK])\
                        .then_inc(staged, 1)
            with dve.Fori(0, 2) as i:
                evict(i, i + 1)
            evict(2, None)

        @block.tensor
        def _(pe):
            with pe.Fori(0, 3) as i:
                for k in range(tiles):
                    j, t = k // TT, k % TT
                    if t == 0:
                        pe.wait_ge(split, 2 * i + j + 1)
                    if k >= BANKS:
                        pe.wait_ge(staged, tiles * i + k + 1 - BANKS)
                    else:
                        pe.wait_ge(staged, tiles * i)
                    at = (k % BANKS) * BANK
                    cols = slice(t * P, (t + 1) * P)
                    for c in range(DC):
                        for n, (h, w) in enumerate(((h_hi, w_hi), (h_hi, w_lo), (h_lo, w_hi))):
                            last = nc.tensor.matmul(psum[:, at:at + BANK], h[:, c, cols], w[j][:, c, :],
                                                    start=(c == 0 and n == 0), stop=(c == DC - 1 and n == 2))
                    last.then_inc(multiplied, 1)


def features(nc, g, h_hi, h_lo):
    with ExitStack() as es:
        sb = lambda n, s, dt=F32: es.enter_context(nc.sbuf_tensor(f"ft_{n}", s, dt))
        sem = semaphores(nc, es, "ft")
        raw = sb("raw", [P, 2, DC, P])
        w_hi, w_lo = sb("w_hi", [P, 2, DC, P], F32R), sb("w_lo", [P, 2, DC, P], F32R)
        stage, tmp = sb("stage", [P, 2, TOK]), sb("tmp", [P, 2, TOK])
        prods = sb("prods", [P, 4, TOK])
        cos, sin = sb("cos", [P, TOK]), sb("sin", [P, TOK])
        bias = sb("bias", [HF, 1])
        loaded, rounded, split = [sem(f"loaded{j}") for j in range(2)], sem("rounded"), sem("split")
        tables, multiplied = sem("tables"), sem("multiplied")
        copied, rotated, silued = sem("copied"), sem("rotated"), sem("silued")
        stored, rope_products = [sem(f"stored{j}") for j in range(2)], sem("rope_products")
        sigmoid = sem("sigmoid")
        S0 = SEQ + PAST
        zf, low, logf, ones, cum = sb("zf", [HF, TOK]), sb("low", [HF, TOK]), sb("logf", [HF, KEYS]), \
            sb("ones", [HF, KEYS]), sb("cum", [HF, KEYS])
        cum_hi = sb("cum_hi", [HF, KEYS], F32R)
        cum_lo, neg_hi, neg_lo = sb("cum_lo", [HF, KEYS]), sb("neg_hi", [HF, KEYS]), sb("neg_lo", [HF, KEYS])
        f_loaded, f_rounded, f_split, f_multiplied = (sem("f_loaded"), sem("f_rounded"), sem("f_split"),
                                                      sem("f_multiplied"))
        zf_ready, lowered, soft_step, logf_ready = sem("zf_ready"), sem("lowered"), sem("soft_step"), sem("logf_ready")
        cached, decay_step, decay_stored = sem("cached"), sem("decay_step"), sem("decay_stored")
        psum = g.psum
        plain, rope = (0, NPLAIN // 2), (NPLAIN // 2, (NPLAIN + NROPE) // 2)
        silu = (rope[1], rope[1] + NSILU // 2)
        sigm = (silu[1], silu[1] + NSIG // 2)
        block = es.enter_context(nc.Block())

        def at(j):
            return 3 * j

        @block.sync
        def _(sp):
            sp.dma_start(raw[:, 1].rearrange("p c n -> p (c n)"), g.w_feat[NFEAT, :, :]).then_inc(f_loaded, 16)
            sp.dma_start(raw[:, 0].rearrange("p c n -> p (c n)"), g.w_feat[0, :, :]).then_inc(loaded[0], 16)
            sp.dma_start(logf[:, SEQ:S0], g.cache_logf).then_inc(cached, 16)
            sp.wait_ge(f_split, 1)
            sp.dma_start(raw[:, 1].rearrange("p c n -> p (c n)"), g.w_feat[1, :, :]).then_inc(loaded[1], 16)
            sp.dma_start(bias[:], g.b_forget).then_inc(tables, 16)
            sp.dma_start(cos[:], g.cos_t).then_inc(tables, 16)
            sp.dma_start(sin[:], g.sin_t).then_inc(tables, 16)

            for j in range(2):
                sp.sem_inc(stored[j], 16)

            def next_load(t, j):
                sp.wait_ge(split, t - 1)
                sp.dma_start(raw[:, j].rearrange("p c n -> p (c n)"), g.w_feat[t, :, :]).then_inc(loaded[j], 16)

            def store(dst, first, staged, before, t, j):
                sp.wait_ge(staged, t + 1 - before)
                sp.dma_start(dst[t - first, :, :], stage[:, j, :]).then_inc(stored[j], 16)

            def body(i, dst, first, staged, before):
                for j in range(2):
                    next_load(2 * i + 2 + j, j)
                for j in range(2):
                    store(dst, first, staged, before, 2 * i + j, j)

            def bodies(start, end, *what):
                with sp.Fori(start, end) as i:
                    body(i, *what)
            body(0, g.qk_out, 0, copied, 0)
            sp.wait_ge(logf_ready, 2)
            sp.dma_start(g.logf_out[:, 0:SEQ], logf[:, 0:SEQ]).then_inc(decay_stored, 16)
            sp.dma_start(g.logf_out[:, SEQ:TOK], logf[:, S0:S0 + DEC]).then_inc(decay_stored, 16)
            sp.wait_ge(decay_step, 7)
            for row in range(2):
                sp.dma_start(g.q_rows[:, row, :], ones[:, 0:TOK]).then_inc(decay_stored, 16)
                sp.dma_start(g.k_rows[:, 2 + row, :], ones[:]).then_inc(decay_stored, 16)
            for row, part in enumerate((cum_hi.bitcast(F32), cum_lo)):
                sp.dma_start(g.q_rows[:, 2 + row, 0:SEQ], part[:, 0:SEQ]).then_inc(decay_stored, 16)
                sp.dma_start(g.q_rows[:, 2 + row, SEQ:TOK], part[:, S0:S0 + DEC]).then_inc(decay_stored, 16)
            for row, part in enumerate((neg_hi, neg_lo)):
                sp.dma_start(g.k_rows[:, row, :], part[:]).then_inc(decay_stored, 16)
            bodies(plain[0] + 1, plain[1], g.qk_out, 0, copied, 0)
            bodies(*rope, g.qk_ret, NPLAIN, rotated, NPLAIN)
            bodies(*silu, g.gates, NPLAIN + NROPE, silued, NPLAIN + NROPE)
            bodies(sigm[0], sigm[1] - 1, g.gates, NPLAIN + NROPE, copied, NROPE + NSILU)
            for j in range(2):
                store(g.gates, NPLAIN + NROPE, copied, NROPE + NSILU, NFEAT - 2 + j, j)
            for j in range(2):
                sp.wait_ge(stored[j], 16 + 16 * NFEAT // 2)
            sp.wait_ge(decay_stored, 16 * 12)

        @block.gpsimd
        def _(pool):
            with pool.Fori(*rope) as i:
                for j in range(2):
                    pool.wait_ge(rope_products, 4 * i - 4 * rope[0] + 3 + j)
                    pool.wait_ge(stored[j], 16 * (i + 1))
                    nc.gpsimd.tensor_tensor(stage[:, j, :], prods[:, 2 * j, :], prods[:, 2 * j + 1, :],
                                            ALU.subtract if j == 0 else ALU.add).then_inc(rotated, 1)

        @block.scalar
        def _(act):
            def round_tile(t, j, nth):
                act.wait_ge(loaded[j], 16 * (nth + 1))
                nc.scalar.activation(w_hi[:, j], raw[:, j], ACT.Copy).then_inc(rounded, 1)

            def ahead(i, j):
                act.wait_ge(multiplied, 2 * i + j)
                round_tile(2 * i + j + 1, 1 - j, i + j)
            act.wait_ge(f_loaded, 16)
            nc.scalar.activation(w_hi[:, 1], raw[:, 1], ACT.Copy).then_inc(f_rounded, 1)
            round_tile(0, 0, 0)
            act.wait_ge(tables, 48)
            act.wait_ge(f_multiplied, 1)
            for dst, src in ((zf[:, 0:768].rearrange("p (s n) -> p s n", n=384),
                              psum[0:HF, at(1) * BANK:(at(1) + 2) * BANK].rearrange("p (s n) -> p s n", n=BANK)[:, :, 0:384]),
                             (zf[:, 768:TOK], psum[0:HF, (at(1) + 2) * BANK:(at(1) + 2) * BANK + 320])):
                last = nc.scalar.activation(dst, src, ACT.Identity, bias=bias[:, 0:1])
            last.then_inc(zf_ready, 1)
            round_tile(1, 1, 0)
            act.wait_ge(zf_ready, 1)
            act.wait_ge(lowered, 1)
            nc.scalar.activation(zf[:], zf[:], ACT.Abs).then_inc(soft_step, 1)
            act.wait_ge(soft_step, 1)
            nc.scalar.activation(zf[:], zf[:], ACT.Exp, scale=-1.0).then_inc(soft_step, 1)
            act.wait_ge(soft_step, 2)
            nc.scalar.activation(zf[:], zf[:], ACT.Ln, bias=1.0).then_inc(soft_step, 1)

            def plain_body(i, scale, first=False):
                for j in range(2):
                    if not (first and j == 0):
                        ahead(i, j)
                    act.wait_ge(multiplied, 2 * i + j + 1)
                    act.wait_ge(stored[j], 16 * (i + 1))
                    views = slab_views(psum, at(j), stage[:, j, :])
                    nc.scalar.activation(views[0][1], views[0][0], ACT.Copy, scale=scale)
                    nc.scalar.activation(views[1][1], views[1][0], ACT.Copy, scale=scale).then_inc(copied, 1)
            plain_body(0, DF ** -0.5, first=True)
            with act.Fori(1, DC // 2) as i:
                plain_body(i, DF ** -0.5)
            with act.Fori(DC // 2, plain[1]) as i:
                plain_body(i, 1.0)
            with act.Fori(*rope) as i:
                for j in range(2):
                    ahead(i, j)
            with act.Fori(*silu) as i:
                for j in range(2):
                    ahead(i, j)
                    act.wait_ge(multiplied, 2 * i + j + 1)
                    act.wait_ge(silued, 2 * i + j - NPLAIN - NROPE)
                    views = slab_views(psum, at(j), tmp[:, j, :])
                    nc.scalar.activation(views[0][1], views[0][0], ACT.Sigmoid)
                    nc.scalar.activation(views[1][1], views[1][0], ACT.Sigmoid).then_inc(sigmoid, 1)
            def sigmoid_body(i, final=False):
                for j in range(2):
                    if not (final and j == 1):
                        ahead(i, j)
                    act.wait_ge(multiplied, 2 * i + j + 1)
                    act.wait_ge(stored[j], 16 * (i + 1))
                    views = slab_views(psum, at(j), stage[:, j, :])
                    nc.scalar.activation(views[0][1], views[0][0], ACT.Sigmoid)
                    nc.scalar.activation(views[1][1], views[1][0], ACT.Sigmoid).then_inc(copied, 1)
            with act.Fori(sigm[0], sigm[1] - 1) as i:
                sigmoid_body(i)
            sigmoid_body(sigm[1] - 1, final=True)

        @block.vector
        def _(dve):
            def rest(t, j):
                dve.wait_ge(rounded, t + 1)
                nc.vector.tensor_tensor(w_lo[:, j], raw[:, j], w_hi[:, j].bitcast(F32),
                                        ALU.subtract).then_inc(split, 1)
            dve.wait_ge(f_rounded, 1)
            nc.vector.tensor_tensor(w_lo[:, 1], raw[:, 1], w_hi[:, 1].bitcast(F32), ALU.subtract).then_inc(f_split, 1)
            rest(0, 0)
            nc.vector.memset(ones[:], 1.0)
            nc.vector.memset(logf[:, S0 + DEC:KEYS], 0.0)
            dve.wait_ge(zf_ready, 1)
            nc.vector.tensor_scalar(low[:], zf[:], 0.0, None, ALU.min).then_inc(lowered, 1)
            rest(1, 1)
            dve.wait_ge(lowered, 1)
            dve.wait_ge(soft_step, 3)
            nc.vector.tensor_tensor(logf[:, 0:SEQ], low[:, 0:SEQ], zf[:, 0:SEQ], ALU.subtract).then_inc(logf_ready, 1)
            nc.vector.tensor_tensor(logf[:, S0:S0 + DEC], low[:, SEQ:TOK], zf[:, SEQ:TOK],
                                    ALU.subtract).then_inc(logf_ready, 1)
            dve.wait_ge(logf_ready, 2)
            dve.wait_ge(cached, 16)
            nc.vector.tensor_tensor_scan(cum[:, 0:SEQ], ones[:, 0:SEQ], logf[:, 0:SEQ], 0.0,
                                         ALU.mult, ALU.add).then_inc(decay_step, 1)
            nc.vector.tensor_tensor_scan(cum[:, SEQ:KEYS], ones[:, SEQ:KEYS], logf[:, SEQ:KEYS], 0.0,
                                         ALU.mult, ALU.add).then_inc(decay_step, 1)
            rest(2, 0)
            dve.wait_ge(decay_step, 2)
            nc.vector.tensor_copy(cum_hi[:], cum[:]).then_inc(decay_step, 1)
            dve.wait_ge(decay_step, 3)
            hi = cum_hi[:].bitcast(F32)
            nc.vector.tensor_tensor(cum_lo[:], cum[:], hi, ALU.subtract).then_inc(decay_step, 1)
            nc.vector.tensor_tensor(neg_lo[:], hi, cum[:], ALU.subtract).then_inc(decay_step, 1)
            nc.vector.tensor_scalar(neg_hi[:], hi, -1.0, None, ALU.mult).then_inc(decay_step, 1)
            dve.wait_ge(decay_step, 6)
            nc.vector.memset(ones[:, 0:1], 1.0).then_inc(decay_step, 1)
            with dve.Fori(plain[0] + 1, plain[1]) as i:
                for j in range(2):
                    rest(2 * i + j + 1, 1 - j)
            dve.wait_ge(tables, 48)
            with dve.Fori(*rope) as i:
                rest(2 * i + 1, 1)
                for half, (table, n0, n1) in enumerate(((0, 0, 2), (1, 1, 3))):
                    dve.wait_ge(multiplied, 2 * i + half + 1)
                    if half == 1:
                        rest(2 * i + 2, 0)
                    for dst, table in (((0, cos), (2, sin)) if half == 0 else ((1, sin), (3, cos))):
                        dve.wait_ge(rotated, 2 * i - NPLAIN)
                        pv = slab_views(psum, at(half), prods[:, dst, :])
                        tv = slab_views(psum, at(half), table[:, :])
                        nc.vector.tensor_tensor(pv[0][1], pv[0][0], tv[0][1], ALU.mult)
                        nc.vector.tensor_tensor(pv[1][1], pv[1][0], tv[1][1], ALU.mult).then_inc(rope_products, 1)
            with dve.Fori(*silu) as i:
                for j in range(2):
                    t = 2 * i + j
                    rest(t + 1, 1 - j)
                    dve.wait_ge(sigmoid, t + 1 - 2 * silu[0])
                    dve.wait_ge(stored[j], 16 * (i + 1))
                    views = slab_views(psum, at(j), stage[:, j, :])
                    tv = slab_views(psum, at(j), tmp[:, j, :])
                    nc.vector.tensor_tensor(views[0][1], views[0][0], tv[0][1], ALU.mult)
                    nc.vector.tensor_tensor(views[1][1], views[1][0], tv[1][1], ALU.mult).then_inc(silued, 1)
            with dve.Fori(sigm[0], sigm[1] - 1) as i:
                for j in range(2):
                    rest(2 * i + j + 1, 1 - j)
            rest(NFEAT - 1, 1)

        @block.tensor
        def _(pe):
            def tile(t, j):
                pe.wait_ge(split, t + 1)
                gemm_tile(nc, psum, at(j), w_hi[:, j], w_lo[:, j], h_hi, h_lo, DC).then_inc(multiplied, 1)
            pe.wait_ge(f_split, 1)
            gemm_tile(nc, psum, at(1), w_hi[:, 1], w_lo[:, 1], h_hi, h_lo, DC).then_inc(f_multiplied, 1)
            tile(0, 0)
            pe.wait_ge(zf_ready, 1)
            tile(1, 1)

            def bodies(start, end, staged, before):
                with pe.Fori(start, end) as i:
                    for j in range(2):
                        pe.wait_ge(staged, 2 * i + j - 1 - before)
                        tile(2 * i + j, j)
            bodies(1, rope[0] + 1, copied, 0)
            with pe.Fori(rope[0] + 1, rope[1] + 1) as i:
                for j in range(2):
                    pe.wait_ge(rope_products, 4 * i - 4 * rope[0] - 2 + 2 * j)
                    tile(2 * i + j, j)
            bodies(silu[0] + 1, silu[1] + 1, silued, NPLAIN + NROPE)
            bodies(sigm[0] + 1, sigm[1], copied, NROPE + NSILU)


def retention(nc, g):
    NV = DV // P
    steps = [(b, j, max(BANK * b, P * j)) for b in range(2) for j in range(4 * b + 4)]
    steps = [(b, j, n0, BANK * (b + 1) - n0) for b, j, n0 in steps] + [(2, TT - 1, SEQ, DEC)]
    NS = len(steps)
    ends = [max(s for s in range(NS) if steps[s][0] == b) for b in range(3)]
    blocks = ((0, BANK), (BANK, BANK), (SEQ, DEC))
    v_order = [TT - 1] + list(range(TT - 1))
    pairs = [list(range(2 * p, min(2 * p + 2, TT))) for p in range((TT + 1) // 2)]
    NPR = len(pairs)
    VR = 3
    LATE = {2: 5, 4: 6, 5: 7, 6: 8}
    with ExitStack() as es:
        sb = lambda n, s, dt=F32: es.enter_context(nc.sbuf_tensor(f"rt_{n}", s, dt))
        sem = semaphores(nc, es, "rt")
        slots = lambda n, k: [sem(f"{n}{j}") for j in range(k)]
        q_raw, k_raw = sb("q_raw", [P, 2, TOKP]), sb("k_raw", [P, 2, TOKP])
        v_raw, s_raw = sb("v_raw", [P, VR, DV]), sb("s_raw", [P, 2, DV])
        q_hi, q_lo = sb("q_hi", [P, 2, TOKP], F32R), sb("q_lo", [P, 2, TOKP], F32R)
        k_hi, k_lo = sb("k_hi", [P, 2, TOKP], F32R), sb("k_lo", [P, 2, TOKP], F32R)
        v_hi, v_lo = sb("v_hi", [P, TT, DV], F32R), sb("v_lo", [P, TT, DV], F32R)
        s_hi, s_lo = sb("s_hi", [P, 2, DV], F32R), sb("s_lo", [P, 2, DV], F32R)
        kt, kt_hi, kt_lo = sb("kt", [P, 2, 2, DK]), sb("kt_hi", [P, TT, DK], F32R), sb("kt_lo", [P, TT, DK], F32R)
        qd, qd_hi, qd_lo = sb("qd", [P, 2, DEC]), sb("qd_hi", [P, 2, DEC], F32R), sb("qd_lo", [P, 2, DEC], F32R)
        w, w_hi, w_lo = sb("w", [P, 2, BANK]), sb("w_hi", [P, 2, BANK], F32R), sb("w_lo", [P, 2, BANK], F32R)
        table, cols, qdec = sb("table", [P, SEQ]), sb("cols", [P, TT + 1 + NV]), sb("qdec", [P, DEC])
        y, sq, new_state = sb("y", [P, NV, TOK]), sb("sq", [P, NV, BANK]), sb("new_state", [P, 2 * DV])
        sums = g.acc
        gain, gate = sb("gain", [P, NV]), sb("gate", [P, NV, TOK])
        ident = sb("ident", [P, P])
        const_loaded, padded = sem("const_loaded"), sem("padded")
        q_loaded, k_loaded, v_loaded = sem("q_loaded"), sem("k_loaded"), slots("v_loaded", VR)
        table_loaded, aux_loaded, gate_loaded = sem("table_loaded"), sem("aux_loaded"), slots("gate_loaded", NV)
        k_rounded, q_rounded, v_rounded, s_rounded = (sem("k_rounded"), sem("q_rounded"), sem("v_rounded"),
                                                      sem("s_rounded"))
        k_split, q_split, v_split, s_split = sem("k_split"), sem("q_split"), sem("v_split"), sem("s_split")
        q_decayed, qd_rounded, qd_split = sem("q_decayed"), sem("qd_rounded"), sem("qd_split")
        transposed, kt_decayed, kt_rounded, kt_split = (sem("transposed"), sem("kt_decayed"), sem("kt_rounded"),
                                                        sem("kt_split"))
        scored, weighted, w_rounded, w_split = sem("scored"), sem("weighted"), sem("w_rounded"), sem("w_split")
        y_step, y_copied, squared, summed = sem("y_step"), sem("y_copied"), sem("squared"), sem("summed")
        state_tile, states_copied, states_summed = sem("state_tile"), sem("states_copied"), sem("states_summed")
        states_stored, total, logged, inverted = sem("states_stored"), sem("total"), sem("logged"), sem("inverted")
        gain_ready, gate_scaled, gated, o_stored = (sem("gain_ready"), sem("gate_scaled"), sem("gated"),
                                                    slots("o_stored", NV))
        psum = g.psum
        bank = lambda b, n=BANK: psum[:, b * BANK:b * BANK + n]
        block = es.enter_context(nc.Block())

        @block.sync
        def _(sp):
            def load_q(i):
                sp.dma_start(q_raw[:, :, 0:TOK], g.qk_ret[bass.ds(2 * i, 2), :, :].rearrange("c p t -> p c t"))\
                    .then_inc(q_loaded, 16)

            def load_k(i):
                sp.dma_start(k_raw[:, :, 0:TOK], g.qk_ret[bass.ds(2 * i + DC, 2), :, :].rearrange("c p t -> p c t"))\
                    .then_inc(k_loaded, 16)

            def load_v(i, m):
                t = v_order[m]
                rows = DEC if t == TT - 1 else P
                row = 0 if t == TT - 1 else DEC + t * P
                sp.dma_start(v_raw[0:rows, m % VR, :], g.v_ret[i, row:row + rows, :]).then_inc(v_loaded[m % VR], 16)

            def load_table(i):
                sp.dma_start(table[:], g.ret_decay[i, :, :]).then_inc(table_loaded, 16)

            def load_aux(i):
                sp.dma_start(cols[:], g.ret_cols[i, :, :]).then_inc(aux_loaded, 16)
                sp.dma_start(qdec[:], g.ret_qdec[i, :, :]).then_inc(aux_loaded, 16)
                sp.dma_start(s_raw[:], g.state_in[i, :, :].rearrange("(c p) n -> p c n", p=P)).then_inc(aux_loaded, 16)

            def load_gate(i, c):
                sp.dma_start(gate[:, c, :], g.gates[NV * i + c, :, :]).then_inc(gate_loaded[c], 16)

            def store_state(i, which):
                sp.dma_start(g.state_out[which, i, :, :].rearrange("(c p) n -> p c n", p=P),
                             new_state[:].rearrange("p (c n) -> p c n", n=DV)).then_inc(states_stored, 16)

            def store_out(i, c):
                sp.wait_ge(gated, NV * i + c + 1)
                sp.dma_start(g.o_ret[NV * i + c, :, :], gate[:, c, :]).then_inc(o_stored[c], 16)

            def head(i, next_i, first=False):
                if not first:
                    for c in range(NV):
                        store_out(i - 1, c)
                if next_i is not None:
                    for m in range(VR):
                        sp.wait_ge(v_split, TT * i + TT - VR + m + 1)
                        load_v(next_i, m)
                if not first:
                    for c in range(NV):
                        sp.wait_ge(o_stored[c], 16 * i)
                        load_gate(i, c)
                if next_i is not None:
                    sp.wait_ge(q_decayed, i + 1)
                    load_q(next_i)
                    sp.wait_ge(transposed, NPR * i + NPR)
                    load_k(next_i)
                    sp.wait_ge(weighted, NS * i + NS)
                    load_table(next_i)
                sp.wait_ge(states_summed, i + 1)
                store_state(i, 0)
                if next_i is not None:
                    sp.wait_ge(gain_ready, i + 1)
                    load_aux(next_i)
                    for m in range(VR, TT):
                        sp.wait_ge(v_split, TT * i + TT + m - VR + 1)
                        load_v(next_i, m)
                sp.wait_ge(states_copied, i + 1)
                store_state(i, 1)

            sp.dma_start(ident[:], g.ident_t).then_inc(const_loaded, 16)
            load_k(0)
            for m in range(VR):
                load_v(0, m)
            load_aux(0)
            for m in range(VR, TT):
                sp.wait_ge(v_split, m - VR + 1)
                load_v(0, m)
            for c in range(NV):
                load_gate(0, c)
            head(0, 1, first=True)
            with sp.Fori(1, HR - 1) as i:
                head(i, i + 1)
            head(HR - 1, None)
            for c in range(NV):
                store_out(HR - 1, c)
            for c in range(NV):
                sp.wait_ge(o_stored[c], 16 * HR)
            sp.wait_ge(states_stored, 32 * HR)

        @block.gpsimd
        def _(pool):
            def rest_k(i):
                pool.wait_ge(k_rounded, i + 1)
                pool.wait_ge(k_split, i)
                nc.gpsimd.tensor_tensor(k_lo[:], k_raw[:], k_hi[:].bitcast(F32), ALU.subtract).then_inc(k_split, 1)

            def head(i, next_i):
                if next_i is not None:
                    rest_k(next_i)
                for c in range(NV):
                    pool.wait_ge(gate_loaded[c], 16 * (i + 1))
                    if c == 0:
                        pool.wait_ge(inverted, i + 1)
                    nc.gpsimd.tensor_tensor(gate[:, c, :], gate[:, c, :], sums[:], ALU.mult)\
                        .then_inc(gate_scaled, 1)
            with pool.Fori(0, HR - 1) as i:
                head(i, i + 1)
            head(HR - 1, None)

        @block.scalar
        def _(act):
            def round_k(i):
                act.wait_ge(k_loaded, 16 * (i + 1))
                nc.scalar.activation(k_hi[:], k_raw[:], ACT.Copy).then_inc(k_rounded, 1)

            def round_q(i):
                act.wait_ge(q_loaded, 16 * (i + 1))
                nc.scalar.activation(q_hi[:], q_raw[:], ACT.Copy).then_inc(q_rounded, 1)

            def round_v(i, m):
                t = v_order[m]
                rows = DEC if t == TT - 1 else P
                act.wait_ge(v_loaded[m % VR], 48 * i + 16 * (m // VR + 1))
                nc.scalar.activation(v_hi[0:rows, t, :], v_raw[0:rows, m % VR, :], ACT.Copy).then_inc(v_rounded, 1)

            def copy_y(i, b):
                n0, n = blocks[b]
                act.wait_ge(y_step, NS * i + ends[b] + 1)
                src = psum[:, 0:NV * BANK] if b < 2 else bank(6, NV * DEC)
                nc.scalar.activation(y[:, :, n0:n0 + n], src.rearrange("p (c n) -> p c n", c=NV),
                                     ACT.Copy).then_inc(y_copied, 1)

            def square(i, b, first):
                n0, n = blocks[b]
                act.wait_ge(y_copied, 3 * i + b + 1)
                if b > 0 or not first:
                    act.wait_ge(summed, 3 * i + b)
                nc.scalar.activation(sq[:, :, 0:n], y[:, :, n0:n0 + n], ACT.Square).then_inc(squared, 1)

            def head(i, next_i, first=False):
                for s, (b, j, n0, n) in enumerate(steps):
                    act.wait_ge(weighted, NS * i + s + 1)
                    if s >= 2:
                        act.wait_ge(y_step, NS * i + s - 1)
                    elif not first:
                        act.wait_ge(y_step, NS * i)
                    nc.scalar.activation(w_hi[:, s % 2, 0:n], w[:, s % 2, 0:n], ACT.Copy).then_inc(w_rounded, 1)
                    if s in LATE:
                        round_v(i, LATE[s])
                    if s % 2 == 1 and s // 2 < NPR:
                        p, tiles = s // 2, pairs[s // 2]
                        act.wait_ge(kt_decayed, TT * i + tiles[-1] + 1)
                        nc.scalar.activation(kt_hi[:, tiles[0]:tiles[-1] + 1, :], kt[:, p % 2, 0:len(tiles), :],
                                             ACT.Copy).then_inc(kt_rounded, 1)
                    if s == ends[0] + 1:
                        if not first:
                            act.wait_ge(gated, NV * i)
                        copy_y(i, 0)
                    if s == ends[0] + 2:
                        square(i, 0, first)
                    if s == 6:
                        act.wait_ge(aux_loaded, 48 * (i + 1))
                        nc.scalar.activation(s_hi[:], s_raw[:], ACT.Copy).then_inc(s_rounded, 1)
                    if s == 8:
                        act.wait_ge(q_decayed, i + 1)
                        nc.scalar.activation(qd_hi[:], qd[:], ACT.Copy).then_inc(qd_rounded, 1)
                copy_y(i, 1)
                copy_y(i, 2)
                square(i, 1, first)
                square(i, 2, first)
                for m in range(TT - len(LATE)):
                    if next_i is not None:
                        if m == 0:
                            act.wait_ge(scored, NS * i + NS)
                            round_k(next_i)
                        act.wait_ge(state_tile, TT * i + m + 1)
                        round_v(next_i, m)
                        if m == 1:
                            round_q(next_i)
                    if m == 4:
                        act.wait_ge(total, i + 1)
                        for src, dst in slab_views(psum, 0, sums):
                            last = nc.scalar.activation(dst, src, ACT.Ln, bias=g.eps[:, 0:1], scale=1.0 / DV)
                        last.then_inc(logged, 1)
                        act.wait_ge(logged, i + 1)
                        nc.scalar.activation(sums[:], sums[:], ACT.Exp, scale=-0.5).then_inc(inverted, 1)
                act.wait_ge(state_tile, TT * i + TT)
                act.wait_ge(states_stored, 32 * i + 16)
                nc.scalar.activation(new_state[:], psum[:, 6 * BANK:8 * BANK], ACT.Copy).then_inc(states_copied, 1)

            act.dma_start(q_raw[:, :, 0:TOK], g.qk_ret[0:2, :, :].rearrange("c p t -> p c t")).then_inc(q_loaded, 16)
            act.dma_start(table[:], g.ret_decay[0, :, :]).then_inc(table_loaded, 16)
            act.wait_ge(padded, 4)
            round_k(0)
            round_q(0)
            for m in range(TT - len(LATE)):
                round_v(0, m)
            head(0, 1, first=True)
            with act.Fori(1, HR - 1) as i:
                head(i, i + 1)
            head(HR - 1, None)

        @block.vector
        def _(dve):
            nc.vector.memset(q_raw[:, :, TOK:TOKP], 0.0).then_inc(padded, 1)
            nc.vector.memset(k_raw[:, :, TOK:TOKP], 0.0).then_inc(padded, 1)
            nc.vector.memset(v_hi[DEC:P, TT - 1, :].bitcast(F32), 0.0).then_inc(padded, 1)
            nc.vector.memset(v_lo[DEC:P, TT - 1, :].bitcast(F32), 0.0).then_inc(padded, 1)

            def rest_q(i):
                dve.wait_ge(q_rounded, i + 1)
                nc.vector.tensor_tensor(q_lo[:], q_raw[:], q_hi[:].bitcast(F32), ALU.subtract).then_inc(q_split, 1)

            def rest_v(i, m):
                t = v_order[m]
                rows = DEC if t == TT - 1 else P
                dve.wait_ge(v_rounded, TT * i + m + 1)
                nc.vector.tensor_tensor(v_lo[0:rows, t, :], v_raw[0:rows, m % VR, :],
                                        v_hi[0:rows, t, :].bitcast(F32), ALU.subtract).then_inc(v_split, 1)

            def rest_kt(i, p):
                tiles = pairs[p]
                dve.wait_ge(kt_rounded, NPR * i + p + 1)
                nc.vector.tensor_tensor(kt_lo[:, tiles[0]:tiles[-1] + 1, :], kt[:, p % 2, 0:len(tiles), :],
                                        kt_hi[:, tiles[0]:tiles[-1] + 1, :].bitcast(F32), ALU.subtract)\
                    .then_inc(kt_split, 1)

            def sum_squares(i, b):
                n0, n = blocks[b]
                dve.wait_ge(squared, 3 * i + b + 1)
                nc.vector.reduce_sum(sums[:, n0:n0 + n], sq[:, :, 0:n].rearrange("p c n -> p n c"), AX)\
                    .then_inc(summed, 1)

            def apply_gate(i, c):
                dve.wait_ge(gate_scaled, NV * i + c + 1)
                nc.vector.scalar_tensor_tensor(gate[:, c, :], y[:, c, :], gain[:, c:c + 1], gate[:, c, :],
                                               ALU.mult, ALU.mult).then_inc(gated, 1)

            def head(i, next_i, first=False):
                dve.wait_ge(table_loaded, 16 * (i + 1))
                dve.wait_ge(aux_loaded, 48 * (i + 1))
                for s, (b, j, n0, n) in enumerate(steps):
                    dve.wait_ge(scored, NS * i + s + 1)
                    if s >= 2 or not first:
                        dve.wait_ge(w_split, NS * i + s - 1)
                    off = n0 - j * P
                    nc.vector.tensor_tensor(w[:, s % 2, 0:n], bank(4 + s % 2, n), table[:, off:off + n], ALU.mult)\
                        .then_inc(weighted, 1)
                    dve.wait_ge(w_rounded, NS * i + s + 1)
                    nc.vector.tensor_tensor(w_lo[:, s % 2, 0:n], w[:, s % 2, 0:n], w_hi[:, s % 2, 0:n].bitcast(F32),
                                            ALU.subtract).then_inc(w_split, 1)
                    if s in LATE:
                        rest_v(i, LATE[s])
                    if s % 2 == 1 and s // 2 < NPR:
                        p = s // 2
                        dve.wait_ge(transposed, NPR * i + p + 1)
                        if p >= 2 or not first:
                            dve.wait_ge(kt_split, NPR * i + p - 1)
                        for m, t in enumerate(pairs[p]):
                            at = (6 + p % 2) * BANK + m * DK
                            nc.vector.tensor_scalar(kt[:, p % 2, m, :], psum[:, at:at + DK], cols[:, t:t + 1], None,
                                                    ALU.mult).then_inc(kt_decayed, 1)
                    if s % 2 == 0 and 0 < s // 2 <= NPR:
                        rest_kt(i, s // 2 - 1)
                    if s < NV and not first:
                        if s == 0:
                            dve.wait_ge(gain_ready, i)
                        apply_gate(i - 1, s)
                    if s == 5:
                        for c in range(2):
                            last = nc.vector.tensor_tensor(qd[:, c, :], q_raw[:, c, SEQ:TOK], qdec[:], ALU.mult)
                        last.then_inc(q_decayed, 1)
                    if s == 7:
                        dve.wait_ge(s_rounded, i + 1)
                        nc.vector.tensor_tensor(s_lo[:], s_raw[:], s_hi[:].bitcast(F32), ALU.subtract)\
                            .then_inc(s_split, 1)
                    if s == 8:
                        sum_squares(i, 0)
                    if s == 9:
                        dve.wait_ge(qd_rounded, i + 1)
                        nc.vector.tensor_tensor(qd_lo[:], qd[:], qd_hi[:].bitcast(F32), ALU.subtract)\
                            .then_inc(qd_split, 1)
                dve.wait_ge(state_tile, TT * i + 1)
                if not first:
                    dve.wait_ge(states_stored, 32 * i)
                nc.vector.scalar_tensor_tensor(new_state[:], s_raw[:].rearrange("p c n -> p (c n)"),
                                               cols[:, TT:TT + 1], psum[:, 4 * BANK:6 * BANK], ALU.mult, ALU.add)\
                    .then_inc(states_summed, 1)
                if not first:
                    dve.wait_ge(gated, NV * i)
                nc.vector.tensor_copy(gain[:], cols[:, TT + 1:TT + 1 + NV]).then_inc(gain_ready, 1)
                sum_squares(i, 1)
                sum_squares(i, 2)
                if next_i is not None:
                    for m in range(TT - len(LATE)):
                        rest_v(next_i, m)
                        if m == 1:
                            rest_q(next_i)

            dve.wait_ge(padded, 4)
            dve.wait_ge(k_rounded, 1)
            nc.vector.tensor_tensor(k_lo[:], k_raw[:], k_hi[:].bitcast(F32), ALU.subtract).then_inc(k_split, 1)
            rest_q(0)
            for m in range(TT - len(LATE)):
                rest_v(0, m)
            head(0, 1, first=True)
            with dve.Fori(1, HR - 1) as i:
                head(i, i + 1)
            head(HR - 1, None)
            dve.wait_ge(gain_ready, HR)
            for c in range(NV):
                apply_gate(HR - 1, c)

        @block.tensor
        def _(pe):
            three = lambda a_hi, a_lo, b_hi, b_lo: ((a_hi, b_hi), (a_hi, b_lo), (a_lo, b_hi))

            def scores(i, s):
                b, j, n0, n = steps[s]
                for c in range(2):
                    for m, (k, q) in enumerate(three(k_hi, k_lo, q_hi, q_lo)):
                        last = nc.tensor.matmul(bank(4 + s % 2, n), k[:, c, j * P:(j + 1) * P], q[:, c, n0:n0 + n],
                                                start=(c == 0 and m == 0), stop=(c == 1 and m == 2))
                last.then_inc(scored, 1)

            def head(i, first=False):
                pe.wait_ge(k_split, i + 1)
                pe.wait_ge(q_split, i + 1)
                if not first:
                    pe.wait_ge(states_summed, i)
                scores(i, 0)
                scores(i, 1)
                for s, (b, j, n0, n) in enumerate(steps):
                    if s + 2 < NS:
                        pe.wait_ge(weighted, NS * i + s + 1)
                        scores(i, s + 2)
                    if s % 2 == 1 and s // 2 < NPR:
                        p = s // 2
                        if p >= 2:
                            pe.wait_ge(kt_decayed, TT * i + 2 * p - 2)
                        elif not first:
                            pe.wait_ge(states_copied, i)
                        for m, t in enumerate(pairs[p]):
                            for c in range(2):
                                at = (6 + p % 2) * BANK + m * DK + c * P
                                last = nc.tensor.transpose(psum[:, at:at + P], k_raw[:, c, t * P:(t + 1) * P], ident[:])
                        last.then_inc(transposed, 1)
                    pe.wait_ge(w_split, NS * i + s + 1)
                    pe.wait_ge(v_split, TT * i + v_order.index(j) + 1)
                    new = s == 0 or s - 1 in ends
                    if new and b == 1:
                        pe.wait_ge(y_copied, 3 * i + 1)
                    elif new and b == 2:
                        pe.wait_ge(kt_decayed, TT * i + TT)
                    elif new and not first:
                        pe.wait_ge(logged, i)
                    if b == 2:
                        pe.wait_ge(s_split, i + 1)
                        pe.wait_ge(qd_split, i + 1)
                    for c in range(NV):
                        at = c * BANK + n0 - b * BANK if b < 2 else 6 * BANK + c * n
                        dst = psum[:, at:at + n]
                        vc = slice(c * P, (c + 1) * P)
                        if b == 2:
                            for kc in range(2):
                                for m, (st, q) in enumerate(three(s_hi, s_lo, qd_hi, qd_lo)):
                                    nc.tensor.matmul(dst, st[:, kc, vc], q[:, kc, :],
                                                     start=(kc == 0 and m == 0), stop=False)
                        for m, (v, x) in enumerate(three(v_hi, v_lo, w_hi, w_lo)):
                            last = nc.tensor.matmul(dst, v[:, j, vc], x[:, s % 2, 0:n],
                                                    start=(new and b < 2 and m == 0), stop=(s in ends and m == 2))
                    last.then_inc(y_step, 1)
                pe.wait_ge(kt_split, NPR * i + NPR)
                for n, t in enumerate(v_order):
                    sample = t == TT - 1
                    if n == 1:
                        pe.wait_ge(y_copied, 3 * i + 3)
                    for c in range(2):
                        for m, (k, v) in enumerate(three(kt_hi, kt_lo, v_hi, v_lo)):
                            last = nc.tensor.matmul(bank((4 if sample else 6) + c), k[:, t, c * P:(c + 1) * P],
                                                    v[:, t, :], start=(m == 0 and (sample or t == 0)),
                                                    stop=(m == 2 and t >= TT - 2))
                    last.then_inc(state_tile, 1)
                    if n == 4:
                        pe.wait_ge(summed, 3 * i + 3)
                        for sl, (t0, width) in enumerate(SLABS):
                            last = nc.tensor.matmul(bank(sl, width), g.ones[:, :],
                                                    sums[:, t0:t0 + width], start=True, stop=True)
                        last.then_inc(total, 1)
            pe.wait_ge(const_loaded, 16)
            head(0, first=True)
            with pe.Fori(1, HR) as i:
                head(i)


def fox(nc, g):
    UH = TT
    U = 2 * UH
    order = [4, 5, 6, 7, 3, 2, 8, 1, 0]
    units = [(j, u, (0 if u < UH - 1 else UH - 1), (u + 1 if u < UH - 1 else KT - UH + 1))
             for j in range(2) for u in order]
    groups = [(n, t0, min(4, kt - t0)) for n, (_, _, _, kt) in enumerate(units) for t0 in range(0, kt, 4)]
    NG = len(groups)
    last_group = [max(x for x, q in enumerate(groups) if q[0] == n) for n in range(U)]
    block_of = lambda u: (1 if u < 4 else 0) if u < UH - 1 else 2
    NB = 3
    q0_of, nq_of = (BANK, 0, SEQ), (BANK, BANK, DEC)
    out_bank = (6, 7, 6)
    before = (0, -1, 1)
    products = [(UH * j + n, j, x, a, b) for j in range(2)
                for n, x, a, b in ((4, 0, 0, 3), (5, 0, 3, 6), (6, 0, 6, 8), (9, 1, 0, 4), (10, 2, 0, 3))]
    takes = [(UH * j + n, j, x) for j in range(2) for n, x in ((7, 0), (10, 1), (11, 2))]
    with ExitStack() as es:
        sb = lambda n, s, dt=F32: es.enter_context(nc.sbuf_tensor(f"fx_{n}", s, dt))
        sem = semaphores(nc, es, "fx")
        two = lambda n: [sem(f"{n}{j}") for j in range(2)]
        k_raw, q_raw, v_raw = sb("k_raw", [P, 2, KEYS]), sb("q_raw", [P, 2, TOKP]), sb("v_raw", [P, 2, KT, DF])
        q_a, q_b = sb("q_a", [P, 2, TOKP], F32R), sb("q_b", [DF + 4, 2, TOKP], F32R)
        k_a, k_b = sb("k_a", [P, 2, KEYS], F32R), sb("k_b", [DF + 4, 2, KEYS], F32R)
        v_a = sb("v_a", [P, 2, KT, 2 * DF], F32R)
        e = sb("e", [P, 2, SEQ])
        pb = lambda part: (sb(f"{part}0", [P, 8, BANK], F32R), sb(f"{part}1", [P, 4, BANK], F32R),
                           sb(f"{part}2", [P, 3, P], F32R))
        p_hi, p_lo = pb("p_hi"), pb("p_lo")
        neg_max, rowsum, inv = sb("neg_max", [P, U]), sb("rowsum", [P, U]), sb("inv", [P, U])
        o_low, o_t = sb("o_low", [DF, 2, BANK]), sb("o_t", [DF, 2, TOK])
        ident, masks = sb("ident", [P, P]), sb("masks", [P, 2, P])
        ident_r, masks_r = sb("ident_r", [P, P], F32R), sb("masks_r", [P, 2, P], F32R)
        raw_loaded, rows_loaded = two("raw_loaded"), two("rows_loaded")
        const_loaded, const_ready, padded = sem("const_loaded"), sem("const_ready"), sem("padded")
        rounded, split = sem("rounded"), sem("split")
        scored, maxed, exped, inverted, scaled = (sem("scored"), sem("maxed"), sem("exped"), sem("inverted"),
                                                  sem("scaled"))
        transposed, p_rounded, p_split = sem("transposed"), sem("p_rounded"), sem("p_split")
        multiplied, o_lowered, o_added, o_stored = sem("multiplied"), sem("o_lowered"), sem("o_added"), two("o_stored")
        psum = g.psum
        block = es.enter_context(nc.Block())
        PAIRS = HF // 2

        def tiles_of(p, n, t0, nt):
            u = units[n][1]
            x = block_of(u)
            q = u * P - q0_of[x]
            return p[x][:, t0:t0 + nt, q:q + P]

        def load_half(engine, i, j, half):
            own, rows = slice(half * DF, (half + 1) * DF), slice(j * DF, (j + 1) * DF)
            engine.dma_start(k_raw[own, j, 0:SEQ], g.qk_out[i + DC, rows, 0:SEQ]).then_inc(raw_loaded[j], 16)
            engine.dma_start(k_raw[own, j, SEQ:SEQ + PAST], g.cache_kt[2 * i + j, :, :]).then_inc(raw_loaded[j], 16)
            engine.dma_start(k_raw[own, j, SEQ + PAST:SEQ + PAST + DEC], g.qk_out[i + DC, rows, SEQ:TOK])\
                .then_inc(raw_loaded[j], 16)
            engine.dma_start(q_raw[own, j, 0:TOK], g.qk_out[i, rows, :]).then_inc(raw_loaded[j], 16)

        @block.sync
        def _(sp):
            def load_raw(i, j, halves=(0, 1)):
                for half in halves:
                    load_half(sp, i, j, half)
                cols = bass.ds(i * P + j * DF, DF)
                sp.dma_start(v_raw[:, j, 0:8, :], g.v_out[0:SEQ, cols].rearrange("(t p) n -> p t n", p=P))\
                    .then_inc(raw_loaded[j], 16)
                sp.dma_start(v_raw[:, j, 8:10, :], g.cache_v[:, cols].rearrange("(t p) n -> p t n", p=P))\
                    .then_inc(raw_loaded[j], 16)
                sp.dma_start(v_raw[0:DEC, j, 10, :], g.v_out[SEQ:TOK, cols]).then_inc(raw_loaded[j], 16)

            def load_rows(i, j):
                sp.dma_start(q_b[DF:DF + 4, j, 0:TOK].bitcast(F32), g.q_rows[2 * i + j, :, :])\
                    .then_inc(rows_loaded[j], 16)
                sp.dma_start(k_b[DF:DF + 4, j, :].bitcast(F32), g.k_rows[2 * i + j, :, :]).then_inc(rows_loaded[j], 16)

            def store(i, j):
                sp.wait_ge(o_added, NB * (2 * i + j) + NB)
                sp.dma_start(g.o_fox[i, j * DF:(j + 1) * DF, :], o_t[:, j, :]).then_inc(o_stored[j], 16)

            def pair(i, next_i, first=False):
                if not first:
                    sp.wait_ge(scored, U * i)
                load_rows(i, 1)
                if next_i is not None:
                    sp.wait_ge(split, 6 * i + 3)
                    load_raw(next_i, 0)
                if not first:
                    store(i - 1, 1)
                if next_i is not None:
                    sp.wait_ge(split, 6 * i + 6)
                    load_raw(next_i, 1)
                    sp.wait_ge(scored, U * i + UH)
                    load_rows(next_i, 0)
                store(i, 0)
            load_raw(0, 0, halves=(0,))
            sp.wait_ge(padded, 4)
            load_rows(0, 0)
            sp.dma_start(ident[:], g.ident_t).then_inc(const_loaded, 16)
            sp.dma_start(masks[:], g.masks).then_inc(const_loaded, 16)
            load_raw(0, 1)
            for j in range(2):
                sp.sem_inc(o_stored[j], 16)
            pair(0, 1, first=True)
            with sp.Fori(1, PAIRS - 1) as i:
                pair(i, i + 1)
            pair(PAIRS - 1, None)
            store(PAIRS - 1, 1)
            for j in range(2):
                sp.wait_ge(o_stored[j], 16 * PAIRS + 16)

        @block.gpsimd
        def _(pool):
            def split_head(i, j):
                n = 8 * i + 4 * j
                pool.wait_ge(rounded, n + 1)
                nc.gpsimd.tensor_tensor(k_b[0:DF, j, :], k_raw[0:DF, j, :], k_a[0:DF, j, :].bitcast(F32),
                                        ALU.subtract).then_inc(split, 1)
                pool.wait_ge(rounded, n + 3)
                pool.wait_ge(split, 6 * i + 3 * j + 1)
                nc.gpsimd.tensor_tensor(q_a[DF:P, j, :], q_raw[DF:P, j, :], q_a[DF:P, j, :].bitcast(F32),
                                        ALU.subtract).then_inc(split, 1)
                pool.wait_ge(rounded, n + 4)
                pool.wait_ge(split, 6 * i + 3 * j + 2)
                nc.gpsimd.tensor_tensor(v_a[:, j, :, DF:P], v_raw[:, j, :, :], v_a[:, j, :, 0:DF].bitcast(F32),
                                        ALU.subtract).then_inc(split, 1)
            pool.wait_ge(split, 3)
            split_head(0, 1)
            with pool.Fori(1, PAIRS) as i:
                for j in range(2):
                    split_head(i, j)

        @block.scalar
        def _(act):
            load_half(act, 0, 0, 1)
            act.wait_ge(padded, 4)

            def round_part(i, j, part):
                if part == 0:
                    act.wait_ge(raw_loaded[j], 11 * 16 * (i + 1))
                    nc.scalar.activation(k_a[:, j, :], k_raw[:, j, :], ACT.Copy).then_inc(rounded, 1)
                elif part == 1:
                    nc.scalar.activation(q_a[:, j, :], q_raw[:, j, :], ACT.Copy).then_inc(rounded, 1)
                elif part == 2:
                    nc.scalar.activation(q_b[0:DF, j, :], q_raw[0:DF, j, :], ACT.Copy).then_inc(rounded, 1)
                else:
                    nc.scalar.activation(v_a[:, j, :, 0:DF], v_raw[:, j, :, :], ACT.Copy).then_inc(rounded, 1)

            def exp(i, n, first):
                j, u, k0, kt = units[n]
                act.wait_ge(maxed, U * i + n + 1)
                if n >= 2:
                    act.wait_ge(transposed, NG * i + last_group[n - 2] + 1)
                elif not first:
                    act.wait_ge(transposed, NG * i - NG + last_group[n - 2 + U] + 1)
                s0 = (n % 2) * 2 * BANK
                nc.scalar.activation(e[:, n % 2, 0:kt * P], psum[:, s0:s0 + kt * P], ACT.Exp,
                                     bias=neg_max[:, n:n + 1], accum_out=rowsum[:, n:n + 1]).then_inc(exped, 1)

            def lower(i, j, x, first=False):
                nq, h3 = nq_of[x], NB * (2 * i + j)
                act.wait_ge(multiplied, h3 + x + 1)
                if not (first and j == 0 and x < 2):
                    act.wait_ge(o_added, h3 + before[x])
                at = out_bank[x] * BANK
                nc.scalar.activation(o_low[:, out_bank[x] % 2, 0:nq], psum[DF:P, at:at + nq],
                                     ACT.Copy).then_inc(o_lowered, 1)

            def pair(i, next_i, first=False):
                for n in range(U):
                    if n + 1 < U:
                        exp(i, n + 1, first)
                    elif next_i is not None:
                        exp(next_i, 0, False)
                    for step, j, x in takes:
                        if step == n:
                            lower(i, j, x, first)
                        elif step == n + U and not first:
                            lower(i - 1, j, x)
                    for x, (m, t0, nt) in enumerate(groups):
                        if m == n:
                            h3 = NB * (2 * i + n // UH)
                            act.wait_ge(transposed, NG * i + x + 1)
                            if n >= UH or not first:
                                act.wait_ge(multiplied, h3 - 2 if n % UH < 4 else h3)
                            at = (4 + x % 2) * BANK
                            nc.scalar.activation(tiles_of(p_hi, n, t0, nt),
                                                 psum[:, at:at + nt * P].rearrange("p (t n) -> p t n", n=P),
                                                 ACT.Copy).then_inc(p_rounded, 1)
                    if 1 <= n <= 4:
                        if n == 1 and not first:
                            act.wait_ge(multiplied, 2 * NB * i)
                        round_part(i, 1, n - 1)
                    if UH + 1 <= n <= UH + 4 and next_i is not None:
                        if n == UH + 1:
                            act.wait_ge(multiplied, 2 * NB * i + NB)
                        round_part(next_i, 0, n - UH - 1)
            for part in range(4):
                round_part(0, 0, part)
            act.wait_ge(const_loaded, 32)
            nc.scalar.activation(ident_r[:], ident[:], ACT.Copy).then_inc(const_ready, 1)
            nc.scalar.activation(masks_r[:], masks[:], ACT.Copy).then_inc(const_ready, 1)
            exp(0, 0, True)
            pair(0, 1, first=True)
            with act.Fori(1, PAIRS - 1) as i:
                pair(i, i + 1)
            pair(PAIRS - 1, None)
            for step, j, x in takes:
                if step >= U:
                    lower(PAIRS - 1, j, x)

        @block.vector
        def _(dve):
            nc.vector.memset(k_raw[:, :, SEQ + PAST + DEC:KEYS], 0.0).then_inc(padded, 1)
            nc.vector.memset(q_raw[:, :, TOK:TOKP], 0.0).then_inc(padded, 1)
            nc.vector.memset(v_raw[DEC:P, :, 10, :], 0.0).then_inc(padded, 1)
            nc.vector.memset(q_b[DF:DF + 4, :, TOK:TOKP].bitcast(F32), 0.0).then_inc(padded, 1)
            dve.wait_ge(padded, 4)

            def row_max(i, n):
                j, u, k0, kt = units[n]
                dve.wait_ge(scored, U * i + n + 1)
                s0 = (n % 2) * 2 * BANK
                nc.vector.reduce_max(neg_max[:, n:n + 1], psum[:, s0:s0 + kt * P], AX, negate=True).then_inc(maxed, 1)

            def scale(i, n):
                kt = units[n][3]
                dve.wait_ge(exped, U * i + n + 1)
                nc.vector.reciprocal(inv[:, n:n + 1], rowsum[:, n:n + 1]).then_inc(inverted, 1)
                dve.wait_ge(inverted, U * i + n + 1)
                nc.vector.tensor_scalar(e[:, n % 2, 0:kt * P], e[:, n % 2, 0:kt * P], inv[:, n:n + 1], None,
                                        ALU.mult).then_inc(scaled, 1)

            def add(i, j, x):
                q0, nq, at = q0_of[x], nq_of[x], out_bank[x] * BANK
                dve.wait_ge(o_lowered, NB * (2 * i + j) + x + 1)
                if x == 0:
                    dve.wait_ge(o_stored[j], 16 * i + 16)
                nc.vector.tensor_tensor(o_t[:, j, q0:q0 + nq], psum[0:DF, at:at + nq],
                                        o_low[:, out_bank[x] % 2, 0:nq], ALU.add).then_inc(o_added, 1)

            def pair(i, next_i, first=False):
                for n in range(U):
                    if n + 2 < U:
                        row_max(i, n + 2)
                    elif next_i is not None:
                        row_max(next_i, n + 2 - U)
                    if n + 1 < U:
                        scale(i, n + 1)
                    elif next_i is not None:
                        scale(next_i, 0)
                    for step, j, x in takes:
                        if step == n:
                            add(i, j, x)
                        elif step == n + U and not first:
                            add(i - 1, j, x)
                    for x, (m, t0, nt) in enumerate(groups):
                        if m == n:
                            dve.wait_ge(p_rounded, NG * i + x + 1)
                            at = (4 + x % 2) * BANK
                            nc.vector.tensor_tensor(tiles_of(p_lo, n, t0, nt),
                                                    psum[:, at:at + nt * P].rearrange("p (t n) -> p t n", n=P),
                                                    tiles_of(p_hi, n, t0, nt).bitcast(F32),
                                                    ALU.subtract).then_inc(p_split, 1)
            first_head = ((1, k_b[0:DF, 0, :], k_raw[0:DF, 0, :], k_a[0:DF, 0, :]),
                          (3, q_a[DF:P, 0, :], q_raw[DF:P, 0, :], q_a[DF:P, 0, :]),
                          (4, v_a[:, 0, :, DF:P], v_raw[:, 0, :, :], v_a[:, 0, :, 0:DF]))
            for nth, lo, raw, hi in first_head:
                dve.wait_ge(rounded, nth)
                nc.vector.tensor_tensor(lo, raw, hi.bitcast(F32), ALU.subtract).then_inc(split, 1)
            row_max(0, 0)
            row_max(0, 1)
            scale(0, 0)
            pair(0, 1, first=True)
            with dve.Fori(1, PAIRS - 1) as i:
                pair(i, i + 1)
            pair(PAIRS - 1, None)
            for step, j, x in takes:
                if step >= U:
                    add(PAIRS - 1, j, x)

        @block.tensor
        def _(pe):
            pe.wait_ge(const_ready, 2)

            def score(i, n):
                j, u, k0, kt = units[n]
                if n % UH == 0:
                    pe.wait_ge(split, 6 * i + 3 * j + 2)
                    pe.wait_ge(rows_loaded[j], 32 * i + 32)
                q = slice(u * P, (u + 1) * P)
                s0 = (n % 2) * 2 * BANK
                for t in range(0, kt, 4):
                    nt = min(4, kt - t)
                    out = psum[:, s0 + t * P:s0 + (t + nt) * P]
                    keys = slice((k0 + t) * P, (k0 + t + nt) * P)
                    masked = t + nt == kt
                    nc.tensor.matmul(out, q_a[:, j, q], k_a[:, j, keys], start=True, stop=False)
                    last = nc.tensor.matmul(out, q_b[:, j, q], k_b[:, j, keys], start=False, stop=not masked)
                    if masked:
                        last = nc.tensor.matmul(psum[:, s0 + (kt - 1) * P:s0 + kt * P], ident_r[:],
                                                masks_r[:, 0 if u < UH - 1 else 1, :], start=False, stop=True)
                last.then_inc(scored, 1)

            def transpose(i, n, first):
                pe.wait_ge(scaled, U * i + n + 1)
                for x, (m, t0, nt) in enumerate(groups):
                    if m == n:
                        if x >= 2 or not first:
                            pe.wait_ge(p_split, NG * i + x - 1)
                        for t in range(nt):
                            at = (4 + x % 2) * BANK + t * P
                            last = nc.tensor.transpose(psum[:, at:at + P], e[:, n % 2, (t0 + t) * P:(t0 + t + 1) * P],
                                                       ident[:])
                        last.then_inc(transposed, 1)

            def values(i, j, x, a, b, first=False):
                h3, at, nq = NB * (2 * i + j), out_bank[x] * BANK, nq_of[x]
                k0, end = (UH - 1, 3) if x == 2 else (0, 4 if x == 1 else 8)
                if a == 0:
                    last_unit = UH * j + (3 if x == 0 else UH - 1)
                    pe.wait_ge(p_split, NG * i + last_group[last_unit] + 1)
                    pe.wait_ge(split, 6 * i + 3 * j + 3)
                    if not (first and j == 0 and x < 2):
                        pe.wait_ge(o_added, h3 + before[x])
                for t in range(a, b):
                    q = 0 if x == 2 else max(0, t * P - q0_of[x])
                    for m, p in enumerate((p_hi, p_lo)):
                        last = nc.tensor.matmul(psum[:, at + q:at + nq], v_a[:, j, k0 + t, :], p[x][:, t, q:nq],
                                                start=(t == 0 and m == 0), stop=(t == end - 1 and m == 1))
                if b == end:
                    last.then_inc(multiplied, 1)

            def pair(i, next_i, first=False):
                for n in range(U):
                    pe.wait_ge(exped, U * i + n + 1)
                    if n + 2 < U:
                        score(i, n + 2)
                    elif next_i is not None:
                        score(next_i, n + 2 - U)
                    transpose(i, n, first)
                    for step, j, x, a, b in products:
                        if step == n:
                            values(i, j, x, a, b, first)
                        elif step == n + U and not first:
                            values(i - 1, j, x, a, b)
            score(0, 0)
            score(0, 1)
            pair(0, 1, first=True)
            with pe.Fori(1, PAIRS - 1) as i:
                pair(i, i + 1)
            pair(PAIRS - 1, None)
            for step, j, x, a, b in products:
                if step >= U:
                    values(PAIRS - 1, j, x, a, b)


def merge(nc, g, x1):
    GA, GB = NSILU, NSILU + DC
    ROUNDS, XR = 4, 4
    gate_of = {0: 0, 2: 1, 3: 2}
    with ExitStack() as es:
        sb = lambda n, s, dt=F32: es.enter_context(nc.sbuf_tensor(f"mg_{n}", s, dt))
        sem = semaphores(nc, es, "mg")
        slots = lambda n, k=2: [sem(f"{n}{j}") for j in range(k)]
        x_hi, x_lo = sb("x_hi", [P, DC, TOK], F32R), sb("x_lo", [P, DC, TOK], F32R)
        x_raw, merged = sb("x_raw", [P, XR, TOK]), sb("merged", [P, DC, TOK])
        raw, w_hi, w_lo = sb("raw", [P, 2, DC, P]), sb("w_hi", [P, 2, DC, P], F32R), sb("w_lo", [P, 2, DC, P], F32R)
        gate = sb("gate", [P, 2, TOK])
        part_a = x1
        loaded, x_loaded, gate_loaded = slots("loaded"), slots("x_loaded", XR), slots("gate_loaded")
        rounded, split, x_rounded, x_split = sem("rounded"), sem("split"), sem("x_rounded"), sem("x_split")
        x_used, evicted, step = sem("x_used"), sem("evicted"), sem("step")
        squared, summed = sem("squared"), sem("summed")
        sq = x_raw[:, 0, :]
        psum = g.psum
        block = es.enter_context(nc.Block())

        @block.sync
        def _(sp):
            def load(t, slot, splits):
                if splits is not None:
                    sp.wait_ge(split, splits)
                sp.dma_start(raw[:, slot].rearrange("p c n -> p (c n)"), g.w_merge[t, :, :]).then_inc(loaded[slot], 16)

            def load_gate(r, k, slot, evicts):
                if evicts is not None:
                    sp.wait_ge(evicted, evicts)
                src = (g.gates[GA + k, :, :] if r == 0 else g.gates[GB + k, :, :] if r == 2
                       else g.x_c[k, :, :])
                sp.dma_start(gate[:, slot, :], src).then_inc(gate_loaded[slot], 16)

            def load_x(r, c):
                if r > 0 or c >= XR:
                    sp.wait_ge(x_split, DC * r + c - XR + 1)
                src = g.o_fox[c, :, :] if r == 0 else g.o_ret[DC * (r - 1) + c, :, :]
                sp.dma_start(x_raw[:, c % XR, :], src).then_inc(x_loaded[c % XR], 16)

            load(0, 0, None)
            for c in range(DC):
                load_x(0, c)
            load(1, 1, None)
            for r in range(ROUNDS):
                gated, t0 = r in gate_of, DC * r
                if gated:
                    for k in range(2):
                        load_gate(r, k, k, t0 + k - 1 if r > 0 else None)
                with sp.Fori(0, 3) as i:
                    for j in range(2):
                        load(t0 + 2 * i + j + 2, j, t0 + 2 * i + j + 1)
                        if gated:
                            load_gate(r, 2 * i + j + 2, j, t0 + 2 * i + j + 1)
                if r + 1 < ROUNDS:
                    for c in range(DC if r + 1 < ROUNDS - 1 else 0):
                        if c == XR:
                            load(t0 + DC, 0, t0 + DC - 1)
                        load_x(r + 1, c)
                    if r + 1 == ROUNDS - 1:
                        load(t0 + DC, 0, t0 + DC - 1)
                    load(t0 + DC + 1, 1, t0 + DC)

        @block.scalar
        def _(act):
            def round_w(t, slot, nth):
                act.wait_ge(loaded[slot], 16 * (nth + 1))
                nc.scalar.activation(w_hi[:, slot], raw[:, slot], ACT.Copy).then_inc(rounded, 1)

            def round_x(r, c):
                if r > 0:
                    act.wait_ge(x_used, DC * (DC * r - 1) + c + 1)
                if r < ROUNDS - 1:
                    act.wait_ge(x_loaded[c % XR], 16 * (DC // XR * r + c // XR + 1))
                else:
                    act.wait_ge(evicted, DC * (r - 1) + c + 1)
                nc.scalar.activation(x_hi[:, c, :], x_raw[:, c % XR, :] if r < ROUNDS - 1 else merged[:, c, :],
                                     ACT.Copy).then_inc(x_rounded, 1)

            def square(k):
                act.wait_ge(evicted, DC * (ROUNDS - 1) + k + 1)
                act.wait_ge(summed, k + 1)
                nc.scalar.activation(sq, x1[:, bass.ds(k, 1), :].rearrange("p o t -> p (o t)"), ACT.Square)\
                    .then_inc(squared, 1)

            round_w(0, 0, 0)
            for c in range(DC):
                round_x(0, c)
            round_w(1, 1, 0)
            for r in range(ROUNDS):
                with act.Fori(0, 3) as i:
                    for j in range(2):
                        act.wait_ge(x_used, DC * (DC * r + 2 * i + j + 1))
                        round_w(DC * r + 2 * i + j + 2, j, DC // 2 * r + i + 1)
                        if r == ROUNDS - 1:
                            square(2 * i + j)
                if r + 1 < ROUNDS:
                    act.wait_ge(x_used, DC * (DC * r + DC - 1))
                    round_w(DC * r + DC, 0, DC // 2 * (r + 1))
                    for c in range(DC):
                        round_x(r + 1, c)
                    act.wait_ge(x_used, DC * (DC * r + DC))
                    round_w(DC * r + DC + 1, 1, DC // 2 * (r + 1))
            square(DC - 2)
            square(DC - 1)

        @block.vector
        def _(dve):
            def rest_w(t, slot):
                dve.wait_ge(rounded, t + 1)
                nc.vector.tensor_tensor(w_lo[:, slot], raw[:, slot], w_hi[:, slot].bitcast(F32),
                                        ALU.subtract).then_inc(split, 1)

            def rest_x(r, c):
                dve.wait_ge(x_rounded, DC * r + c + 1)
                nc.vector.tensor_tensor(x_lo[:, c, :], x_raw[:, c % XR, :] if r < ROUNDS - 1 else merged[:, c, :],
                                        x_hi[:, c, :].bitcast(F32), ALU.subtract).then_inc(x_split, 1)

            def evict(r, k, j, half):
                dve.wait_ge(x_used, DC * (DC * r + k + 1))
                if r in gate_of:
                    dve.wait_ge(gate_loaded[j], 16 * (DC // 2 * gate_of[r] + half + 1))
                out = (part_a if r in (0, 3) else merged)
                own = lambda x: x[:, bass.ds(k, 1), :].rearrange("p o t -> p (o t)")
                for (p, o), (_, x) in zip(slab_views(psum, 3 * j, own(out)), slab_views(psum, 0, gate[:, j, :])):
                    if r == 1:
                        last = nc.vector.tensor_copy(o, p)
                    elif r in (0, 3):
                        last = nc.vector.tensor_tensor(o, p, x, ALU.mult if r == 0 else ALU.add)
                    else:
                        last = nc.vector.tensor_tensor(o, p, o, ALU.add)
                if r == 2:
                    last.then_inc(step, 1)
                    dve.wait_ge(step, 2 * k + 1)
                    nc.vector.tensor_tensor(own(out), own(out), gate[:, j, :], ALU.mult).then_inc(step, 1)
                    dve.wait_ge(step, 2 * k + 2)
                    last = nc.vector.tensor_tensor(own(out), own(out), own(part_a), ALU.add)
                last.then_inc(evicted, 1)

            def add_squares(k):
                dve.wait_ge(squared, k + 1)
                nc.vector.tensor_tensor(g.acc[:], g.acc[:], sq, ALU.add).then_inc(summed, 1)

            nc.vector.memset(g.acc[:], 0.0).then_inc(summed, 1)
            dve.wait_ge(summed, 1)
            rest_w(0, 0)
            for c in range(DC):
                rest_x(0, c)
            rest_w(1, 1)
            for r in range(ROUNDS):
                with dve.Fori(0, 3) as i:
                    for j in range(2):
                        evict(r, 2 * i + j, j, i)
                        rest_w(DC * r + 2 * i + j + 2, j)
                        if r == ROUNDS - 1:
                            add_squares(2 * i + j)
                evict(r, DC - 2, 0, 3)
                if r + 1 < ROUNDS:
                    rest_w(DC * r + DC, 0)
                    for c in range(DC - 1):
                        rest_x(r + 1, c)
                    if r + 1 < ROUNDS - 1:
                        rest_x(r + 1, DC - 1)
                evict(r, DC - 1, 1, 3)
                if r + 1 == ROUNDS - 1:
                    rest_x(r + 1, DC - 1)
                if r + 1 < ROUNDS:
                    rest_w(DC * r + DC + 1, 1)
            add_squares(DC - 2)
            dve.wait_ge(summed, DC)
            add_squares(DC - 1)

        @block.tensor
        def _(pe):
            def tile(r, k, j, first=False):
                pe.wait_ge(split, DC * r + k + 1)
                if not first:
                    pe.wait_ge(evicted, DC * r + k - 1)
                for c in range(DC):
                    pe.wait_ge(x_split, DC * r + c + 1)
                    for n, (w, x) in enumerate(((w_hi, x_hi), (w_hi, x_lo), (w_lo, x_hi))):
                        for s, (t0, width) in enumerate(SLABS):
                            at = (3 * j + s) * BANK
                            last = nc.tensor.matmul(psum[:, at:at + width], w[:, j, c, :], x[:, c, t0:t0 + width],
                                                    start=(c == 0 and n == 0), stop=(c == DC - 1 and n == 2))
                    last.then_inc(x_used, 1)
            tile(0, 0, 0, first=True)
            tile(0, 1, 1, first=True)
            for r in range(ROUNDS):
                with pe.Fori(1 if r == 0 else 0, DC // 2) as i:
                    for j in range(2):
                        tile(r, 2 * i + j, j)


def mlp(nc, g, x1, h_hi, h_lo, raw, w_hi, w_lo):
    GROUPS = DFF // D
    NT = 2 * DC
    with ExitStack() as es:
        sb = lambda n, s, dt=F32: es.enter_context(nc.sbuf_tensor(f"ml_{n}", s, dt))
        sem = semaphores(nc, es, "ml")
        u_hi, u_lo = sb("u_hi", [P, DC, TOK], F32R), sb("u_lo", [P, DC, TOK], F32R)
        relu = sb("relu", [P, TOK])
        loaded, rounded, split, multiplied = sem("loaded"), sem("rounded"), sem("split"), sem("multiplied")
        relued, squared, u_rounded, u_split, added = (sem("relued"), sem("squared"), sem("u_rounded"),
                                                      sem("u_split"), sem("added"))
        norm_squared, norm_summed = sem("norm_squared"), sem("norm_summed")
        sq = relu
        psum = g.psum
        block = es.enter_context(nc.Block())

        @block.sync
        def _(sp):
            def group(i, first):
                for k in range(first, NT):
                    src = g.w_up[DC * i + k, :, :] if k < DC else g.w_down[DC * i + k - DC, :, :]
                    sp.wait_ge(split, NT * i + k)
                    sp.dma_start(raw[:].rearrange("p c n -> p (c n)"), src).then_inc(loaded, 16)
            sp.sem_inc(loaded, 16)
            group(0, 1)
            with sp.Fori(1, GROUPS) as i:
                group(i, 0)

        @block.scalar
        def _(act):
            def round_tile(i, k):
                act.wait_ge(loaded, 16 * (NT * i + k + 1))
                nc.scalar.activation(w_hi[:, k % 2], raw[:], ACT.Copy).then_inc(rounded, 1)

            def group(i, next_i):
                for k in range(NT):
                    if k + 1 < NT or next_i is not None:
                        act.wait_ge(multiplied, NT * i + k)
                        if k + 1 < NT:
                            round_tile(i, k + 1)
                        else:
                            round_tile(next_i, 0)
                    if k < DC:
                        act.wait_ge(squared, DC * i + k + 1)
                        nc.scalar.activation(u_hi[:, k, :], relu[:], ACT.Copy).then_inc(u_rounded, 1)
                    elif next_i is None:
                        act.wait_ge(added, DC * i + k - DC + 1)
                        act.wait_ge(norm_summed, k - DC + 1)
                        nc.scalar.activation(sq[:], x1[:, k - DC, :], ACT.Square).then_inc(norm_squared, 1)
            act.sem_inc(rounded, 1)
            with act.Fori(0, GROUPS - 1) as i:
                group(i, i + 1)
            group(GROUPS - 1, None)

        @block.vector
        def _(dve):
            def rest(i, k):
                dve.wait_ge(rounded, NT * i + k + 1)
                nc.vector.tensor_tensor(w_lo[:, k % 2], raw[:], w_hi[:, k % 2].bitcast(F32), ALU.subtract)\
                    .then_inc(split, 1)

            def group(i, next_i):
                for k in range(NT):
                    if k + 1 < NT:
                        rest(i, k + 1)
                    elif next_i is not None:
                        rest(next_i, 0)
                    dve.wait_ge(multiplied, NT * i + k + 1)
                    if k < DC:
                        for src, dst in slab_views(psum, 3 * (k % 2), relu):
                            last = nc.vector.tensor_scalar(dst, src, 0.0, None, ALU.max)
                        last.then_inc(relued, 1)
                        dve.wait_ge(relued, DC * i + k + 1)
                        nc.vector.tensor_tensor(relu[:], relu[:], relu[:], ALU.mult).then_inc(squared, 1)
                        dve.wait_ge(u_rounded, DC * i + k + 1)
                        nc.vector.tensor_tensor(u_lo[:, k, :], relu[:], u_hi[:, k, :].bitcast(F32), ALU.subtract)\
                            .then_inc(u_split, 1)
                        dve.wait_ge(u_split, DC * i + k + 1)
                    else:
                        for src, dst in slab_views(psum, 3 * (k % 2), x1[:, k - DC, :]):
                            last = nc.vector.tensor_tensor(dst, src, dst, ALU.add)
                        last.then_inc(added, 1)
                        if next_i is None:
                            dve.wait_ge(norm_squared, k - DC + 1)
                            dve.wait_ge(norm_summed, k - DC + 1)
                            nc.vector.tensor_tensor(g.acc[:], g.acc[:], sq[:], ALU.add).then_inc(norm_summed, 1)
            nc.vector.memset(g.acc[:], 0.0).then_inc(norm_summed, 1)
            dve.sem_inc(split, 1)
            with dve.Fori(0, GROUPS - 1) as i:
                group(i, i + 1)
            group(GROUPS - 1, None)

        @block.tensor
        def _(pe):
            with pe.Fori(0, GROUPS) as i:
                for k in range(NT):
                    pe.wait_ge(split, NT * i + k + 1)
                    up = k < DC
                    if k < 2:
                        pe.wait_ge(added, DC * i)
                    elif k < DC + 2:
                        pe.wait_ge(relued, DC * i + k - 1)
                    else:
                        pe.wait_ge(added, DC * i + k - 1 - DC)
                    x_hi, x_lo = (h_hi, h_lo) if up else (u_hi, u_lo)
                    for c in range(DC):
                        if k == DC:
                            pe.wait_ge(u_split, DC * i + c + 1)
                        for n, (w, x) in enumerate(((w_hi, x_hi), (w_hi, x_lo), (w_lo, x_hi))):
                            for s, (t0, width) in enumerate(SLABS):
                                at = (3 * (k % 2) + s) * BANK
                                last = nc.tensor.matmul(psum[:, at:at + width], w[:, k % 2, c, :],
                                                        x[:, c, t0:t0 + width],
                                                        start=(c == 0 and n == 0), stop=(c == DC - 1 and n == 2))
                    last.then_inc(multiplied, 1)


class Shared:
    pass


def run(nc, a):
    with ExitStack() as es:
        g = Shared()
        (g.x_t, g.w_tok, g.w_feat, g.b_forget, g.g_attn, g.g_mlp, g.g_final, g.cos_t, g.sin_t, g.cache_logf,
         g.cache_kt, g.cache_v, g.state_in, g.w_merge, g.w_up, g.w_down,
         g.ret_cols, g.ret_decay, g.ret_qdec, g.masks, g.ident_t) = a["ins"]
        g.v_out, g.qk_out, g.logf_out, g.state_out, g.y_out = a["outs"]
        g.x_c = g.x_t.rearrange("(c p) t -> c p t", p=P)
        scratch = lambda n, s: nc.dram_tensor(n, s, F32, kind="Internal").ap()
        g.qk_ret, g.gates = scratch("qk_ret", [NROPE, P, TOK]), scratch("gates", [NSILU + NSIG, P, TOK])
        g.v_ret, g.o_ret = scratch("v_ret", [HR, TOK, DV]), scratch("o_ret", [2 * DC, P, TOK])
        g.o_fox = scratch("o_fox", [DC, P, TOK])
        g.q_rows, g.k_rows = scratch("q_rows", [HF, 4, TOK]), scratch("k_rows", [HF, 4, KEYS])
        g.psum = es.enter_context(nc.psum_tensor("psum", [P, 8 * BANK], F32))
        sb = lambda n, s, dt=F32: es.enter_context(nc.sbuf_tensor(n, s, dt))
        g.ones, g.eps = sb("ones", [P, P]), sb("eps", [P, 1])
        g.acc = sb("acc", [P, TOK])
        with nc.Block() as block:
            @block.vector
            def _(dve):
                nc.vector.memset(g.ones[:], 1.0)
                nc.vector.memset(g.eps[:], EPS)
        with ExitStack() as hs:
            h_hi = hs.enter_context(nc.sbuf_tensor("h_hi", [P, DC, TOKP], F32R))
            h_lo = hs.enter_context(nc.sbuf_tensor("h_lo", [P, DC, TOKP], F32R))
            with nc.Block() as block:
                @block.vector
                def _(dve):
                    nc.vector.memset(h_hi[:, :, TOK:TOKP].bitcast(F32), 0.0)
                    nc.vector.memset(h_lo[:, :, TOK:TOKP].bitcast(F32), 0.0)
            with ExitStack() as ws:
                first = [ws.enter_context(nc.sbuf_tensor(f"val_{n}", [P, DC, VGROUP], dt))
                         for n, dt in (("raw", F32), ("w_hi0", F32R), ("w_lo0", F32R))]
                with nc.sbuf_tensor("x0", [P, DC, TOK], F32) as x0:
                    rms_norm(nc, g, "n1", x0, g.g_attn, load=g.x_t, hi=h_hi[:, :, 0:TOK], lo=h_lo[:, :, 0:TOK],
                             ahead=[t[:].rearrange("p c n -> p (c n)") for t in first] + [g.w_tok[0, :, :]])
                values(nc, g, h_hi, h_lo, *first)
            features(nc, g, h_hi, h_lo)
        retention(nc, g)
        fox(nc, g)
        x1 = sb("x1", [P, DC, TOK])
        merge(nc, g, x1)
        with ExitStack() as hs:
            h_hi = hs.enter_context(nc.sbuf_tensor("m_hi", [P, DC, TOK], F32R))
            h_lo = hs.enter_context(nc.sbuf_tensor("m_lo", [P, DC, TOK], F32R))
            weights = [hs.enter_context(nc.sbuf_tensor(f"ml_{n}", s, dt)) for n, s, dt in
                       (("raw", [P, DC, P], F32), ("w_hi", [P, 2, DC, P], F32R), ("w_lo", [P, 2, DC, P], F32R))]
            flat = lambda w: w.rearrange("p c n -> p (c n)")
            rms_norm(nc, g, "n2", x1, g.g_mlp, hi=h_hi, lo=h_lo,
                     ahead=[flat(weights[0][:]), flat(weights[1][:, 0]), flat(weights[2][:, 0]), g.w_up[0, :, :]])
            mlp(nc, g, x1, h_hi, h_lo, *weights)
        rms_norm(nc, g, "n3", x1, g.g_final, out=g.y_out)



def _tiles(w, chunks, width):
    k, n = w.shape
    return np.ascontiguousarray(w.reshape(chunks, P, n // width, width).transpose(2, 1, 0, 3)
                                .reshape(n // width, P, chunks * width))


def _cols(v):
    return np.ascontiguousarray(v.reshape(-1, P).T)


def _tables():
    f = np.float32
    inv = (f(10000.0) ** (-np.arange(0, DK, 2, dtype=f) / f(DK))).astype(f)
    pos = np.concatenate([np.arange(SEQ), PAST + np.arange(DEC)]).astype(f)
    ang = inv[:, None] * pos[None, :]
    lg = np.log(f(1.0) - f(2.0) ** (f(-5.0) - np.arange(HR, dtype=f))).astype(f)
    m, j = np.arange(P), np.arange(SEQ)
    dist = np.abs(j[None, :] - m[:, None]).astype(f)
    seen = (m[:, None] // CHUNK) <= (j[None, :] // CHUNK)
    kscale = f(DK ** -0.5)
    table = np.where(seen[None], np.exp(lg[:, None, None] * dist[None]), 0).astype(f) * kscale
    cols = np.zeros((HR, P, TT + 1), f)
    for t in range(TT - 1):
        cols[:, :, t] = np.exp(lg[:, None] * (SEQ - 1 - t * P - m)[None].astype(f)) * kscale
    cols[:, :DEC, TT - 1] = np.exp(lg[:, None] * (DEC - 1 - m[:DEC])[None].astype(f)) * kscale
    cols[:, :, TT] = np.exp(lg * f(DEC))[:, None]
    qdec = np.broadcast_to(np.exp(lg[:, None] * (np.arange(DEC, dtype=f) + 1))[:, None, :], (HR, P, DEC))
    q, k = np.arange(P)[:, None], np.arange(P)[None, :]
    masks = np.stack([np.where(k <= q, 0, NEG), np.where((k <= q) & (k < DEC), 0, NEG)], 1).astype(f)
    return (np.cos(ang).astype(f), np.sin(ang).astype(f), cols, np.ascontiguousarray(table),
            np.ascontiguousarray(qdec), np.ascontiguousarray(masks), np.eye(P, dtype=f))


def kernel(x_prompt, x_sample, cache_fox_k, cache_fox_v, cache_fox_logf, state_ret,
           g_attn, w_in, b_forget, g_ret_norm, w_branch, w_out, g_mlp, w_up, w_down, g_final):
    import concourse.bacc as bacc
    from concourse.bass_utils import run_bass_kernel_spmd

    npa = lambda v: np.asarray(v)
    x_t = np.ascontiguousarray(np.concatenate([npa(x_prompt)[0], npa(x_sample)[0]], 0).T)
    w_in, w_branch, w_out, w_up, w_down = (npa(w)[0] for w in (w_in, w_branch, w_out, w_up, w_down))
    widths = (1024, 1024, 1024, HF, 1024, 1024, 2048, 2048, 1024, 1024)
    qf, kf, vf, ff, qr, kr, vr, gr, ga, gb = np.split(w_in, np.cumsum(widths)[:-1], 1)
    w_tok = _tiles(np.concatenate([vf, vr], 1), DC, 512)
    w_feat = _tiles(np.concatenate([qf, kf, qr, kr, gr, ga, gb, ff, np.zeros((D, P - HF), np.float32)], 1), DC, P)
    cos, sin, cols, table, qdec, masks, ident = _tables()
    ret_cols = np.concatenate([cols, npa(g_ret_norm)[0].reshape(HR, DV // P, P).transpose(0, 2, 1)], 2)
    ins = {
        "x_t": x_t, "w_tok": w_tok, "w_feat": w_feat, "b_forget": npa(b_forget)[0].reshape(HF, 1),
        "g_attn": _cols(npa(g_attn)[0]), "g_mlp": _cols(npa(g_mlp)[0]), "g_final": _cols(npa(g_final)),
        "cos_t": cos, "sin_t": sin,
        "cache_logf": npa(cache_fox_logf)[0, 0].T, "cache_kt": npa(cache_fox_k)[0, 0].transpose(1, 2, 0),
        "cache_v": npa(cache_fox_v)[0, 0].reshape(PAST, HF * DF), "state_in": npa(state_ret)[0, 0],
        "w_merge": np.concatenate([_tiles(w_branch[n * D:(n + 1) * D], DC, P) for n in range(3)]
                                  + [_tiles(w_out, DC, P)], 0),
        "w_up": _tiles(w_up, DC, P),
        "w_down": np.concatenate([_tiles(w_down[n * D:(n + 1) * D], DC, P) for n in range(DFF // D)], 0),
        "ret_cols": ret_cols, "ret_decay": table, "ret_qdec": qdec, "masks": masks, "ident_t": ident,
    }
    ins = {n: np.ascontiguousarray(v) for n, v in ins.items()}
    outs = {"v": (TOK, D), "qk": (NPLAIN, P, TOK), "logf": (HF, TOK),
            "state": (2, HR, DK, DV), "y": (D, TOK)}
    nc = bacc.Bacc("TRN2", target_bir_lowering=False, num_devices=1)
    args = {
        "ins": [nc.dram_tensor(f"in_{n}", v.shape, F32, kind="ExternalInput").ap() for n, v in ins.items()],
        "outs": [nc.dram_tensor(f"out_{n}", s, F32, kind="ExternalOutput").ap() for n, s in outs.items()],
    }
    run(nc, args)
    got = run_bass_kernel_spmd(nc, [{f"in_{n}": v for n, v in ins.items()}], core_ids=[0]).results[0]
    v, qk, logf, state, y = (got[f"out_{n}"] for n in outs)
    y = y.T
    k = qk[DC:].reshape(D, TOK).T.reshape(TOK, HF, DF)
    v = v.reshape(TOK, HF, DF)
    f = logf.T
    own = np.ascontiguousarray
    return (own(y[None, :SEQ]), own(y[None, SEQ:]), own(k[None, None, :SEQ]), own(v[None, None, :SEQ]),
            own(f[None, None, :SEQ]), own(state[None, 1:2]), own(k[None, None, SEQ:]),
            own(v[None, None, SEQ:]), own(f[None, None, SEQ:]), own(state[None, 0:1]))
```
